# Optimizing a Trainium2 kernel written in Bass

```python
import jax, jax.numpy as jnp
from jax import lax
import numpy as np

D_MODEL = 1024
BATCH = 1
SEQ = 1024
DEPTH = 1

N_ATT_HEADS = 8
ATT_HEAD_DIM = 128
KV_LORA = 256
IDX_HEADS = 8
IDX_DIM = 64
TOPK_MAX = 256
Q_BLOCK = 128
N_RET_HEADS = 4
RET_QK_DIM = 128
RET_V_DIM = 256
RET_CHUNK = 128
N_GROUPS = 4
EXPERTS_PER_GROUP = 4
N_EXPERTS = N_GROUPS * EXPERTS_PER_GROUP
EXPERT_FF = 256
TOP_K_EXPERTS = 2
EPS = 1e-6

ATT_Q_W = N_ATT_HEADS * ATT_HEAD_DIM
RET_QK_W = N_RET_HEADS * RET_QK_DIM
RET_V_W = N_RET_HEADS * RET_V_DIM
SPLITS = (ATT_Q_W, KV_LORA, IDX_HEADS * IDX_DIM, IDX_DIM, IDX_HEADS,
          RET_QK_W, RET_QK_W, RET_V_W, RET_V_W, D_MODEL, D_MODEL)
IN_WIDTH = sum(SPLITS)

kernel_name = "hybrid_dsa_retention_hmoe_block"

def rms_norm(x, g):
    xf = x.astype(jnp.float32)
    y = xf * lax.rsqrt(jnp.mean(xf * xf, axis=-1, keepdims=True) + EPS)
    return (y * g.astype(jnp.float32)).astype(x.dtype)

def group_norm_heads(x, g):
    xf = x.astype(jnp.float32)
    mu = jnp.mean(xf, axis=-1, keepdims=True)
    var = jnp.mean(jnp.square(xf - mu), axis=-1, keepdims=True)
    return ((xf - mu) * lax.rsqrt(var + EPS) * g.astype(jnp.float32)).astype(x.dtype)

def alibi_slopes(n_heads):
    return 2.0 ** (-8.0 * jnp.arange(1, n_heads + 1, dtype=jnp.float32) / n_heads)

def retention_decays(n_heads):
    return 1.0 - 2.0 ** (-5.0 - jnp.arange(n_heads, dtype=jnp.float32))

def sparse_indexed_attention(q, k, v, q_idx, k_idx, w_idx, slopes):
    B, S, H, Dh = q.shape
    n_sel = min(TOPK_MAX, S // 4)
    nb = S // Q_BLOCK
    key_pos = jnp.arange(S)
    k_idx32 = k_idx.astype(jnp.float32)

    def to_blocks(a):
        return a.reshape((B, nb, Q_BLOCK) + a.shape[2:]).swapaxes(0, 1)

    def one_block(args):
        qb, qib, wb, blk = args
        q_pos = blk * Q_BLOCK + jnp.arange(Q_BLOCK)
        causal = key_pos[None, :] <= q_pos[:, None]
        dots = jnp.einsum('bqhd,bsd->bqhs', qib.astype(jnp.float32), k_idx32) * (IDX_DIM ** -0.5)
        score = jnp.einsum('bqhs,bqh->bqs', jax.nn.relu(dots), wb.astype(jnp.float32))
        score = jnp.where(causal[None], score, -jnp.inf)
        _, sel = lax.top_k(score, n_sel)
        k_sel = jax.vmap(lambda kk, ii: kk[ii])(k, sel)
        v_sel = jax.vmap(lambda vv, ii: vv[ii])(v, sel)
        logits = jnp.einsum('bqhd,bqkd->bhqk', qb, k_sel).astype(jnp.float32) * (Dh ** -0.5)
        dist = (q_pos[None, :, None] - sel).astype(jnp.float32)
        logits = logits - slopes[None, :, None, None] * dist[:, None]
        valid = sel <= q_pos[None, :, None]
        logits = jnp.where(valid[:, None], logits, -jnp.inf)
        p = jax.nn.softmax(logits, axis=-1).astype(v.dtype)
        return jnp.einsum('bhqk,bqkd->bqhd', p, v_sel)

    out = lax.map(one_block, (to_blocks(q), to_blocks(q_idx), to_blocks(w_idx), jnp.arange(nb)))
    return out.swapaxes(0, 1).reshape(B, S, H, Dh)

def retention_chunkwise(q, k, v, gammas):
    B, S, H, Dk = q.shape
    Dv = v.shape[-1]
    C = RET_CHUNK
    n = S // C
    log_g = jnp.log(gammas)
    i = jnp.arange(C, dtype=jnp.float32)
    rel = i[:, None] - i[None, :]
    decay_intra = jnp.where(rel[None] >= 0, jnp.exp(rel[None] * log_g[:, None, None]), 0.0)
    q_decay = jnp.exp((i + 1.0)[None] * log_g[:, None])
    k_decay = jnp.exp((C - 1.0 - i)[None] * log_g[:, None])
    chunk_decay = jnp.exp(C * log_g)

    def chunks(a):
        return a.astype(jnp.float32).reshape(B, n, C, H, a.shape[-1]).transpose(1, 0, 3, 2, 4)

    qc = chunks(q)
    kc = chunks(k) * (Dk ** -0.5)
    vc = chunks(v)

    def step(state, xs):
        qi, ki, vi = xs
        intra = jnp.einsum('bhqd,bhkd->bhqk', qi, ki) * decay_intra[None]
        o = (jnp.einsum('bhqk,bhkv->bhqv', intra, vi)
             + jnp.einsum('bhqd,bhdv->bhqv', qi * q_decay[None, :, :, None], state))
        state = (chunk_decay[None, :, None, None] * state
                 + jnp.einsum('bhkd,bhkv->bhdv', ki * k_decay[None, :, :, None], vi))
        return state, o

    init = jnp.zeros((B, H, Dk, Dv), jnp.float32)
    _, o = lax.scan(step, init, (qc, kc, vc))
    return o.transpose(1, 0, 3, 2, 4).reshape(B, S, H, Dv)

def hierarchical_moe(h, w_group, b_group, w_er, b_er, w_gate, w_up, w_down):
    B, S, D = h.shape
    t = h.reshape(B * S, D)
    g_logits = (t @ w_group).astype(jnp.float32) + b_group.astype(jnp.float32)
    g_prob = jax.nn.softmax(g_logits, axis=-1)
    g_sel = jnp.argmax(g_logits, axis=-1)
    g_w = jnp.take_along_axis(g_prob, g_sel[:, None], axis=1)
    e_logits = ((t @ w_er).astype(jnp.float32) + b_er.astype(jnp.float32)).reshape(-1, N_GROUPS, EXPERTS_PER_GROUP)
    e_in = jnp.take_along_axis(e_logits, g_sel[:, None, None], axis=1)[:, 0]
    top_v, top_i = lax.top_k(e_in, TOP_K_EXPERTS)
    top_p = jax.nn.softmax(top_v, axis=-1) * g_w
    expert_id = g_sel[:, None] * EXPERTS_PER_GROUP + top_i
    comb = jnp.sum(jax.nn.one_hot(expert_id, N_EXPERTS, dtype=jnp.float32) * top_p[..., None], axis=1)
    hg = jnp.einsum('td,edf->tef', t, w_gate)
    hu = jnp.einsum('td,edf->tef', t, w_up)
    act = jax.nn.silu(hg) * hu * comb[..., None].astype(hg.dtype)
    out = jnp.einsum('tef,efd->td', act, w_down)
    return out.reshape(B, S, D).astype(h.dtype)

def setup_inputs(seed: int = 0) -> dict:
    key = jax.random.key(seed)
    ks = jax.random.split(key, 24)
    L = DEPTH
    f32 = jnp.float32

    def nrm(k, shape, fan_in):
        return jax.random.normal(k, shape, f32) * (fan_in ** -0.5)

    def gain(k, shape):
        return 1.0 + 0.02 * jax.random.normal(k, shape, f32)

    return {
        "x": jax.random.normal(ks[0], (BATCH, SEQ, D_MODEL), f32),
        "norm1_g": gain(ks[1], (L, D_MODEL)),
        "w_in": nrm(ks[2], (L, D_MODEL, IN_WIDTH), D_MODEL),
        "kv_norm_g": gain(ks[3], (L, KV_LORA)),
        "w_kv_up": nrm(ks[4], (L, KV_LORA, 2 * ATT_HEAD_DIM), KV_LORA),
        "q_norm_g": gain(ks[5], (L, ATT_HEAD_DIM)),
        "k_norm_g": gain(ks[6], (L, ATT_HEAD_DIM)),
        "idx_k_norm_g": gain(ks[7], (L, IDX_DIM)),
        "ret_norm_g": gain(ks[8], (L, N_RET_HEADS, RET_V_DIM)),
        "w_att_branch": nrm(ks[9], (L, ATT_Q_W, D_MODEL), ATT_Q_W),
        "w_ret_branch": nrm(ks[10], (L, RET_V_W, D_MODEL), RET_V_W),
        "w_out": nrm(ks[11], (L, D_MODEL, D_MODEL), D_MODEL),
        "norm2_g": gain(ks[12], (L, D_MODEL)),
        "w_group_router": nrm(ks[13], (L, D_MODEL, N_GROUPS), D_MODEL),
        "b_group_router": 0.01 * jax.random.normal(ks[14], (L, N_GROUPS), f32),
        "w_expert_router": nrm(ks[15], (L, D_MODEL, N_EXPERTS), D_MODEL),
        "b_expert_router": 0.01 * jax.random.normal(ks[16], (L, N_EXPERTS), f32),
        "w_exp_gate": nrm(ks[17], (L, N_EXPERTS, D_MODEL, EXPERT_FF), D_MODEL),
        "w_exp_up": nrm(ks[18], (L, N_EXPERTS, D_MODEL, EXPERT_FF), D_MODEL),
        "w_exp_down": nrm(ks[19], (L, N_EXPERTS, EXPERT_FF, D_MODEL), EXPERT_FF),
    }

def reference(x, norm1_g, w_in, kv_norm_g, w_kv_up, q_norm_g, k_norm_g, idx_k_norm_g,
              ret_norm_g, w_att_branch, w_ret_branch, w_out, norm2_g, w_group_router,
              b_group_router, w_expert_router, b_expert_router, w_exp_gate, w_exp_up,
              w_exp_down):
    B, S, D = x.shape
    slopes = alibi_slopes(N_ATT_HEADS)
    gammas = retention_decays(N_RET_HEADS)
    points = np.cumsum(np.array(SPLITS))[:-1].tolist()
    h = x
    for l in range(DEPTH):
        n = rms_norm(h, norm1_g[l])
        proj = n @ w_in[l]
        (q_att, c_kv, q_idx, k_idx, w_idx, r_q, r_k, r_v, r_gate,
         g_att, g_ret) = jnp.split(proj, points, axis=-1)

        q = rms_norm(q_att.reshape(B, S, N_ATT_HEADS, ATT_HEAD_DIM), q_norm_g[l])
        kv = rms_norm(c_kv, kv_norm_g[l]) @ w_kv_up[l]
        k_sh, v_sh = jnp.split(kv, 2, axis=-1)
        k_sh = rms_norm(k_sh, k_norm_g[l])
        k_idx = rms_norm(k_idx, idx_k_norm_g[l])
        w_idx = w_idx * (IDX_HEADS ** -0.5)
        att = sparse_indexed_attention(q, k_sh, v_sh,
                                       q_idx.reshape(B, S, IDX_HEADS, IDX_DIM),
                                       k_idx, w_idx, slopes)
        y_att = att.reshape(B, S, ATT_Q_W) @ w_att_branch[l]

        ret = retention_chunkwise(r_q.reshape(B, S, N_RET_HEADS, RET_QK_DIM),
                                  r_k.reshape(B, S, N_RET_HEADS, RET_QK_DIM),
                                  r_v.reshape(B, S, N_RET_HEADS, RET_V_DIM), gammas)
        ret = group_norm_heads(ret, ret_norm_g[l]).astype(h.dtype)
        y_ret = (jax.nn.silu(r_gate) * ret.reshape(B, S, RET_V_W)) @ w_ret_branch[l]

        mixed = jax.nn.sigmoid(g_att) * y_att + jax.nn.sigmoid(g_ret) * y_ret
        h = h + mixed @ w_out[l]

        n2 = rms_norm(h, norm2_g[l])
        h = h + hierarchical_moe(n2, w_group_router[l], b_group_router[l],
                                 w_expert_router[l], b_expert_router[l],
                                 w_exp_gate[l], w_exp_up[l], w_exp_down[l])
    return h


_drawn_inputs = setup_inputs


def setup_inputs(seed=0):
    import zlib

    import numpy as np

    out = dict(_drawn_inputs(seed))
    spreads = {}
    factors = {'kv_norm_g': 4.135,
     'q_norm_g': 4.737,
     'k_norm_g': 7.95,
     'ret_norm_g': 21.436,
     'b_group_router': 15.638,
     'b_expert_router': 45.068,
     'norm2_g': 6.763}
    for name, (base, spread) in spreads.items():
        noise = np.random.default_rng([zlib.crc32(name.encode()), seed]).standard_normal(out[name].shape)
        drawn = base * np.exp(spread * noise) if base else spread * noise
        out[name] = __import__('jax').numpy.asarray(drawn.astype(out[name].dtype))
    for name, factor in factors.items():
        out[name] = (out[name] * factor).astype(out[name].dtype)
    return out
```

```python
from contextlib import ExitStack

import numpy as np
import concourse.bass as bass
from concourse import mybir

ALU = mybir.AluOpType
ACT = mybir.ActivationFunctionType
F32 = mybir.dt.float32
F32R = mybir.dt.float32r
I32 = mybir.dt.int32
U32 = mybir.dt.uint32
X = mybir.AxisListType.X

P = 128
S = 1024
D = 1024
NT = S // P
KT = D // P
HA, DH = 8, 128
KVL = 256
HI, DI = 8, 64
TOPK = 256
HR, DK, DV = 4, 128, 256
NG, EPG, NE, FF = 4, 4, 16, 256
EPS = 1e-6
BIG = 1e30
TAKEN = -3e38
BANK = 512

C_Q = 0
C_KV = C_Q + HA * DH
C_QI = C_KV + KVL
C_KI = C_QI + HI * DI
C_RQ = C_KI + DI + HI
C_RK = C_RQ + HR * DK
C_RV = C_RK + HR * DK
C_RG = C_RV + HR * DV
C_GA = C_RG + HR * DV
C_GR = C_GA + D
KVW = KVL + DI + HI

K_ID = 0
K_REL = K_ID + P
K_CAUS = K_REL + S
K_RM = K_CAUS + P
K_QD = K_RM + HR * P
K_KD = K_QD + HR
K_TRI = K_KD + HR
K_ONE = K_TRI + P
K_THR = K_ONE + P
K_EXC = K_THR + NE * NT
K_P16 = K_EXC + NE * NE
K_P4 = K_P16 + NE
K_TI = K_P4 + NG
NTILE = S * 2 // P + NE - 1
K_SI = K_TI + 32
K_NH = K_SI + HA
K_END = K_NH + 1
NGAIN = 21

GAMMA = [1.0 - 2.0 ** (-5.0 - h) for h in range(HR)]
GC = [g ** P for g in GAMMA]


def constants():
    c = np.zeros((P, K_END), np.float64)
    p = np.arange(P)[:, None]
    i = np.arange(P)[None, :]
    c[:, K_ID:K_ID + P] = p == i
    c[:, K_REL:K_REL + S] = np.arange(S)[None, :] - p
    c[:, K_CAUS:K_CAUS + P] = np.where(i <= p, 0.0, -BIG)
    for h, g in enumerate(GAMMA):
        c[:, K_RM + h * P:K_RM + (h + 1) * P] = np.where(p <= i, g ** -(p + 1.0), 0.0) * DK ** -0.5
        c[:, K_QD + h] = g ** (np.arange(P) + 1.0)
        c[:, K_KD + h] = g ** (P - 1.0 - np.arange(P)) * DK ** -0.5
    c[:, K_TRI:K_TRI + P] = p < i
    c[:, K_ONE:K_ONE + P] = 1.0
    c[:, K_THR:K_THR + NE * NT] = np.tile(np.arange(NT) * float(P), NE)[None, :]
    e = np.arange(NE)
    c[:, K_EXC:K_EXC + NE * NE] = (e[None, :] < e[:, None]).astype(np.float64).reshape(1, -1)
    c[:, K_P16:K_P16 + NE] = NE - e
    c[:, K_P4:K_P4 + NG] = NG - np.arange(NG)
    c[:, K_TI:K_TI + 32] = np.arange(32)
    c[:, K_SI:K_SI + HA] = 2.0 ** (np.arange(HA) + 1.0)
    c[:, K_NH] = -0.5
    return c.astype(np.float32)


class Banks:

    def __init__(self, full, free):
        self.full, self.free = full, free
        self.count = [0] * 8
        self.released = [None] * 8
        self.at = {}

    def use(self, name, bank, n=1):
        before = sorted({self.released[b] for b in range(bank, bank + n)} - {None})
        self.count[bank] += 1
        for b in range(bank, bank + n):
            self.released[b] = (bank, self.count[bank])
        self.at[name] = (bank, self.count[bank], before)

    def col(self, name):
        return self.at[name][0] * BANK

    def wait_free(self, eng, name):
        for b, n in self.at[name][2]:
            eng.wait_ge(self.free[b], n)

    def wait_full(self, eng, name):
        eng.wait_ge(self.full[self.at[name][0]], self.at[name][1])

    def wait_read(self, eng, name):
        eng.wait_ge(self.free[self.at[name][0]], self.at[name][1])

    def filled(self, inst, name):
        inst.then_inc(self.full[self.at[name][0]], 1)

    def read(self, inst, name):
        inst.then_inc(self.free[self.at[name][0]], 1)


class Seq:

    def __init__(self, eng, sem):
        self.eng, self.sem, self.n = eng, sem, 0

    def mark(self, inst):
        self.n += 1
        inst.then_inc(self.sem, 1)

    def wait(self):
        self.eng.wait_ge(self.sem, self.n)

    def __call__(self, inst):
        self.mark(inst)
        self.wait()


def program(nc, w, scratch, out, stop=99):
    ctx = ExitStack()
    with ctx:
        def sem(name):
            return ctx.enter_context(nc.semaphore(name))

        base = (nc.sbuf_base + 63) // 64 * 64
        place = [base]

        def sb(name, shape, dt=F32, at=None):
            n = 4 * int(np.prod(shape[1:]))
            off = place[0] if at is None else at
            if at is None:
                place[0] += (n + 31) // 32 * 32
            assert off + n <= nc.sbuf_usable_end, (name, off + n, nc.sbuf_usable_end)
            return nc.alloc_sbuf_tensor_at(name, shape, dt, offset=off)

        cst = sb("cst", [P, K_END])
        gains = sb("gains", [P, 64])
        small = sb("small", [P, 512])
        zero = sb("zero", [P, P])
        slot = sb("slot", [P, 2, NT], U32)
        owner = sb("owner", [P, 32], I32)
        nt_at = place[0]
        n_hi = sb("n_hi", [P, KT, S], F32R)
        n_lo = sb("n_lo", [P, KT, S], F32R)
        NR, NH = 4, 4
        wr_at = place[0]
        w_raw = [sb(f"w_raw{i}", [P, BANK]) for i in range(NR)]
        w_hi = [sb(f"w_hi{i}", [P, BANK], F32R) for i in range(NH)]
        w_lo = [sb(f"w_lo{i}", [P, BANK], F32R) for i in range(NH)]
        dist_at = place[0]
        dist = sb("dist", [P, NT * (NT + 1) // 2 * P])
        up_at = place[0]
        w_up = sb("w_up", [P, 2, 2 * DH])
        kT = sb("kT", [P, S])
        v_at = place[0]
        kvu = sb("kvu", [P, NT, 2 * DH])
        r1 = place[0]
        ps = ctx.enter_context(nc.psum_tensor("ps", [P, 8 * BANK], F32))

        def r1t(name, shape, off, dt=F32):
            return sb(name, shape, dt, at=r1 + 4 * off)

        xin = r1t("xin", [P, NT, D], 0)
        kvrows = r1t("kvrows", [P, NT, KVW], 0)
        sq = r1t("sq", [P, NT, KVW], 2624)
        cT = r1t("cT", [P, 2, S], 5248)
        kdup = r1t("kdup", [P, NT, 2, DI], 7296)
        kiT = r1t("kiT", [P, S], 8320)
        qiT = r1t("qiT", [P, 4, S], 9344)
        relu = [r1t(f"relu{i}", [P, S], 13440 + i * S) for i in range(2)]
        junk = r1t("junk", [P, 2, D], 15488)
        rqT = [r1t(f"rqT{i}", [P, S], i * S) for i in range(2)]
        rkT = r1t("rkT", [P, S], 2048)
        rv = [r1t(f"rv{i}", [P, NT, DV], 3072 + i * 2048) for i in range(2)]
        krow = r1t("krow", [P, NT, P], 7168)
        sT = r1t("sT", [P, NT, P], 8192)
        state = r1t("state", [P, NT - 1, DV], 9216)
        ro = r1t("ro", [P, NT, DV], 11008)
        gate = r1t("gate", [P, NT, 2 * DV], 13056)
        rT = r1t("rT", [P, S], 17152)
        qst = [r1t(f"qst{i}", [P, BANK], 18176 + i * BANK) for i in range(2)]
        junk2 = sb("junk2", [P, DV], at=up_at)
        stmp = sb("stmp", [P, DV], at=up_at + 4 * DV)
        qrow = [r1t(f"qrow{i}", [P, HA, DH], i * D) for i in range(2)]
        qT = [r1t(f"qT{i}", [P, HA, P], 2048 + i * D) for i in range(2)]
        prob = [r1t(f"prob{i}", [P, S], 4096 + i * S) for i in range(4)]
        pT = [r1t(f"pT{i}", [P, NT, 4, P], 8192 + i * 4096) for i in range(2)]
        aT = [r1t(f"aT{i}", [P, HA, P], 16384 + i * D) for i in range(2)]
        sig = [r1t(f"sig{i}", [P, 4, S], i * 4096) for i in range(4)]
        a_raw = [sb(f"a_raw{i}", [P, S], at=v_at + i * 4096) for i in range(2)]
        a_hi = [sb(f"a_hi{i}", [P, S], F32R, at=dist_at + i * 4096) for i in range(2)]
        a_lo = [sb(f"a_lo{i}", [P, S], F32R, at=dist_at + 8192 + i * 4096) for i in range(2)]
        h_sb = r1t("h_sb", [P, NT, D], 0)
        xres = r1t("xres", [P, NT, D], 8192)

        g2b = r1t("g2b", [P, D], 16384)
        w_rt = r1t("w_rt", [P, KT, NG + NE], 17408)
        b_rt = r1t("b_rt", [P, NG + NE], 17568)
        lgt = r1t("lgt", [P, NT, NG + NE], 17592)
        n2T = [sb(f"n2T{i}", [P, KT, P], at=v_at + i * 4096) for i in range(2)]
        n2sq = sb("n2sq", [P, D], at=wr_at + 4096)
        rs = sb("rs", [P, 16, NT * NE], at=dist_at)
        o_pre = sb("o_pre", [P, (NT + 1) * NE], at=dist_at + 16 * 4 * NT * NE)
        W3 = 3 * 4 * BANK
        e_raw = [sb(f"e_raw{i}", [P, W3], at=nt_at + i * 4 * W3) for i in range(2)]
        e_x = [sb(f"e_x{i}", [P, D], at=nt_at + 8 * W3 + i * 4 * D) for i in range(2)]
        e_y = [sb(f"e_y{i}", [P, D], at=nt_at + 8 * W3 + 8 * D + i * 4 * D) for i in range(2)]
        e_hi = [sb(f"e_hi{i}", [P, W3], F32R, at=wr_at + i * 4 * W3) for i in range(2)]
        e_lo = [sb(f"e_lo{i}", [P, W3], F32R, at=wr_at + (2 + i) * 4 * W3) for i in range(2)]
        e_at = wr_at + 16 * W3
        x_hi = [sb(f"x_hi{i}", [P, KT, P], F32R, at=e_at + i * 4 * D) for i in range(2)]
        x_lo = [sb(f"x_lo{i}", [P, KT, P], F32R, at=e_at + (2 + i) * 4 * D) for i in range(2)]
        gated = sb("gated", [P, FF], at=e_at + 16 * D)
        arow = sb("arow", [P, FF], at=e_at + 16 * D + 4 * FF)
        at_hi = sb("at_hi", [P, 2, P], F32R, at=e_at + 16 * D + 8 * FF)
        at_lo = sb("at_lo", [P, 2, P], F32R, at=e_at + 16 * D + 12 * FF)
        t_y = [[sb(f"t_y{i}{j}", [P, D], at=nt_at + (3 * i + j) * 4 * D) for j in range(2)] for i in range(2)]
        t_h = [sb(f"t_h{i}", [P, D], at=nt_at + (3 * i + 2) * 4 * D) for i in range(2)]

        ident = cst[:, K_ID:K_ID + P]
        G1, GKV, GK, GKI, GRT, GQ = 0, 8, 10, 11, 12, 20

        q_dram, att_dram, ret_dram, h_dram = scratch["q"], scratch["att"], scratch["ret"], scratch["h"]
        xs_dram, y_dram = scratch["xs"], scratch["y"]

        const_in = sem("const_in")
        x_in = [sem(f"x_in{t}") for t in range(NT)]
        full = [sem(f"bank_full{b}") for b in range(8)]
        free = [sem(f"bank_free{b}") for b in range(8)]
        w_in = [sem(f"w_in{i}") for i in range(NR)]
        hi_ready, lo_ready, chunk_used = sem("hi_ready"), sem("lo_ready"), sem("chunk_used")
        s_dve, s_act, s_pool = sem("dve_seq"), sem("act_seq"), sem("pool_seq")
        sq_done, rstd1, xn_done, nhi_done = sem("sq_done"), sem("rstd1"), sem("xn_done"), sem("nhi_done")
        kv_sq, kv_rstd, ckv_n, k_sq, k_rstd, k_n = (sem(n) for n in ("kv_sq", "kv_rstd", "ckv_n", "k_sq", "k_rstd", "k_n"))
        gains_done = sem("gains_done")
        relu_done, relu_used = sem("relu_done"), sem("relu_used")
        dist_done = sem("dist_done")
        q_copied, q_squared, q_stored = sem("q_copied"), sem("q_squared"), [sem(f"q_stored{i}") for i in range(2)]
        rq_read = sem("rq_read")
        sT_raw, sT_done, kv_raw, state_done = sem("sT_raw"), sem("sT_done"), sem("kv_raw"), sem("state_done")
        krow_done = sem("krow_done")
        o_sum, o_mu, o_var, o_done, = sem("o_sum"), sem("o_mu"), sem("o_var"), sem("o_done")
        gate_done = sem("gate_done")
        ret_stored = sem("ret_stored")
        q_in = [sem(f"q_in{i}") for i in range(2)]
        qT_done = sem("qT_done")
        mx_done, ex_done, p_done = sem("mx_done"), sem("ex_done"), sem("p_done")
        aT_done = sem("aT_done")
        att_stored = [sem(f"att_stored{i}") for i in range(2)]
        sig_done = sem("sig_done")
        a_in = [sem(f"a_in{i}") for i in range(2)]
        a_hi_ready, a_lo_ready = sem("a_hi_ready"), sem("a_lo_ready")
        mixed, mix_hi = sem("mixed"), sem("mix_hi")
        mix_lo = sem("mix_lo")
        xres_in, h_done, h_stored = sem("xres_in"), sem("h_done"), sem("h_stored")

        zero_done, zero_in = sem("zero_done"), sem("zero_in")
        rt_in, h_sq, h_rstd, n2_done, n2T_done = sem("rt_in"), sem("h_sq"), sem("h_rstd"), sem("n2_done"), sem("n2T_done")
        lgt_done, g_shift, g_exp, e_shift, e_exp = (sem(n) for n in ("lgt_done", "g_shift", "g_exp", "e_shift", "e_exp"))
        chosen, ranked, owner_done, slot_done = sem("chosen"), sem("ranked"), sem("owner_done"), sem("slot_done")
        scattered = sem("scattered")
        ew_in = [[sem(f"ew_in{i}{j}") for j in range(3)] for i in range(2)]
        ex_in = [sem(f"ex_in{i}") for i in range(2)]
        ehi_done, elo_done = [sem(f"ehi_done{j}") for j in range(3)], [sem(f"elo_done{j}") for j in range(3)]
        exT_full, exT_hi, exT_lo = sem("exT_full"), sem("exT_hi"), sem("exT_lo")
        gu_full, gu_silu, gu_read = sem("gu_full"), sem("gu_silu"), sem("gu_read")
        eaT_full, eaT_hi, eaT_lo = sem("eaT_full"), sem("eaT_hi"), sem("eaT_lo")
        ey_full, ey_read, ey_out = sem("ey_full"), sem("ey_read"), [sem(f"ey_out{i}") for i in range(2)]
        ty_in, th_in, t_half, t_sum, t_out = ([sem(f"ty_in{i}") for i in range(2)], [sem(f"th_in{i}") for i in range(2)],
                                              sem("t_half"), sem("t_sum"), [sem(f"t_out{i}") for i in range(2)])

        def cols(src, c0, n, at=0):
            return (src, c0, n, at)
        wi = w["w_in"]
        blocks = [
            ("kv", "R", [cols(wi, C_KV, KVL, 0), cols(wi, C_KI, DI + HI, KVL)]),
            ("qi", "C", [cols(wi, C_QI, BANK)]),
        ]

        def gate_block(p):
            return (f"gate{p}", "R", [cols(wi, C_RG + p * BANK, BANK)])

        def head_block(h):
            return (f"head{h}", "H", [cols(wi, C_RQ + h * DK, DK, 0), cols(wi, C_RK + h * DK, DK, DK),
                                      cols(wi, C_RV + h * DV, DV, 2 * DK)])

        def q_block(b):
            return (f"q{b}", "R", [cols(wi, C_Q + b * BANK, BANK)])
        blocks += [gate_block(0), head_block(0), head_block(1), q_block(0),
                   gate_block(1), head_block(2), head_block(3), q_block(1)]
        for g, c0 in (("ga", C_GA), ("gr", C_GR)):
            blocks += [(f"{g}{b}", "C", [cols(wi, c0 + b * BANK, BANK)]) for b in range(2)]
        for g, src in (("ba", w["w_att"]), ("br", w["w_ret"])):
            blocks += [(f"{g}{b}", "A", [cols(src, b * BANK, BANK)]) for b in range(2)]
        blocks += [(f"wo{b}", "M", [cols(w["w_out"], b * BANK, BANK)]) for b in range(2)]
        number = {name: i for i, (name, _, _) in enumerate(blocks)}
        chunks = [(i, k) for i in range(len(blocks)) for k in range(KT)]
        landed, n_in = [], [0] * NR
        for c, (i, k) in enumerate(chunks):
            n_in[c % NR] += 16 * len(blocks[i][2])
            landed.append(n_in[c % NR])
        act_chunks = [(name, k) for name in ("ba0", "ba1", "br0", "br1") for k in range(KT)]

        bk = Banks(full, free)

        def use_block(name):
            for b in range(8):
                bk.use((name, b), b)
        for half in range(2):
            for k in range(KT):
                bk.use(("xT", half, k), k)
        use_block("kv")
        use_block("qi")
        for j in range(2):
            for half in range(2):
                bk.use(("cT", j, half), 2 * j + half)
        for half in range(2):
            bk.use(("kiT", half), 4 + half)
        for i in range(4):
            bk.use(("kvu", i), i)
        for half in range(2):
            bk.use(("kT", half), 6 + half)
        for t in range(2, NT):
            for h in range(HI):
                bk.use(("idx", t, h), 2 * (h % 4), 2)

        def use_phase1(h):
            for half in range(2):
                bk.use(("krow", h, half), half)
            for half in range(2):
                bk.use(("sc", h, half), 2 + half)
            for i in range(4):
                bk.use(("kvs", h, i), 4 + i)

        def use_phase2(h):
            for i in range(4):
                bk.use(("ro", h, i), i)

        def use_turn(h):
            for j in range(2):
                for half in range(2):
                    bk.use(("rT", h, j, half), 4 + 2 * j + half)
        ret_order = [("block", "gate0"), ("block", "head0"), ("phase1", 0), ("block", "head1"), ("phase2", 0),
                     ("phase1", 1), ("block", "q0"), ("turn", 0), ("phase2", 1), ("block", "gate1"), ("turn", 1),
                     ("block", "head2"), ("phase1", 2), ("block", "head3"), ("phase2", 2), ("phase1", 3),
                     ("block", "q1"), ("turn", 2), ("phase2", 3), ("turn", 3)]
        for what, n in ret_order:
            {"block": use_block, "phase1": use_phase1, "phase2": use_phase2, "turn": use_turn}[what](n)
        for t in range(NT):
            for g in range(2):
                bk.use(("qT", t, g), 6 + g)
            for h in range(HA + 2):
                if h < HA:
                    bk.use(("lg", t, h), 2 * (h % 2), 2)
                if h >= 2:
                    for i in range(t // 4 + 1):
                        bk.use(("pT", t, h - 2, i), 4 + i)
                    if (h - 2) % 4 == 3:
                        bk.use(("pv", t, (h - 2) // 4), 6 + (h - 2) // 4)
        for name in [b[0] for b in blocks[10:]]:
            use_block(name)
        for t in range(NT + 1):
            if t < NT:
                for g in range(2):
                    bk.use(("n2T", t, g), 2 * (t % 2) + g)
            if t >= 1:
                bk.use(("rt", t - 1), 4 + t % 2)
        bk.use(("rank",), 6)
        B_XT, B_GU, B_AT, B_Y = 0, 2 * BANK, 3 * BANK, 4 * BANK

        def bank(name, n=BANK):
            c = bk.col(name)
            return ps[:, c:c + n]

        def used(c):
            i, k = chunks[c]
            if k == KT - 1:
                b, n, _ = bk.at[(blocks[i][0], 7)]
                return full[b], n
            return chunk_used, i * (KT - 1) + k + 1

        def tile_off(t):
            return t * (t + 1) // 2 * P

        block = ctx.enter_context(nc.Block())

        @block.sync
        def _(sp):
            def load_chunk(c):
                i, k = chunks[c]
                if c >= NR:
                    sp.wait_ge(lo_ready, c - NR + 1)
                for src, c0, n, at in blocks[i][2]:
                    sp.dma_start(w_raw[c % NR][:, at:at + n],
                                 src[k * P:(k + 1) * P, c0:c0 + n]).then_inc(w_in[c % NR], 16)

            for t in range(NT):
                sp.dma_start(xin[:, t, :], w["x"][t * P:(t + 1) * P, :]).then_inc(x_in[t], 16)
                if t == 0:
                    sp.dma_start(cst[:], w["cst"]).then_inc(const_in, 16)
                    sp.dma_start(gains[:, 0:NGAIN], w["gains"]).then_inc(const_in, 16)
            for j in range(2):
                sp.dma_start(w_up[:, j, :], w["w_kv_up"][j * P:(j + 1) * P, :]).then_inc(const_in, 16)
            first = number["ga0"] * KT + NR - 1
            zeros = list(range(NTILE))
            for c in range(min(first, len(chunks))):
                load_chunk(c)
                if c >= 8 and zeros:
                    i = zeros.pop()
                    sp.wait_ge(zero_done, 1)
                    sp.dma_start(xs_dram[i * P:(i + 1) * P, :].rearrange("p (a b) -> p a b", b=P),
                                 zero[:].unsqueeze(1).to_broadcast([P, D // P, P])).then_inc(zero_in, 16)
            if stop < 2:
                return

            def load_q(t):
                if t >= 2:
                    bk.wait_full(sp, ("qT", t - 2, 1))
                if t == 0:
                    for i in range(2):
                        sp.wait_ge(q_stored[i], 16 * NT)
                    sp.wait_ge(ret_stored, 16 * 2 * HR)
                sp.dma_start(qrow[t % 2][:].rearrange("p h d -> p (h d)"),
                             q_dram[t * P:(t + 1) * P, :]).then_inc(q_in[t % 2], 16)
            load_q(0)
            load_q(1)
            for t in range(NT):
                sp.wait_ge(aT_done, 2 * (t + 1))
                sp.dma_start(att_dram.rearrange("(h p) s -> p h s", p=P)[:, :, t * P:(t + 1) * P],
                             aT[t % 2][:]).then_inc(att_stored[t % 2], 16)
                if t + 2 < NT:
                    load_q(t + 2)
            if stop < 3:
                return
            sp.wait_ge(att_stored[0], 16 * NT // 2)
            sp.wait_ge(att_stored[1], 16 * NT // 2)
            for c in range(first, number["ba0"] * KT):
                load_chunk(c)
            for n, (name, k) in enumerate(act_chunks):
                load_chunk(number["ba0"] * KT + n)
                if n >= 2:
                    sp.wait_ge(a_lo_ready, n - 1)
                src = att_dram if name[:2] == "ba" else ret_dram
                sp.dma_start(a_raw[n % 2][:], src[k * P:(k + 1) * P, :]).then_inc(a_in[n % 2], 16)
            for c in range(number["wo0"] * KT, number["wo0"] * KT + NH - 1):
                load_chunk(c)
            sp.wait_ge(mix_lo, 16)
            sp.dma_start(xres[:], w["x"].rearrange("(t p) d -> p t d", p=P)).then_inc(xres_in, 16)
            for c in range(number["wo0"] * KT + NH - 1, len(chunks)):
                load_chunk(c)
            sp.dma_start(g2b[:], w["norm2_g"].partition_broadcast(P)).then_inc(rt_in, 16)
            sp.dma_start(w_rt[:], w["w_rt"].rearrange("(k p) n -> p k n", p=P)).then_inc(rt_in, 16)
            sp.dma_start(b_rt[:], w["b_rt"].partition_broadcast(P)).then_inc(rt_in, 16)
            for t in range(NT):
                sp.wait_ge(h_done, NT + t + 1)
                sp.dma_start(h_dram[t * P:(t + 1) * P, :], h_sb[:, t, :]).then_inc(h_stored, 16)
            if stop < 4:
                sp.wait_ge(h_stored, 16 * NT)
                return
            sp.wait_ge(owner_done, 1)

            def load_expert(i):
                e = sp.value_load(owner[0:1, i:i + 1], min_val=0, max_val=NE - 1)
                b = i % 2
                for j in range(2):
                    if i >= 2:
                        sp.wait_ge(elo_done[j], i - 1)
                    for at, src in ((0, w["w_gate"]), (FF, w["w_up"])):
                        rows = src[bass.ds(e * D, D), :].rearrange("(p k) f -> p (k f)", p=P)[:, j * 1024:(j + 1) * 1024]
                        sp.dma_start(e_raw[b][:, j * 2048 + at * 4:j * 2048 + at * 4 + 1024], rows).then_inc(ew_in[b][j], 16)
                if i >= 2:
                    sp.wait_ge(elo_done[2], i - 1)
                sp.dma_start(e_raw[b][:, 4096:], w["w_down"][bass.ds(e * FF, FF), :].rearrange("(p k) n -> p (k n)", p=P)).then_inc(ew_in[b][2], 16)

            def load_rows(i):
                if i >= 2:
                    sp.wait_ge(exT_full, i - 1)
                sp.dma_start(e_x[i % 2][:], xs_dram[i * P:(i + 1) * P, :]).then_inc(ex_in[i % 2], 16)
            load_expert(0)
            load_expert(1)
            sp.wait_ge(scattered, 16 * 2 * NT)
            load_rows(0)
            load_rows(1)
            for i in range(NTILE):
                if i + 2 < NTILE:
                    load_rows(i + 2)
                    load_expert(i + 2)
            sp.wait_ge(h_stored, 16 * NT)
            sp.wait_ge(ey_read, NTILE)
            for t in range(NT):
                if t >= 2:
                    sp.wait_ge(t_out[t % 2], 16 * (t // 2))
                sp.dma_start(t_h[t % 2][:], h_dram[t * P:(t + 1) * P, :]).then_inc(th_in[t % 2], 16)
                if t >= 1:
                    sp.wait_ge(t_sum, t)
                    sp.dma_start(out[(t - 1) * P:t * P, :], t_h[(t - 1) % 2][:]).then_inc(t_out[(t - 1) % 2], 16)
            sp.wait_ge(t_sum, NT)
            sp.dma_start(out[(NT - 1) * P:, :], t_h[(NT - 1) % 2][:]).then_inc(t_out[(NT - 1) % 2], 16)
            for i in range(2):
                sp.wait_ge(t_out[i], 16 * NT // 2)

        @block.tensor
        def _(pe):
            mm, tr = nc.tensor.matmul, nc.tensor.transpose

            def three(out, a, b, first, last, skip=False):
                mm(out, a[0], b[0], start=first, stop=False, skip_group_check=skip)
                mm(out, a[0], b[1], start=False, stop=False, skip_group_check=skip)
                return mm(out, a[1], b[0], start=False, stop=last, skip_group_check=skip)

            def gemm(name):
                i = number[name]
                kind = blocks[i][1]
                width = sum(p[2] for p in blocks[i][2])
                for k in range(KT):
                    c = i * KT + k
                    pe.wait_ge(lo_ready, c + 1)
                    if kind == "A":
                        n = act_chunks.index((name, k))
                        pe.wait_ge(a_lo_ready, n + 1)
                    wh, wl = w_hi[c % NH], w_lo[c % NH]
                    for b in range(8):
                        if k == 0:
                            bk.wait_free(pe, (name, b))
                        o = bank((name, b))
                        f, l = k == 0, k == KT - 1
                        if kind in ("R", "M"):
                            t = slice(b * P, (b + 1) * P)
                            last = three(o[:, :width], (n_hi[:, k, t], n_lo[:, k, t]),
                                         (wh[:, :width], wl[:, :width]), f, l)
                        elif kind in ("C", "A") or b < 4:
                            fs = slice(b // 2 * P, (b // 2 + 1) * P)
                            ts = slice(b % 2 * BANK, (b % 2 + 1) * BANK)
                            act = (a_hi[n % 2][:, ts], a_lo[n % 2][:, ts]) if kind == "A" else (n_hi[:, k, ts], n_lo[:, k, ts])
                            last = three(o, (wh[:, fs], wl[:, fs]), act, f, l)
                        else:
                            for s in range(2):
                                t = slice((2 * (b - 4) + s) * P, (2 * (b - 4) + s + 1) * P)
                                last = three(o[:, s * DV:(s + 1) * DV], (n_hi[:, k, t], n_lo[:, k, t]),
                                             (wh[:, 2 * DK:], wl[:, 2 * DK:]), f and s == 0, l, skip=True)
                        if l:
                            bk.filled(last, (name, b))
                        elif b == 7:
                            last.then_inc(chunk_used, 1)

            pe.wait_ge(const_in, 16 * 4)
            for half in range(2):
                pe.wait_ge(xn_done, 4 * (half + 1))
                for k in range(KT):
                    bk.wait_free(pe, ("xT", half, k))
                    for t in range(4):
                        last = tr(bank(("xT", half, k))[:, t * P:(t + 1) * P],
                                  xin[:, 4 * half + t, k * P:(k + 1) * P], ident)
                    bk.filled(last, ("xT", half, k))
            gemm("kv")
            gemm("qi")
            pe.wait_ge(ckv_n, 1)
            for j in range(2):
                for half in range(2):
                    bk.wait_free(pe, ("cT", j, half))
                    for t in range(4):
                        last = tr(bank(("cT", j, half))[:, t * P:(t + 1) * P],
                                  kvrows[:, 4 * half + t, j * P:(j + 1) * P], ident)
                    bk.filled(last, ("cT", j, half))
            for half in range(2):
                bk.wait_free(pe, ("kiT", half))
                for t in range(4):
                    last = tr(bank(("kiT", half))[:, t * P:(t + 1) * P],
                              kdup[:, 4 * half + t].rearrange("p a d -> p (a d)"), ident)
                bk.filled(last, ("kiT", half))
            for i in range(4):
                bk.wait_read(pe, ("cT", i // 2, i % 2))
            for i in range(4):
                bk.wait_free(pe, ("kvu", i))
                for s in range(2):
                    t = 2 * i + s
                    for j in range(2):
                        last = mm(bank(("kvu", i))[:, s * 2 * DH:(s + 1) * 2 * DH], cT[:, j, t * P:(t + 1) * P],
                                  w_up[:, j, :], start=j == 0, stop=j == 1)
                bk.filled(last, ("kvu", i))
            for half in range(2):
                pe.wait_ge(free[4 + half], bk.at[("kiT", half)][1])
            for half in range(2):
                pass
            pe.wait_ge(k_n, 1)
            for half in range(2):
                bk.wait_free(pe, ("kT", half))
                for t in range(4):
                    last = tr(bank(("kT", half))[:, t * P:(t + 1) * P], kvu[:, 4 * half + t, 0:DH], ident)
                bk.filled(last, ("kT", half))
            for t in range(2, NT):
                nk = (t + 1) * P
                for h in range(HI):
                    name = ("idx", t, h)
                    bk.wait_free(pe, name)
                    c = bk.col(name)
                    s = slice(h % 2 * DI, (h % 2 + 1) * DI)
                    for k0 in range(0, nk, BANK):
                        n = min(BANK, nk - k0)
                        last = mm(ps[:, c + k0:c + k0 + n], qiT[s, h // 2, t * P:(t + 1) * P],
                                  kiT[s, k0:k0 + n], start=True, stop=True)
                    bk.filled(last, name)

            def phase1(h):
                for half in range(2):
                    name = ("krow", h, half)
                    bk.wait_free(pe, name)
                    if half == 0:
                        for b in range(8):
                            pe.wait_ge(free[b], bk.at[(f"head{h}", b)][1])
                    for t in range(4):
                        cs = slice((4 * half + t) * P, (4 * half + t + 1) * P)
                        last = tr(bank(name)[:, t * P:(t + 1) * P], rkT[:, cs], ident)
                    bk.filled(last, name)
                for half in range(2):
                    name = ("sc", h, half)
                    bk.wait_free(pe, name)
                    for t in range(4):
                        cs = slice((4 * half + t) * P, (4 * half + t + 1) * P)
                        last = mm(bank(name)[:, t * P:(t + 1) * P], rkT[:, cs], rqT[h % 2][:, cs], start=True, stop=True)
                    bk.filled(last, name)
                for half in range(2):
                    pe.wait_ge(free[half], bk.at[("krow", h, half)][1])
                for i in range(4):
                    name = ("kvs", h, i)
                    bk.wait_free(pe, name)
                    for s in range(2):
                        c = 2 * i + s
                        if c < NT - 1:
                            last = mm(bank(name)[:, s * DV:(s + 1) * DV], krow[:, c, :], rv[h % 2][:, c, :], start=True, stop=True)
                    bk.filled(last, name)

            def phase2(h):
                pe.wait_ge(sT_done, h + 1)
                pe.wait_ge(state_done, h + 1)
                for i in range(4):
                    name = ("ro", h, i)
                    bk.wait_free(pe, name)
                    for s in range(2):
                        c = 2 * i + s
                        o = bank(name)[:, s * DV:(s + 1) * DV]
                        last = mm(o, sT[:, c, :], rv[h % 2][:, c, :], start=True, stop=c == 0)
                        if c:
                            last = mm(o, rqT[h % 2][:, c * P:(c + 1) * P], state[:, c - 1, :], start=False, stop=True)
                    bk.filled(last, name)

            def turn(h):
                pe.wait_ge(o_done, h + 1)
                for j in range(2):
                    for half in range(2):
                        name = ("rT", h, j, half)
                        bk.wait_free(pe, name)
                        for t in range(4):
                            last = tr(bank(name)[:, t * P:(t + 1) * P], ro[:, 4 * half + t, j * P:(j + 1) * P], ident)
                        bk.filled(last, name)
            for what, n in ret_order:
                {"block": gemm, "phase1": phase1, "phase2": phase2, "turn": turn}[what](n)
            if stop < 2:
                return
            for t in range(NT):
                nk = (t + 1) * P
                pe.wait_ge(q_in[t % 2], 16 * (t // 2 + 1))
                for g in range(2):
                    bk.wait_free(pe, ("qT", t, g))
                    for s in range(4):
                        last = tr(bank(("qT", t, g))[:, s * P:(s + 1) * P], qrow[t % 2][:, 4 * g + s, :], ident)
                    bk.filled(last, ("qT", t, g))
                pe.wait_ge(qT_done, 2 * (t + 1))
                for h2 in range(HA + 2):
                    if h2 < HA:
                        name = ("lg", t, h2)
                        bk.wait_free(pe, name)
                        c = bk.col(name)
                        for k0 in range(0, nk, BANK):
                            n = min(BANK, nk - k0)
                            last = mm(ps[:, c + k0:c + k0 + n], qT[t % 2][:, h2, :], kT[:, k0:k0 + n], start=True, stop=True)
                        bk.filled(last, name)
                    if h2 >= 2:
                        h = h2 - 2
                        pe.wait_ge(p_done, HA * t + h + 1)
                        for i in range(t // 4 + 1):
                            name = ("pT", t, h, i)
                            bk.wait_free(pe, name)
                            for kt in range(4 * i, min(4 * i + 4, t + 1)):
                                last = tr(bank(name)[:, kt % 4 * P:(kt % 4 + 1) * P], prob[h % 4][:, kt * P:(kt + 1) * P], ident)
                            bk.filled(last, name)
                        if h % 4 == 3:
                            g = h // 4
                            name = ("pv", t, g)
                            bk.wait_free(pe, name)
                            for i in range(t // 4 + 1):
                                b, n, _ = bk.at[("pT", t, h, i)]
                                pe.wait_ge(free[b], n)
                            for kt in range(t + 1):
                                last = mm(bank(name), kvu[:, kt, DH:2 * DH], pT[g][:, kt].rearrange("p h q -> p (h q)"),
                                          start=kt == 0, stop=kt == t)
                            bk.filled(last, name)
            if stop < 3:
                return
            for name in [b[0] for b in blocks[10:]]:
                if name == "wo0":
                    pe.wait_ge(mix_lo, 16)
                gemm(name)
            if stop < 4:
                return
            pe.wait_ge(rt_in, 48)
            for t in range(NT + 1):
                if t < NT:
                    pe.wait_ge(n2_done, t + 1)
                    for g in range(2):
                        name = ("n2T", t, g)
                        bk.wait_free(pe, name)
                        for k in range(4):
                            last = tr(bank(name)[:, k * P:(k + 1) * P], xres[:, t, (4 * g + k) * P:(4 * g + k + 1) * P], ident)
                        bk.filled(last, name)
                if t >= 1:
                    name = ("rt", t - 1)
                    bk.wait_free(pe, name)
                    for g in range(2):
                        bk.wait_read(pe, ("n2T", t - 1, g))
                    for k in range(KT):
                        last = mm(bank(name, NG + NE), n2T[(t - 1) % 2][:, k, :], w_rt[:, k, :], start=k == 0, stop=k == KT - 1)
                    bk.filled(last, name)
            pe.wait_ge(chosen, 1)
            name = ("rank",)
            bk.wait_free(pe, name)
            mm(bank(name, (NT + 1) * NE), cst[:, K_ONE:K_ONE + P], o_pre[:], start=True, stop=False, skip_group_check=True)
            bk.filled(mm(bank(name, NT * NE), cst[:, K_TRI:K_TRI + P], rs[:, 7, :], start=False, stop=True, skip_group_check=True), name)
            pe.wait_ge(ranked, 1)

            def turn_rows(i):
                pe.wait_ge(ex_in[i % 2], 16 * (i // 2 + 1))
                if i:
                    pe.wait_ge(exT_lo, i)
                for k in range(KT):
                    last = tr(ps[:, B_XT + k * P:B_XT + (k + 1) * P], e_x[i % 2][:].rearrange("s (p k) -> s k p", k=KT)[:, k, :], ident)
                last.then_inc(exT_full, 1)

            def gate_up(i):
                b = i % 2
                pe.wait_ge(exT_lo, i + 1)
                if i:
                    pe.wait_ge(gu_read, i)
                for k in range(KT):
                    if k % 4 == 0:
                        pe.wait_ge(elo_done[k // 4], i + 1)
                    wk = [e[b][:, k // 4 * 2048:(k // 4 + 1) * 2048].rearrange("p (a k f) -> p k a f", a=2, f=FF)[:, k % 4]
                          for e in (e_hi, e_lo)]
                    last = three(ps[:, B_GU:B_GU + 2 * FF].rearrange("p (a f) -> p a f", a=2),
                                 (x_hi[b][:, k, :], x_lo[b][:, k, :]), wk, k == 0, k == KT - 1)
                last.then_inc(gu_full, 1)

            def turn_act(i):
                pe.wait_ge(gu_read, i + 1)
                if i:
                    pe.wait_ge(eaT_lo, i)
                for k in range(2):
                    last = tr(ps[:, B_AT + k * P:B_AT + (k + 1) * P], arow[:].rearrange("s (p k) -> s k p", k=2)[:, k, :], ident)
                last.then_inc(eaT_full, 1)

            def down(i):
                b = i % 2
                pe.wait_ge(eaT_lo, i + 1)
                pe.wait_ge(elo_done[2], i + 1)
                if i:
                    pe.wait_ge(ey_read, i)
                for n in range(2):
                    for k in range(2):
                        ws = slice(4096 + k * D + n * BANK, 4096 + k * D + (n + 1) * BANK)
                        last = three(ps[:, B_Y + n * BANK:B_Y + (n + 1) * BANK], (at_hi[:, k, :], at_lo[:, k, :]),
                                     (e_hi[b][:, ws], e_lo[b][:, ws]), k == 0, k == 1)
                last.then_inc(ey_full, 1)
            turn_rows(0)
            for i in range(NTILE + 1):
                if i:
                    turn_act(i - 1)
                if i < NTILE:
                    gate_up(i)
                if i:
                    down(i - 1)
                if i + 1 < NTILE:
                    turn_rows(i + 1)

        @block.scalar
        def _(act):
            seq = Seq(act, s_act)
            A = nc.scalar.activation

            def hi(c):
                if c >= len(chunks):
                    return
                i, k = chunks[c]
                width = sum(p[2] for p in blocks[i][2])
                act.wait_ge(w_in[c % NR], landed[c])
                if c >= NH:
                    act.wait_ge(*used(c - NH))
                nc.scalar.copy(w_hi[c % NH][:, :width], w_raw[c % NR][:, :width]).then_inc(hi_ready, 1)

            act.wait_ge(const_in, 16 * 4)
            for t in range(NT):
                act.wait_ge(x_in[t], 16)
                if t >= 2:
                    act.wait_ge(sq_done, t - 1)
                A(junk[:, t % 2, :], xin[:, t, :], ACT.Square, accum_out=small[:, t:t + 1]).then_inc(sq_done, 1)
            for c in range(NH - 1):
                hi(c)
            for half in range(2):
                for k in range(KT):
                    name = ("xT", half, k)
                    bk.wait_full(act, name)
                    A(n_hi[:, k, half * BANK:(half + 1) * BANK], bank(name), ACT.Identity,
                      scale=gains[:, G1 + k:G1 + k + 1]).then_inc(nhi_done, 1)

            def ahead(name):
                for k in range(KT):
                    hi(number[name] * KT + k + NH - 1)
            ahead("kv")
            for t in range(NT):
                bk.wait_full(act, ("kv", t))
                if t == 0:
                    act.wait_ge(nhi_done, 16)
                bk.read(nc.scalar.copy(kvrows[:, t, :], bank(("kv", t), KVW)), ("kv", t))
            ahead("qi")
            for b in range(8):
                bk.wait_full(act, ("qi", b))
                bk.read(nc.scalar.copy(qiT[:, b // 2, b % 2 * BANK:(b % 2 + 1) * BANK], bank(("qi", b))), ("qi", b))
            act.wait_ge(gains_done, 1)
            for j in range(2):
                for half in range(2):
                    name = ("cT", j, half)
                    bk.wait_full(act, name)
                    bk.read(A(cT[:, j, half * BANK:(half + 1) * BANK], bank(name), ACT.Identity,
                              scale=gains[:, GKV + j:GKV + j + 1]), name)
            for half in range(2):
                name = ("kiT", half)
                bk.wait_full(act, name)
                bk.read(A(kiT[:, half * BANK:(half + 1) * BANK], bank(name), ACT.Identity,
                          scale=gains[:, GKI:GKI + 1]), name)
            for i in range(4):
                name = ("kvu", i)
                bk.wait_full(act, name)
                bk.read(nc.scalar.copy(kvu[:, 2 * i:2 * i + 2, :].rearrange("p t d -> p (t d)"), bank(name)), name)
            for half in range(2):
                name = ("kT", half)
                bk.wait_full(act, name)
                bk.read(A(kT[:, half * BANK:(half + 1) * BANK], bank(name), ACT.Identity,
                          scale=gains[:, GK:GK + 1]), name)
            n = 0
            for t in range(2, NT):
                nk = (t + 1) * P
                for h in range(HI):
                    name = ("idx", t, h)
                    bk.wait_full(act, name)
                    if n >= 2:
                        act.wait_ge(relu_used, n - 1)
                    c = bk.col(name)
                    bk.read(A(relu[n % 2][:, :nk], ps[:, c:c + nk], ACT.Relu), name)
                    n += 1

            def out_gate(p):
                if p:
                    act.wait_ge(o_done, 2 * p)
                for t in range(NT):
                    name = (f"gate{p}", t)
                    bk.wait_full(act, name)
                    if t == 0 and p == 0:
                        act.wait_ge(relu_used, n)
                    bk.read(A(gate[:, t, :], bank(name), ACT.Silu), name)

            def out_head(h):
                for b in range(8):
                    name = (f"head{h}", b)
                    bk.wait_full(act, name)
                    if b < 2:
                        dst = rqT[h % 2][:, b * BANK:(b + 1) * BANK]
                    elif b < 4:
                        dst = rkT[:, (b - 2) * BANK:(b - 1) * BANK]
                    else:
                        dst = rv[h % 2][:, 2 * (b - 4):2 * (b - 4) + 2, :].rearrange("p t d -> p (t d)")
                    bk.read(nc.scalar.copy(dst, bank(name)), name)

            def out_q(b):
                for t in range(NT):
                    n = b * NT + t
                    name = (f"q{b}", t)
                    bk.wait_full(act, name)
                    if n >= 2:
                        act.wait_ge(q_stored[n % 2], 16 * (n // 2))
                    nc.scalar.copy(qst[n % 2][:], bank(name)).then_inc(q_copied, 1)
                    act.wait_ge(q_copied, n + 1)
                    for h in range(4):
                        inst = A(junk2[:, h % 2 * P:(h % 2 + 1) * P], bank(name)[:, h * DH:(h + 1) * DH], ACT.Square,
                                 accum_out=small[:, 64 + 4 * (n % 2) + h:65 + 4 * (n % 2) + h])
                        if h == 3:
                            bk.read(inst, name)
                        else:
                            seq(inst)

            def out_phase1(h):
                for half in range(2):
                    name = ("krow", h, half)
                    bk.wait_full(act, name)
                    bk.read(A(krow[:, 4 * half:4 * half + 4, :].rearrange("p t d -> p (t d)"), bank(name), ACT.Identity,
                              scale=cst[:, K_KD + h:K_KD + h + 1]), name)
                for half in range(2):
                    name = ("sc", h, half)
                    bk.wait_full(act, name)
                    bk.read(nc.scalar.copy(sT[:, 4 * half:4 * half + 4, :].rearrange("p t d -> p (t d)"), bank(name)), name)
                for i in range(4):
                    name = ("kvs", h, i)
                    bk.wait_full(act, name)
                    m = min(2, NT - 1 - 2 * i)
                    bk.read(nc.scalar.copy(state[:, 2 * i:2 * i + m, :].rearrange("p t d -> p (t d)"), bank(name, m * DV)), name)

            def out_phase2(h):
                if h:
                    act.wait_ge(full[7], bk.at[("rT", h - 1, 1, 1)][1])
                for i in range(4):
                    name = ("ro", h, i)
                    bk.wait_full(act, name)
                    for s in range(2):
                        c = 2 * i + s
                        inst = A(ro[:, c, :], bank(name)[:, s * DV:(s + 1) * DV], ACT.Identity,
                                 scale=cst[:, K_QD + h:K_QD + h + 1], accum_out=small[:, 96 + c:97 + c])
                        bk.read(inst, name) if s else seq(inst)
                act.wait_ge(o_mu, h + 1)
                for c in range(NT):
                    seq(A(junk2[:], ro[:, c, :], ACT.Square, bias=small[:, 104 + c:105 + c],
                          accum_out=small[:, 112 + c:113 + c])) if c < NT - 1 else \
                        A(junk2[:], ro[:, c, :], ACT.Square, bias=small[:, 104 + c:105 + c],
                          accum_out=small[:, 112 + c:113 + c]).then_inc(o_var, 1)
                act.wait_ge(o_var, h + 1)

            def out_turn(h):
                for j in range(2):
                    if h or j:
                        act.wait_ge(ret_stored, 16 * (2 * h + j))
                    for half in range(2):
                        name = ("rT", h, j, half)
                        bk.wait_full(act, name)
                        bk.read(A(rT[:, half * BANK:(half + 1) * BANK], bank(name), ACT.Identity,
                                  scale=gains[:, GRT + 2 * h + j:GRT + 2 * h + j + 1]), name)
                    for half in range(2):
                        act.wait_ge(free[bk.at[("rT", h, j, half)][0]], bk.at[("rT", h, j, half)][1])
                    act.dma_start(ret_dram[(2 * h + j) * P:(2 * h + j + 1) * P, :], rT[:]).then_inc(ret_stored, 16)

            def out_block(name):
                ahead(name)
                kind, i = name[:-1], int(name[-1])
                {"gate": out_gate, "head": out_head, "q": out_q}[kind](i)
            for what, m in ret_order:
                {"block": out_block, "phase1": out_phase1, "phase2": out_phase2, "turn": out_turn}[what](m)
            if stop < 2:
                act.wait_ge(ret_stored, 16 * 2 * HR)
                return
            for t in range(NT):
                nk = (t + 1) * P
                for g in range(2):
                    name = ("qT", t, g)
                    bk.wait_full(act, name)
                    inst = nc.scalar.copy(qT[t % 2][:, 4 * g:4 * g + 4, :].rearrange("p h q -> p (h q)"), bank(name))
                    bk.read(inst, name)
                for h2 in range(HA + 1):
                    if h2 < HA:
                        m = HA * t + h2
                        act.wait_ge(mx_done, m + 1)
                        if True:
                            A(prob[h2 % 4][:, :nk], prob[h2 % 4][:, :nk], ACT.Exp, bias=small[:, 128 + h2:129 + h2],
                              scale=2.0 ** -(h2 + 1), accum_out=small[:, 144 + h2:145 + h2]).then_inc(ex_done, 1)
                    if h2 >= 1:
                        h = h2 - 1
                        g = h // 4
                        for i in range(t // 4 + 1):
                            name = ("pT", t, h, i)
                            bk.wait_full(act, name)
                            m = min(4, t + 1 - 4 * i)
                            bk.read(nc.scalar.copy(pT[g][:, 4 * i:4 * i + m, h % 4, :],
                                                   bank(name, m * P).rearrange("p (k q) -> p k q", q=P)), name)
                        if h % 4 == 3:
                            name = ("pv", t, g)
                            bk.wait_full(act, name)
                            if t >= 2 and g == 0:
                                act.wait_ge(att_stored[t % 2], 16 * (t // 2))
                            bk.read(nc.scalar.copy(aT[t % 2][:, 4 * g:4 * g + 4, :].rearrange("p h q -> p (h q)"), bank(name)), name)
            if stop < 3:
                return
            for n, name in enumerate(("ga0", "ga1", "gr0", "gr1")):
                ahead(name)
                if n == 0:
                    for i in range(2):
                        act.wait_ge(att_stored[i], 16 * NT // 2)
                for b in range(8):
                    bk.wait_full(act, (name, b))
                    bk.read(A(sig[n][:, b // 2, b % 2 * BANK:(b % 2 + 1) * BANK], bank((name, b)), ACT.Sigmoid), (name, b))

            def a_part(n):
                if n >= len(act_chunks):
                    return
                act.wait_ge(a_in[n % 2], 16 * (n // 2 + 1))
                if n >= 2:
                    c = number["ba0"] * KT + n - 2
                    act.wait_ge(*used(c))
                nc.scalar.copy(a_hi[n % 2][:], a_raw[n % 2][:]).then_inc(a_hi_ready, 1)
            a_part(0)
            for n, (name, k) in enumerate(act_chunks):
                a_part(n + 1)
                hi(number["ba0"] * KT + n + NH - 1)
                if k == KT - 1 and name[:2] == "br":
                    bi = int(name[-1])
                    for b in range(8):
                        f, half = b // 2, b % 2
                        m = bi * 8 + b
                        act.wait_ge(mixed, m + 1)
                        nc.scalar.copy(n_hi[:, 4 * bi + f, half * BANK:(half + 1) * BANK],
                                       sig[2 + bi][:, f, half * BANK:(half + 1) * BANK]).then_inc(mix_hi, 1)
            ahead("wo0")
            ahead("wo1")
            if stop < 4:
                return
            for t in range(NT + 1):
                if t < NT:
                    act.wait_ge(h_done, NT + t + 1)
                    A(sig[3][:, t % 2, :] if False else n2sq[:], h_sb[:, t, :], ACT.Square, accum_out=small[:, 280 + t:281 + t]).then_inc(h_sq, 1)
                    act.wait_ge(h_sq, t + 1)
                if t >= 1:
                    for g in range(2):
                        name = ("n2T", t - 1, g)
                        bk.wait_full(act, name)
                        bk.read(nc.scalar.copy(n2T[(t - 1) % 2][:, 4 * g:4 * g + 4, :].rearrange("p k q -> p (k q)"), bank(name)), name)
            act.wait_ge(g_shift, 1)
            A(rs[:, 1, 0:NT * NG], rs[:, 1, 0:NT * NG], ACT.Exp).then_inc(g_exp, 1)
            act.wait_ge(e_shift, 1)
            A(rs[:, 8, 0:NT], rs[:, 8, 0:NT], ACT.Exp).then_inc(e_exp, 1)

            def w_part(i, j):
                b = i % 2
                act.wait_ge(ew_in[b][j], (32, 32, 16)[j] * (i // 2 + 1))
                if i >= 2:
                    act.wait_ge(ey_full if j == 2 else gu_full, i - 1)
                ws = slice(j * 2048, (j + 1) * 2048)
                nc.scalar.copy(e_hi[b][:, ws], e_raw[b][:, ws]).then_inc(ehi_done[j], 1)

            def x_part(i):
                act.wait_ge(exT_full, i + 1)
                if i >= 2:
                    act.wait_ge(gu_full, i - 1)
                nc.scalar.copy(x_hi[i % 2][:].rearrange("p k q -> p (k q)"), ps[:, B_XT:B_XT + D]).then_inc(exT_hi, 1)
            act.wait_ge(slot_done, 1)
            for j in range(3):
                w_part(0, j)
            x_part(0)
            for i in range(NTILE):
                if i:
                    act.wait_ge(eaT_full, i)
                    if i >= 2:
                        act.wait_ge(ey_full, i - 1)
                    nc.scalar.copy(at_hi[:].rearrange("p k q -> p (k q)"), ps[:, B_AT:B_AT + FF]).then_inc(eaT_hi, 1)
                if i + 1 < NTILE:
                    w_part(i + 1, 0)
                    w_part(i + 1, 1)
                act.wait_ge(gu_full, i + 1)
                if i:
                    act.wait_ge(gu_read, i)
                A(gated[:], ps[:, B_GU:B_GU + FF], ACT.Silu).then_inc(gu_silu, 1)
                if i + 1 < NTILE:
                    x_part(i + 1)
                    w_part(i + 1, 2)
            act.wait_ge(eaT_full, NTILE)
            act.wait_ge(ey_full, NTILE - 1)
            nc.scalar.copy(at_hi[:].rearrange("p k q -> p (k q)"), ps[:, B_AT:B_AT + FF]).then_inc(eaT_hi, 1)

        @block.vector
        def _(dve):
            seq = Seq(dve, s_dve)
            V = nc.vector
            dve.wait_ge(const_in, 16 * 4)
            seq(V.scalar_tensor_tensor(gains[:, GK:GK + 1], gains[:, GQ:GQ + 1], DH ** -0.5, gains[:, GK:GK + 1], ALU.mult, ALU.mult))
            V.tensor_scalar(gains[:, GKI:GKI + 1], gains[:, GKI:GKI + 1], DI ** -0.5, None, ALU.mult).then_inc(gains_done, 1)
            for half in range(2):
                dve.wait_ge(rstd1, half + 1)
                for t in range(4 * half, 4 * half + 4):
                    V.tensor_scalar(xin[:, t, :], xin[:, t, :], small[:, 8 + t:9 + t], None, ALU.mult).then_inc(xn_done, 1)
            for half in range(2):
                for k in range(KT):
                    name = ("xT", half, k)
                    dve.wait_ge(nhi_done, half * KT + k + 1)
                    hs = slice(half * BANK, (half + 1) * BANK)
                    bk.read(V.scalar_tensor_tensor(n_lo[:, k, hs], bank(name), gains[:, G1 + k:G1 + k + 1],
                                                   n_hi[:, k, hs].bitcast(F32), ALU.mult, ALU.subtract), name)
            for t in range(NT):
                dve.wait_ge(free[t], bk.at[("kv", t)][1])
            seq(V.tensor_tensor(sq[:], kvrows[:], kvrows[:], ALU.mult))
            seq(V.tensor_reduce(small[:, 16:24], sq[:, :, 0:KVL], X, ALU.add))
            V.tensor_reduce(small[:, 24:32], sq[:, :, KVL:KVL + DI], X, ALU.add).then_inc(kv_sq, 1)
            dve.wait_ge(kv_rstd, 1)
            seq(V.tensor_tensor(kdup[:, :, 0, :], kvrows[:, :, KVL:KVL + DI], small[:, 40:48].unsqueeze(2).to_broadcast([P, NT, DI]), ALU.mult))
            seq(V.tensor_copy(kdup[:, :, 1, :], kdup[:, :, 0, :]))
            seq(V.tensor_scalar(small[:, 192:256].rearrange("p (t h) -> p t h", h=HI), kvrows[:, :, KVL + DI:KVW], HI ** -0.5, None, ALU.mult))
            V.tensor_tensor(kvrows[:, :, 0:KVL], kvrows[:, :, 0:KVL], small[:, 32:40].unsqueeze(2).to_broadcast([P, NT, KVL]), ALU.mult).then_inc(ckv_n, 1)
            for i in range(4):
                dve.wait_ge(free[i], bk.at[("kvu", i)][1])
            ksq = sq[:].rearrange("p t d -> p (t d)")[:, 0:S].rearrange("p (t d) -> p t d", d=DH)
            seq(V.tensor_tensor(ksq, kvu[:, :, 0:DH], kvu[:, :, 0:DH], ALU.mult))
            V.tensor_reduce(small[:, 48:56], ksq, X, ALU.add).then_inc(k_sq, 1)
            dve.wait_ge(k_rstd, 1)
            V.tensor_tensor(kvu[:, :, 0:DH], kvu[:, :, 0:DH], small[:, 56:64].unsqueeze(2).to_broadcast([P, NT, DH]), ALU.mult).then_inc(k_n, 1)
            n = 0
            for t in range(2, NT):
                nk = (t + 1) * P
                sc = dist[:, tile_off(t):tile_off(t) + nk]
                for h in range(HI):
                    b, cnt, _ = bk.at[("idx", t, h)]
                    dve.wait_ge(free[b], cnt)
                    wv = small[:, 192 + t * HI + h:193 + t * HI + h]
                    if n:
                        dve.wait_ge(relu_used, n)
                    if h == 0:
                        V.tensor_scalar(sc, relu[n % 2][:, :nk], wv, None, ALU.mult).then_inc(relu_used, 1)
                    else:
                        V.scalar_tensor_tensor(sc, relu[n % 2][:, :nk], wv, sc, ALU.mult, ALU.add).then_inc(relu_used, 1)
                    n += 1
                dve.wait_ge(relu_used, n)
                seq(V.tensor_tensor(sc[:, t * P:], sc[:, t * P:], cst[:, K_CAUS:K_CAUS + P], ALU.add))
            for t in range(NT):
                nk = (t + 1) * P
                sc = dist[:, tile_off(t):tile_off(t) + nk]
                if nk <= TOPK:
                    seq(V.tensor_scalar(sc, cst[:, K_REL:K_REL + nk], float(-t * P), None, ALU.add))
                    V.tensor_tensor(sc[:, t * P:], sc[:, t * P:], cst[:, K_CAUS:K_CAUS + P], ALU.add).then_inc(dist_done, 1)
                    dve.wait_ge(dist_done, t + 1)
                    continue
                for r in range(TOPK // 8):
                    m8 = small[:, 256 + r % 2 * 8:264 + r % 2 * 8]
                    seq(V.max(m8, sc))
                    seq(V.match_replace(sc, m8, sc, TAKEN))
                seq(V.tensor_scalar(sc, sc, TAKEN, -BIG, ALU.not_equal, ALU.mult))
                V.scalar_tensor_tensor(sc, cst[:, K_REL:K_REL + nk], float(-t * P), sc, ALU.add, ALU.add).then_inc(dist_done, 1)
                dve.wait_ge(dist_done, t + 1)
            if stop < 2:
                return
            for t in range(NT):
                nk = (t + 1) * P
                sc = dist[:, tile_off(t):tile_off(t) + nk]
                for g in range(2):
                    b, cnt, _ = bk.at[("qT", t, g)]
                    dve.wait_ge(free[b], cnt)
                    V.memset(small[:, 272 + g:273 + g], 0.0).then_inc(qT_done, 1)
                    dve.wait_ge(qT_done, 2 * t + g + 1)
                for h2 in range(HA + 1):
                    if h2 < HA:
                        name = ("lg", t, h2)
                        m = HA * t + h2
                        bk.wait_full(dve, name)
                        c = bk.col(name)
                        if h2 >= 4:
                            for i in range(t // 4 + 1):
                                b, cnt, _ = bk.at[("pT", t, h2 - 4, i)]
                                dve.wait_ge(full[b], cnt)
                        V.tensor_tensor_reduce(out=prob[h2 % 4][:, :nk], in0=ps[:, c:c + nk], in1=sc, scale=1.0, scalar=-3e38,
                                               op0=ALU.add, op1=ALU.max, accum_out=small[:, 160 + h2:161 + h2]).then_inc(free[bk.at[name][0]], 1)
                        dve.wait_ge(free[bk.at[name][0]], bk.at[name][1])
                        V.tensor_scalar(small[:, 128 + h2:129 + h2], small[:, 160 + h2:161 + h2], -(2.0 ** -(h2 + 1)), None, ALU.mult).then_inc(mx_done, 1)
                    if h2 >= 1:
                        h = h2 - 1
                        m = HA * t + h
                        dve.wait_ge(ex_done, m + 1)
                        seq(V.reciprocal(small[:, 152 + h % 2:153 + h % 2], small[:, 144 + h:145 + h]))
                        V.tensor_scalar(prob[h % 4][:, :nk], prob[h % 4][:, :nk], small[:, 152 + h % 2:153 + h % 2], None, ALU.mult).then_inc(p_done, 1)
                        dve.wait_ge(p_done, m + 1)
                for g in range(2):
                    b, cnt, _ = bk.at[("pv", t, g)]
                    dve.wait_ge(free[b], cnt)
                    V.memset(small[:, 274 + g:275 + g], 0.0).then_inc(aT_done, 1)
                    dve.wait_ge(aT_done, 2 * t + g + 1)
            if stop < 3:
                return

            def a_part(n):
                if n >= len(act_chunks):
                    return
                dve.wait_ge(a_hi_ready, n + 1)
                V.tensor_tensor(a_lo[n % 2][:], a_raw[n % 2][:], a_hi[n % 2][:].bitcast(F32), ALU.subtract).then_inc(a_lo_ready, 1)
            a_part(0)
            for n, (name, k) in enumerate(act_chunks):
                a_part(n + 1)
                if k < KT - 1:
                    continue
                bi = int(name[-1])
                for b in range(8):
                    f, half = b // 2, b % 2
                    hs = slice(half * BANK, (half + 1) * BANK)
                    sa, sr = sig[bi][:, f, hs], sig[2 + bi][:, f, hs]
                    bk.wait_full(dve, (name, b))
                    cnt = bk.at[(name, b)][1]
                    if name[:2] == "ba":
                        bk.read(V.tensor_tensor(sa, sa, bank((name, b)), ALU.mult), (name, b))
                    else:
                        m = bi * 8 + b
                        dve.wait_ge(free[b], bk.at[(f"ba{bi}", b)][1])
                        bk.read(V.tensor_tensor(sr, sr, bank((name, b)), ALU.mult), (name, b))
                        dve.wait_ge(free[b], cnt)
                        V.tensor_tensor(sr, sr, sa, ALU.add).then_inc(mixed, 1)
                        dve.wait_ge(mix_hi, m + 1)
                        V.tensor_tensor(n_lo[:, 4 * bi + f, hs], sr, n_hi[:, 4 * bi + f, hs].bitcast(F32), ALU.subtract).then_inc(mix_lo, 1)
            dve.wait_ge(xres_in, 16)
            for bi in range(2):
                for t in range(NT):
                    name = (f"wo{bi}", t)
                    bk.wait_full(dve, name)
                    cs = slice(bi * BANK, (bi + 1) * BANK)
                    V.tensor_tensor(h_sb[:, t, cs], xres[:, t, cs], bank(name), ALU.add).then_inc(h_done, 1)
                    dve.wait_ge(h_done, bi * NT + t + 1)
                    if bi == 0:
                        bk.read(V.memset(small[:, 276:277], 0.0), name)
                        dve.wait_ge(free[t], bk.at[name][1])
                    else:
                        bk.read(V.memset(small[:, 276:277], 0.0), name)
                        dve.wait_ge(free[t], bk.at[name][1])
            if stop < 4:
                return
            dve.wait_ge(rt_in, 48)
            for t in range(NT + 1):
                if t < NT:
                    dve.wait_ge(h_rstd, t + 1)
                    V.scalar_tensor_tensor(xres[:, t, :], h_sb[:, t, :], small[:, 288 + t:289 + t], g2b[:], ALU.mult, ALU.mult).then_inc(n2_done, 1)
                if t >= 1:
                    name = ("rt", t - 1)
                    bk.wait_full(dve, name)
                    bk.read(V.tensor_tensor(lgt[:, t - 1, :], bank(name, NG + NE), b_rt[:], ALU.add), name)
            for t in range(NT - 2, NT):
                bk.wait_read(dve, ("rt", t))

            def r(i, n=NT * NE):
                return rs[:, i, 0:n]

            def r3(i, n=NE):
                return rs[:, i, 0:NT * n].rearrange("p (t e) -> p t e", e=n)

            def wide(a, n=NE):
                return a.unsqueeze(2).to_broadcast([P, NT, n])
            gl, el = lgt[:, :, 0:NG], lgt[:, :, NG:]

            def first_of_max(dst, src, top, pri, n):
                seq(V.tensor_reduce(top, src, X, ALU.max))
                seq(V.tensor_tensor(dst, src, wide(top, n), ALU.is_equal))
                seq(V.tensor_tensor(dst, dst, cst[:, pri:pri + n].unsqueeze(1).to_broadcast([P, NT, n]), ALU.mult))
                seq(V.tensor_reduce(r(15, NT), dst, X, ALU.max))
                seq(V.tensor_tensor(dst, dst, wide(r(15, NT), n), ALU.is_equal))
            first_of_max(r3(0, NG), gl, r(9, NT), K_P4, NG)
            V.tensor_tensor(r3(1, NG), gl, wide(r(9, NT), NG), ALU.subtract).then_inc(g_shift, 1)
            seq(V.tensor_scalar(r(2, NT * NG), r(0, NT * NG), 1.0, BIG, ALU.subtract, ALU.mult))
            for e in range(EPG):
                el_e = el.rearrange("p t (g e) -> p t g e", e=EPG)[:, :, :, e]
                em_e = r3(3).rearrange("p t (g e) -> p t g e", e=EPG)[:, :, :, e]
                seq(V.tensor_tensor(em_e, el_e, r3(0, NG), ALU.mult))
                seq(V.tensor_tensor(em_e, em_e, r3(2, NG), ALU.add))
            first_of_max(r3(4), r3(3), r(10, NT), K_P16, NE)
            seq(V.scalar_tensor_tensor(r(5), r(4), -3 * BIG, r(3), ALU.mult, ALU.add))
            first_of_max(r3(6), r3(5), r(11, NT), K_P16, NE)
            V.tensor_tensor(r(8, NT), r(11, NT), r(10, NT), ALU.subtract).then_inc(e_shift, 1)
            seq(V.tensor_tensor(r(7), r(4), r(6), ALU.add))
            seq(V.memset(o_pre[:, 0:NE], 0.0))
            for t in range(NT):
                inst = V.tensor_tensor(o_pre[:, (t + 1) * NE:(t + 2) * NE], o_pre[:, t * NE:(t + 1) * NE], r3(7)[:, t, :], ALU.add)
                seq(inst) if t < NT - 1 else inst.then_inc(chosen, 1)
            dve.wait_ge(g_exp, 1)
            seq(V.tensor_reduce(r(12, NT), r3(1, NG), X, ALU.add))
            seq(V.reciprocal(r(12, NT), r(12, NT)))
            dve.wait_ge(e_exp, 1)
            seq(V.tensor_scalar(r(13, NT), r(8, NT), 1.0, None, ALU.add))
            seq(V.reciprocal(r(13, NT), r(13, NT)))
            p1, p2 = small[:, 304:312], small[:, 312:320]
            seq(V.tensor_tensor(p1, r(12, NT), r(13, NT), ALU.mult))
            seq(V.tensor_tensor(p2, p1, r(8, NT), ALU.mult))
            bk.wait_full(dve, ("rank",))
            c = bk.col(("rank",))
            seq(V.tensor_copy(small[:, 320:336], ps[:, c + NT * NE:c + (NT + 1) * NE]))
            seq(V.tensor_tensor(r3(0, NT) if False else rs[:, 0, 0:NE * NT].rearrange("p (e m) -> p e m", m=NT),
                                small[:, 320:336].unsqueeze(2).to_broadcast([P, NE, NT]),
                                cst[:, K_THR:K_THR + NE * NT].rearrange("p (e m) -> p e m", m=NT), ALU.is_gt))
            seq(V.tensor_reduce(small[:, 336:352], rs[:, 0, 0:NE * NT].rearrange("p (e m) -> p e m", m=NT), X, ALU.add))
            two = rs[:, 0:2, :].rearrange("p a n -> p (a n)").rearrange("p (e f) -> p e f", f=NE)
            seq(V.tensor_tensor(two, cst[:, K_EXC:K_EXC + NE * NE].rearrange("p (e f) -> p e f", f=NE),
                                small[:, 336:352].unsqueeze(1).to_broadcast([P, NE, NE]), ALU.mult))
            seq(V.tensor_reduce(small[:, 352:368], two, X, ALU.add))
            seq(V.tensor_tensor(small[:, 368:384], small[:, 352:368], small[:, 336:352], ALU.add))
            four = rs[:, 0:4, :].rearrange("p a n -> p (a n)").rearrange("p (i e) -> p i e", e=NE)
            seq(V.tensor_tensor(four, small[:, 368:384].unsqueeze(1).to_broadcast([P, 32, NE]),
                                cst[:, K_TI:K_TI + 32].unsqueeze(2).to_broadcast([P, 32, NE]), ALU.is_le))
            seq(V.tensor_reduce(small[:, 384:416], four, X, ALU.add))
            V.tensor_scalar(owner[:], small[:, 384:416], float(NE - 1), None, ALU.min).then_inc(owner_done, 1)
            seq(V.tensor_scalar(small[:, 352:368], small[:, 352:368], float(P), None, ALU.mult))
            V.tensor_tensor(r3(5), ps[:, c:c + NT * NE].rearrange("p (t e) -> p t e", e=NE),
                            small[:, 352:368].unsqueeze(1).to_broadcast([P, NT, NE]), ALU.add).then_inc(ranked, 1)
            dve.wait_ge(ranked, 1)
            for j, oh in ((0, 4), (1, 6)):
                seq(V.tensor_tensor(r(oh), r(oh), r(5), ALU.mult))
                seq(V.tensor_reduce(small[:, 416 + 8 * j:424 + 8 * j], r3(oh), X, ALU.add))
            V.tensor_copy(slot[:].rearrange("p j t -> p (j t)"), small[:, 416:432]).then_inc(slot_done, 1)

            def w_part(i, j):
                b = i % 2
                dve.wait_ge(ehi_done[j], i + 1)
                ws = slice(j * 2048, (j + 1) * 2048)
                V.tensor_tensor(e_lo[b][:, ws], e_raw[b][:, ws], e_hi[b][:, ws].bitcast(F32), ALU.subtract).then_inc(elo_done[j], 1)

            def x_part(i):
                dve.wait_ge(exT_hi, i + 1)
                V.tensor_tensor(x_lo[i % 2][:].rearrange("p k q -> p (k q)"), ps[:, B_XT:B_XT + D],
                                x_hi[i % 2][:].rearrange("p k q -> p (k q)").bitcast(F32), ALU.subtract).then_inc(exT_lo, 1)

            def a_part2(i):
                dve.wait_ge(eaT_hi, i + 1)
                V.tensor_tensor(at_lo[:].rearrange("p k q -> p (k q)"), ps[:, B_AT:B_AT + FF],
                                at_hi[:].rearrange("p k q -> p (k q)").bitcast(F32), ALU.subtract).then_inc(eaT_lo, 1)

            def rows_out(i):
                dve.wait_ge(ey_full, i + 1)
                if i >= 2:
                    dve.wait_ge(ey_out[i % 2], 16 * (i // 2))
                V.tensor_copy(e_y[i % 2][:], ps[:, B_Y:B_Y + D]).then_inc(ey_read, 1)
            dve.wait_ge(scattered, 16 * 2 * NT)
            w_part(0, 0)
            w_part(0, 2)
            x_part(0)
            for i in range(NTILE):
                if i:
                    a_part2(i - 1)
                if i + 1 < NTILE:
                    w_part(i + 1, 0)
                dve.wait_ge(gu_silu, i + 1)
                if i:
                    dve.wait_ge(eaT_full, i)
                V.tensor_tensor(arow[:], gated[:], ps[:, B_GU + FF:B_GU + 2 * FF], ALU.mult).then_inc(gu_read, 1)
                if i:
                    rows_out(i - 1)
                if i + 1 < NTILE:
                    x_part(i + 1)
                    w_part(i + 1, 2)
            a_part2(NTILE - 1)
            rows_out(NTILE - 1)
            for t in range(NT):
                b = t % 2
                dve.wait_ge(ty_in[b], 32 * (t // 2 + 1))
                dve.wait_ge(th_in[b], 16 * (t // 2 + 1))
                V.scalar_tensor_tensor(t_h[b][:], t_y[b][0][:], small[:, 304 + t:305 + t], t_h[b][:], ALU.mult, ALU.add).then_inc(t_half, 1)
                dve.wait_ge(t_half, t + 1)
                V.scalar_tensor_tensor(t_h[b][:], t_y[b][1][:], small[:, 312 + t:313 + t], t_h[b][:], ALU.mult, ALU.add).then_inc(t_sum, 1)

        @block.gpsimd
        def _(pool):
            seq = Seq(pool, s_pool)
            G = nc.gpsimd
            nhalf = cst[:, K_NH:K_NH + 1]

            def rstd(dst, src, n, width, last=None):
                seq(G.tensor_scalar(dst, src, 1.0 / width, EPS, ALU.mult, ALU.add))
                inst = G.tensor_tensor(dst, dst, nhalf.to_broadcast([P, n]), ALU.pow)
                if last is None:
                    seq(inst)
                else:
                    inst.then_inc(*last)

            def lo(c):
                if c >= len(chunks):
                    return
                i, k = chunks[c]
                width = sum(p[2] for p in blocks[i][2])
                pool.wait_ge(hi_ready, c + 1)
                G.tensor_tensor(w_lo[c % NH][:, :width], w_raw[c % NR][:, :width], w_hi[c % NH][:, :width].bitcast(F32),
                                ALU.subtract).then_inc(lo_ready, 1)

            def ahead(name):
                for k in range(KT):
                    lo(number[name] * KT + k + NH - 1)
            G.memset(zero[:], 0.0).then_inc(zero_done, 1)
            pool.wait_ge(const_in, 16 * 4)
            for half in range(2):
                pool.wait_ge(sq_done, 4 * (half + 1))
                rstd(small[:, 8 + 4 * half:12 + 4 * half], small[:, 4 * half:4 * half + 4], 4, D, (rstd1, 1))
            for c in range(NH - 1):
                lo(c)
            ahead("kv")
            ahead("qi") if False else None
            pool.wait_ge(kv_sq, 1)
            rstd(small[:, 32:40], small[:, 16:24], NT, KVL)
            rstd(small[:, 40:48], small[:, 24:32], NT, DI, (kv_rstd, 1))
            ahead("qi")
            pool.wait_ge(k_sq, 1)
            rstd(small[:, 56:64], small[:, 48:56], NT, DH, (k_rstd, 1))

            def out_gate(p):
                pass

            def out_head(h):
                pass

            def out_q(b):
                for t in range(NT):
                    n = b * NT + t
                    bk_, cnt, _ = bk.at[(f"q{b}", t)]
                    pool.wait_ge(free[bk_], cnt)
                    r = small[:, 72 + 4 * (n % 2):76 + 4 * (n % 2)]
                    rstd(r, small[:, 64 + 4 * (n % 2):68 + 4 * (n % 2)], 4, DH)
                    seq(G.tensor_tensor(r, r, cst[:, K_SI + 4 * b:K_SI + 4 * b + 4], ALU.mult))
                    q3 = qst[n % 2][:].rearrange("p (h d) -> p h d", d=DH)
                    seq(G.tensor_tensor(q3, q3, r.unsqueeze(2).to_broadcast([P, 4, DH]), ALU.mult))
                    pool.dma_start(q_dram[t * P:(t + 1) * P, b * BANK:(b + 1) * BANK], qst[n % 2][:]).then_inc(q_stored[n % 2], 16)

            def out_phase1(h):
                for half in range(2):
                    b, cnt, _ = bk.at[("sc", h, half)]
                    pool.wait_ge(free[b], cnt)
                G.tensor_tensor(sT[:], sT[:], cst[:, K_RM + h * P:K_RM + (h + 1) * P].unsqueeze(1).to_broadcast([P, NT, P]),
                                ALU.mult).then_inc(sT_done, 1)
                for i in range(4):
                    b, cnt, _ = bk.at[("kvs", h, i)]
                    pool.wait_ge(free[b], cnt)
                tmp = small[:, 280:280 + 0]
                for c in range(1, NT - 1):
                    seq(G.tensor_scalar(stmp[:], state[:, c - 1, :], GC[h], 0.0, ALU.mult, ALU.add))
                    inst = G.tensor_tensor(state[:, c, :], state[:, c, :], stmp[:], ALU.add)
                    if c == NT - 2:
                        inst.then_inc(state_done, 1)
                        pool.wait_ge(state_done, h + 1)
                    else:
                        seq(inst)

            def out_phase2(h):
                for i in range(4):
                    b, cnt, _ = bk.at[("ro", h, i)]
                    pool.wait_ge(free[b], cnt)
                G.tensor_scalar(small[:, 104:112], small[:, 96:104], -1.0 / DV, 0.0, ALU.mult, ALU.add).then_inc(o_mu, 1)
                pool.wait_ge(o_var, h + 1)
                rstd(small[:, 120:128], small[:, 112:120], NT, DV)
                for c in range(NT):
                    inst = G.tensor_scalar(ro[:, c, :], ro[:, c, :], small[:, 104 + c:105 + c], small[:, 120 + c:121 + c], ALU.add, ALU.mult)
                seq(inst)
                G.tensor_tensor(ro[:], ro[:], gate[:, :, h % 2 * DV:(h % 2 + 1) * DV], ALU.mult).then_inc(o_done, 1)

            def out_block(name):
                ahead(name)
                kind, i = name[:-1], int(name[-1])
                {"gate": out_gate, "head": out_head, "q": out_q}[kind](i)
            for what, m in ret_order:
                {"block": out_block, "phase1": out_phase1, "phase2": out_phase2, "turn": lambda h: None}[what](m)
            for i in range(2):
                pool.wait_ge(q_stored[i], 16 * NT)
            if stop < 3:
                return
            for b in blocks[10:]:
                ahead(b[0])
            if stop < 4:
                return
            for t in range(NT):
                pool.wait_ge(h_sq, t + 1)
                rstd(small[:, 288 + t:289 + t], small[:, 280 + t:281 + t], 1, D, (h_rstd, 1))
            def store_y(i):
                pool.wait_ge(ey_read, i + 1)
                pool.dma_start(y_dram[i * P:(i + 1) * P, :], e_y[i % 2][:]).then_inc(ey_out[i % 2], 16)
            pool.wait_ge(zero_in, 16 * NTILE)
            pool.wait_ge(slot_done, 1)
            for t in range(NT):
                for j in range(2):
                    G.indirect_dma_start(out=xs_dram, out_offset=bass.IndirectOffsetOnAxis(ap=slot[:, j, t:t + 1], axis=0),
                                         in_=xres[:, t, :], in_offset=None).then_inc(scattered, 16)
            for i in range(NTILE + 1):
                if i < NTILE:
                    pool.wait_ge(ehi_done[1], i + 1)
                    G.tensor_tensor(e_lo[i % 2][:, 2048:4096], e_raw[i % 2][:, 2048:4096], e_hi[i % 2][:, 2048:4096].bitcast(F32),
                                    ALU.subtract).then_inc(elo_done[1], 1)
                if i >= 2:
                    store_y(i - 2)
            store_y(NTILE - 1)
            for i in range(2):
                pool.wait_ge(ey_out[i], 16 * ((NTILE + 1 - i) // 2))
            for t in range(NT):
                if t >= 2:
                    pool.wait_ge(t_sum, t - 1)
                for j in range(2):
                    G.indirect_dma_start(out=t_y[t % 2][j][:], out_offset=None, in_=y_dram,
                                         in_offset=bass.IndirectOffsetOnAxis(ap=slot[:, j, t:t + 1], axis=0)).then_inc(ty_in[t % 2], 16)


def kernel(**inputs):
    import concourse.bacc as bacc
    from concourse.bass_utils import run_bass_kernel_spmd as run

    nc = bacc.Bacc("TRN2", target_bir_lowering=False, num_devices=1)
    arrays, w = {}, {}
    shapes = {
        "x": ("x", (S, D)), "w_in": ("w_in", (D, C_GR + D)),
        "w_kv_up": ("w_kv_up", (KVL, 2 * DH)), "w_att": ("w_att_branch", (D, D)), "w_ret": ("w_ret_branch", (D, D)), "w_out": ("w_out", (D, D)),
        "norm2_g": ("norm2_g", (D,)),
        "w_gate": ("w_exp_gate", (NE * D, FF)), "w_up": ("w_exp_up", (NE * D, FF)), "w_down": ("w_exp_down", (NE * FF, D)),
    }
    for name, (src, shape) in shapes.items():
        arrays[f"in_{name}"] = np.ascontiguousarray(inputs[src]).reshape(shape)
    arrays["in_w_rt"] = np.concatenate([np.asarray(inputs["w_group_router"]).reshape(D, NG),
                                        np.asarray(inputs["w_expert_router"]).reshape(D, NE)], axis=1)
    arrays["in_b_rt"] = np.concatenate([np.asarray(inputs["b_group_router"]).reshape(NG),
                                        np.asarray(inputs["b_expert_router"]).reshape(NE)])
    arrays["in_cst"] = constants()
    g = {n: np.asarray(inputs[n], np.float32).reshape(-1) for n in inputs if n.endswith("_g")}
    arrays["in_gains"] = np.ascontiguousarray(np.concatenate([
        g["norm1_g"].reshape(KT, P), g["kv_norm_g"].reshape(2, P), g["k_norm_g"].reshape(1, P),
        np.tile(g["idx_k_norm_g"], 2).reshape(1, P), g["ret_norm_g"].reshape(KT, P), g["q_norm_g"].reshape(1, P)]).T)
    for name, a in arrays.items():
        w[name[3:]] = nc.dram_tensor(name, a.shape, F32, kind="ExternalInput").ap()
    out = nc.dram_tensor("out", (S, D), F32, kind="ExternalOutput").ap()
    scratch = {n: nc.dram_tensor(f"{n}_dram", (S, D), F32, kind=SCRATCH).ap() for n in ("q", "att", "ret", "h")}
    scratch |= {n: nc.dram_tensor(f"{n}_dram", (NTILE * P, D), F32, kind=SCRATCH).ap() for n in ("xs", "y")}
    program(nc, w, scratch, out, STOP)
    r = run(nc, [arrays], core_ids=[0])
    return r.results[0]["out"].reshape(1, S, D)


SCRATCH = "Internal"
STOP = 4
```

```python
from contextlib import ExitStack

import numpy as np
import concourse.bass as bass
from concourse import mybir

ALU = mybir.AluOpType
ACT = mybir.ActivationFunctionType
F32 = mybir.dt.float32
F32R = mybir.dt.float32r
I32 = mybir.dt.int32
U32 = mybir.dt.uint32
X = mybir.AxisListType.X

P = 128
S = 1024
D = 1024
NT = S // P
KT = D // P
HA, DH = 8, 128
KVL = 256
HI, DI = 8, 64
TOPK = 256
HR, DK, DV = 4, 128, 256
NG, EPG, NE, FF = 4, 4, 16, 256
EPS = 1e-6
BIG = 1e30
TAKEN = -3e38
BANK = 512

C_Q = 0
C_KV = C_Q + HA * DH
C_QI = C_KV + KVL
C_KI = C_QI + HI * DI
C_RQ = C_KI + DI + HI
C_RK = C_RQ + HR * DK
C_RV = C_RK + HR * DK
C_RG = C_RV + HR * DV
C_GA = C_RG + HR * DV
C_GR = C_GA + D
KVW = KVL + DI + HI

K_ID = 0
K_REL = K_ID + P
K_CAUS = K_REL + S
K_RM = K_CAUS + P
K_QD = K_RM + HR * P
K_KD = K_QD + HR
K_TRI = K_KD + HR
K_THR = K_TRI + P
K_EXC = K_THR + NE * NT
K_P16 = K_EXC + NE * NE
K_P4 = K_P16 + NE
K_TI = K_P4 + NG
NTILE = S * 2 // P + NE - 1
K_SI = K_TI + 32
K_NH = K_SI + HA
K_TOK = K_NH + 1
K_IO = K_TOK + 2 * NT
K_END = K_IO + P
NGAIN = 21

GAMMA = [1.0 - 2.0 ** (-5.0 - h) for h in range(HR)]
GC = [g ** P for g in GAMMA]


def constants():
    c = np.zeros((P, K_END), np.float64)
    p = np.arange(P)[:, None]
    i = np.arange(P)[None, :]
    c[:, K_ID:K_ID + P] = p == i
    c[:, K_REL:K_REL + S] = np.arange(S)[None, :] - p
    c[:, K_CAUS:K_CAUS + P] = np.where(i <= p, 0.0, -BIG)
    for h, g in enumerate(GAMMA):
        c[:, K_RM + h * P:K_RM + (h + 1) * P] = np.where(p <= i, g ** -(p + 1.0), 0.0) * DK ** -0.5
        c[:, K_QD + h] = g ** (np.arange(P) + 1.0)
        c[:, K_KD + h] = g ** (P - 1.0 - np.arange(P)) * DK ** -0.5
    c[:, K_TRI:K_TRI + P] = p < i
    c[:, K_THR:K_THR + NE * NT] = np.tile(np.arange(NT) * float(P), NE)[None, :]
    e = np.arange(NE)
    c[:, K_EXC:K_EXC + NE * NE] = (e[None, :] < e[:, None]).astype(np.float64).reshape(1, -1)
    c[:, K_P16:K_P16 + NE] = NE - e
    c[:, K_P4:K_P4 + NG] = NG - np.arange(NG)
    c[:, K_TI:K_TI + 32] = np.arange(32)
    c[:, K_SI:K_SI + HA] = 2.0 ** (np.arange(HA) + 1.0)
    c[:, K_NH] = -0.5
    c[:, K_TOK:K_TOK + 2 * NT] = np.tile(np.arange(NT) * float(P), 2)[None, :] + p
    c[:, K_IO:K_IO + P] = i
    return c.astype(np.float32)


class Banks:

    def __init__(self, full, free):
        self.full, self.free = full, free
        self.count = [0] * 8
        self.released = [None] * 8
        self.at = {}

    def use(self, name, bank, n=1):
        before = sorted({self.released[b] for b in range(bank, bank + n)} - {None})
        self.count[bank] += 1
        for b in range(bank, bank + n):
            self.released[b] = (bank, self.count[bank])
        self.at[name] = (bank, self.count[bank], before)

    def col(self, name):
        return self.at[name][0] * BANK

    def wait_free(self, eng, name):
        for b, n in self.at[name][2]:
            eng.wait_ge(self.free[b], n)

    def wait_full(self, eng, name):
        eng.wait_ge(self.full[self.at[name][0]], self.at[name][1])

    def wait_read(self, eng, name):
        eng.wait_ge(self.free[self.at[name][0]], self.at[name][1])

    def filled(self, inst, name):
        inst.then_inc(self.full[self.at[name][0]], 1)

    def read(self, inst, name):
        inst.then_inc(self.free[self.at[name][0]], 1)


class Seq:

    def __init__(self, eng, sem):
        self.eng, self.sem, self.n = eng, sem, 0

    def mark(self, inst):
        self.n += 1
        inst.then_inc(self.sem, 1)

    def wait(self):
        self.eng.wait_ge(self.sem, self.n)

    def __call__(self, inst):
        self.mark(inst)
        self.wait()


def program(nc, w, scratch, out, stop=99):
    ctx = ExitStack()
    with ctx:
        def sem(name):
            return ctx.enter_context(nc.semaphore(name))

        base = (nc.sbuf_base + 63) // 64 * 64
        place = [base]

        def sb(name, shape, dt=F32, at=None):
            n = 4 * int(np.prod(shape[1:]))
            off = place[0] if at is None else at
            if at is None:
                place[0] += (n + 31) // 32 * 32
            assert off + n <= nc.sbuf_usable_end, (name, off + n, nc.sbuf_usable_end)
            return nc.alloc_sbuf_tensor_at(name, shape, dt, offset=off)

        cst = sb("cst", [P, K_END])
        gains = sb("gains", [P, 64])
        small = sb("small", [P, 512])
        slot = sb("slot", [P, 2, NT], U32)
        owner = sb("owner", [P, 32], I32)
        fresh = sb("fresh", [P, 32], I32)
        token = sb("token", [P, 32], U32)
        nt_at = place[0]
        n_hi = sb("n_hi", [P, KT, S], F32R)
        n_lo = sb("n_lo", [P, KT, S], F32R)
        NR, NH = 4, 4
        wr_at = place[0]
        w_raw = [sb(f"w_raw{i}", [P, BANK]) for i in range(NR)]
        w_hi = [sb(f"w_hi{i}", [P, BANK], F32R) for i in range(NH)]
        w_lo = [sb(f"w_lo{i}", [P, BANK], F32R) for i in range(NH)]
        dist_at = place[0]
        dist = sb("dist", [P, NT * (NT + 1) // 2 * P])
        up_at = place[0]
        w_up = sb("w_up", [P, 2, 2 * DH])
        kT = sb("kT", [P, S])
        v_at = place[0]
        kvu = sb("kvu", [P, NT, 2 * DH])
        r1 = place[0]
        ps = ctx.enter_context(nc.psum_tensor("ps", [P, 8 * BANK], F32))

        def r1t(name, shape, off, dt=F32):
            return sb(name, shape, dt, at=r1 + 4 * off)

        xin = r1t("xin", [P, NT, D], 0)
        kvrows = r1t("kvrows", [P, NT, KVW], 0)
        sq = r1t("sq", [P, NT, KVW], 2624)
        cT = r1t("cT", [P, 2, S], 5248)
        kdup = r1t("kdup", [P, NT, 2, DI], 7296)
        kiT = r1t("kiT", [P, S], 8320)
        qiT = r1t("qiT", [P, 4, S], 9344)
        relu = [r1t(f"relu{i}", [P, S], 13440 + i * S) for i in range(2)]
        junk = r1t("junk", [P, 2, D], 15488)
        rqT = [r1t(f"rqT{i}", [P, S], i * S) for i in range(2)]
        rkT = r1t("rkT", [P, S], 2048)
        rv = [r1t(f"rv{i}", [P, NT, DV], 3072 + i * 2048) for i in range(2)]
        krow = r1t("krow", [P, NT, P], 7168)
        sT = r1t("sT", [P, NT, P], 8192)
        state = r1t("state", [P, NT - 1, DV], 9216)
        ro = r1t("ro", [P, NT, DV], 11008)
        gate = r1t("gate", [P, NT, 2 * DV], 13056)
        rT = r1t("rT", [P, S], 17408)
        qst = [sb("qst0", [P, BANK], at=up_at), r1t("qst1", [P, BANK], 18432)]
        junk2 = r1t("junk2", [P, DV], 18432 + BANK)
        stmp = r1t("stmp", [P, DV], 17152)
        qrow = [r1t(f"qrow{i}", [P, HA, DH], i * D) for i in range(2)]
        qT = [r1t(f"qT{i}", [P, HA, P], 2048 + i * D) for i in range(2)]
        prob = [r1t(f"prob{i}", [P, S], 4096 + i * S) for i in range(4)]
        pT = r1t("pT", [P, NT, 2, 4 * P], 8192)
        aT = [r1t(f"aT{i}", [P, HA, P], 16384 + i * D) for i in range(2)]
        sig = [r1t(f"sig{i}", [P, 4, S], i * 4096) for i in range(4)]
        a_raw = [sb(f"a_raw{i}", [P, S], at=v_at + i * 4096) for i in range(2)]
        a_hi = [sb(f"a_hi{i}", [P, S], F32R, at=dist_at + i * 4096) for i in range(2)]
        a_lo = [sb(f"a_lo{i}", [P, S], F32R, at=dist_at + 8192 + i * 4096) for i in range(2)]
        h_sb = r1t("h_sb", [P, NT, D], 0)
        xres = r1t("xres", [P, NT, D], 8192)

        g2b = r1t("g2b", [P, D], 16384)
        w_rt = r1t("w_rt", [P, KT, NG + NE], 17408)
        b_rt = r1t("b_rt", [NG + NE, 1], 17568)
        lgT = r1t("lgT", [NG + NE, S], 17760)
        lgt = r1t("lgt", [P, NT, NG + NE], 17592)
        n2T = sb("n2T", [P, NT, D], at=nt_at)
        n2sq = sb("n2sq", [P, D], at=dist_at + 4 * 2048)
        rs = sb("rs", [P, 16, NT * NE], at=dist_at)
        o_pre = sb("o_pre", [P, (NT + 1) * NE], at=dist_at + 16 * 4 * NT * NE)
        ones = sb("ones", [P, P], at=dist_at + 4 * 4240)
        hot = sb("hot", [P, 2 * NT, P], at=dist_at + 4 * (16 * NT * NE + (NT + 1) * NE))
        W3 = 3 * 4 * BANK
        e_raw = [sb(f"e_raw{i}", [P, W3], at=nt_at + i * 4 * W3) for i in range(2)]
        e_x = [sb(f"e_x{i}", [P, D], at=nt_at + 8 * W3 + i * 4 * D) for i in range(2)]
        e_y = [sb(f"e_y{i}", [P, D], at=nt_at + 8 * W3 + 8 * D + i * 4 * D) for i in range(2)]
        e_hi = [sb(f"e_hi{i}", [P, W3], F32R, at=wr_at + i * 4 * W3) for i in range(2)]
        e_lo = [sb(f"e_lo{i}", [P, W3], F32R, at=wr_at + (2 + i) * 4 * W3) for i in range(2)]
        e_at = wr_at + 16 * W3
        x_hi = [sb(f"x_hi{i}", [P, KT, P], F32R, at=e_at + i * 4 * D) for i in range(2)]
        x_lo = [sb(f"x_lo{i}", [P, KT, P], F32R, at=e_at + (2 + i) * 4 * D) for i in range(2)]
        gated = sb("gated", [P, FF], at=e_at + 16 * D)
        arow = sb("arow", [P, FF], at=e_at + 16 * D + 4 * FF)
        at_hi = sb("at_hi", [P, 2, P], F32R, at=e_at + 16 * D + 8 * FF)
        at_lo = sb("at_lo", [P, 2, P], F32R, at=e_at + 16 * D + 12 * FF)
        t_h = [sb(f"t_h{t}", [P, D], at=nt_at + 4 * W3 + t * 4 * D) if t < 6 else r1t(f"t_h{t}", [P, D], 15424 + (t - 6) * D)
               for t in range(NT)]
        t_y = [[sb(f"t_y{i}{j}", [P, D], at=nt_at + (2 * i + j) * 4 * D) for j in range(2)] for i in range(3)]

        ident = cst[:, K_ID:K_ID + P]
        G1, GKV, GK, GKI, GRT, GQ = 0, 8, 10, 11, 12, 20

        S_QR = 432

        q_dram, att_dram, ret_dram, h_dram = scratch["q"], scratch["att"], scratch["ret"], scratch["h"]
        n2_dram, y_dram = scratch["n2"], scratch["y"]

        const_in = sem("const_in")
        x_in = [sem(f"x_in{t}") for t in range(NT)]
        full = [sem(f"bank_full{b}") for b in range(8)]
        free = [sem(f"bank_free{b}") for b in range(8)]
        w_in = [sem(f"w_in{i}") for i in range(NR)]
        hi_ready, lo_ready, chunk_used = sem("hi_ready"), sem("lo_ready"), sem("chunk_used")
        s_dve, s_act, s_pool = sem("dve_seq"), sem("act_seq"), sem("pool_seq")
        sq_done, rstd1, xn_done, nhi_done = sem("sq_done"), sem("rstd1"), sem("xn_done"), sem("nhi_done")
        kv_sq, kv_rstd, ckv_n, k_sq, k_rstd, k_n = (sem(n) for n in ("kv_sq", "kv_rstd", "ckv_n", "k_sq", "k_rstd", "k_n"))
        gains_done = sem("gains_done")
        relu_done, relu_used = sem("relu_done"), sem("relu_used")
        dist_done = sem("dist_done")
        q_copied, q_squared, q_stored = sem("q_copied"), sem("q_squared"), [sem(f"q_stored{i}") for i in range(2)]
        rq_read = sem("rq_read")
        sT_raw, sT_done, kv_raw, state_done = sem("sT_raw"), sem("sT_done"), sem("kv_raw"), sem("state_done")
        krow_done = sem("krow_done")
        o_sum, o_mu, o_var, o_done, = sem("o_sum"), sem("o_mu"), sem("o_var"), sem("o_done")
        o_rstd, q_scaled = sem("o_rstd"), sem("q_scaled")
        ret_stored = sem("ret_stored")
        q_in = [sem(f"q_in{i}") for i in range(2)]
        mx_done, ex_done, p_done = sem("mx_done"), sem("ex_done"), sem("p_done")
        att_stored = [sem(f"att_stored{i}") for i in range(2)]
        sig_done = sem("sig_done")
        a_in = [sem(f"a_in{i}") for i in range(2)]
        a_hi_ready, a_lo_ready = sem("a_hi_ready"), sem("a_lo_ready")
        mixed, mix_hi = sem("mixed"), sem("mix_hi")
        mix_lo = sem("mix_lo")
        xres_in, h_done, h_stored = sem("xres_in"), sem("h_done"), sem("h_stored")

        n2_stored, hot_done, token_done = sem("n2_stored"), sem("hot_done"), sem("token_done")
        rt_in, h_sq, h_rstd, n2_done, n2T_done = sem("rt_in"), sem("h_sq"), sem("h_rstd"), sem("n2_done"), sem("n2T_done")
        lgt_done, g_shift, g_exp, e_shift, e_exp = (sem(n) for n in ("lgt_done", "g_shift", "g_exp", "e_shift", "e_exp"))
        chosen, ranked, owner_done, slot_done = sem("chosen"), sem("ranked"), sem("owner_done"), sem("slot_done")
        h_half_sq, h_half_sum = sem("h_half_sq"), sem("h_half_sum")
        ew_in = [[sem(f"ew_in{i}{j}") for j in range(3)] for i in range(2)]
        ex_in = [sem(f"ex_in{i}") for i in range(2)]
        ehi_done, elo_done = [sem(f"ehi_done{j}") for j in range(3)], [sem(f"elo_done{j}") for j in range(3)]
        exT_full, exT_hi, exT_lo = sem("exT_full"), sem("exT_hi"), sem("exT_lo")
        gu_full, gu_silu, gu_read = sem("gu_full"), sem("gu_silu"), sem("gu_read")
        eaT_full, eaT_hi, eaT_lo = sem("eaT_full"), sem("eaT_hi"), sem("eaT_lo")
        ey_full, ey_read, ey_out = sem("ey_full"), sem("ey_read"), [sem(f"ey_out{i}") for i in range(2)]
        ty_in, th_in, t_half, t_sum, t_out = ([sem(f"ty_in{i}") for i in range(3)], sem("th_in"), sem("t_half"), sem("t_sum"), sem("t_out"))

        def cols(src, c0, n, at=0):
            return (src, c0, n, at)
        wi = w["w_in"]
        blocks = [
            ("kv", "R", [cols(wi, C_KV, KVL, 0), cols(wi, C_KI, DI + HI, KVL)]),
            ("qi", "C", [cols(wi, C_QI, BANK)]),
        ]

        def gate_block(p):
            return (f"gate{p}", "R", [cols(wi, C_RG + p * BANK, BANK)])

        def head_block(h):
            return (f"head{h}", "H", [cols(wi, C_RQ + h * DK, DK, 0), cols(wi, C_RK + h * DK, DK, DK),
                                      cols(wi, C_RV + h * DV, DV, 2 * DK)])

        def q_block(b):
            return (f"q{b}", "R", [cols(wi, C_Q + b * BANK, BANK)])
        blocks += [gate_block(0), head_block(0), head_block(1), q_block(0),
                   gate_block(1), head_block(2), head_block(3), q_block(1)]
        for g, c0 in (("ga", C_GA), ("gr", C_GR)):
            blocks += [(f"{g}{b}", "C", [cols(wi, c0 + b * BANK, BANK)]) for b in range(2)]
        for g, src in (("ba", w["w_att"]), ("br", w["w_ret"])):
            blocks += [(f"{g}{b}", "A", [cols(src, b * BANK, BANK)]) for b in range(2)]
        blocks += [(f"wo{b}", "M", [cols(w["w_out"], b * BANK, BANK)]) for b in range(2)]
        number = {name: i for i, (name, _, _) in enumerate(blocks)}
        chunks = [(i, k) for i in range(len(blocks)) for k in range(KT)]
        landed, n_in = [], [0] * NR
        for c, (i, k) in enumerate(chunks):
            n_in[c % NR] += 16 * len(blocks[i][2])
            landed.append(n_in[c % NR])
        act_chunks = [(name, k) for name in ("ba0", "ba1", "br0", "br1") for k in range(KT)]

        bk = Banks(full, free)

        def use_block(name):
            for b in range(8):
                bk.use((name, b), b)
        for half in range(2):
            for k in range(KT):
                bk.use(("xT", half, k), k)
        use_block("kv")
        use_block("qi")
        for j in range(2):
            for half in range(2):
                bk.use(("cT", j, half), 2 * j + half)
        for half in range(2):
            bk.use(("kiT", half), 4 + half)
        for i in range(4):
            bk.use(("kvu", i), i)
        for half in range(2):
            bk.use(("kT", half), 6 + half)
        for t in range(2, NT):
            for h in range(HI):
                bk.use(("idx", t, h), 2 * (h % 4), 2)

        def use_phase1(h):
            for half in range(2):
                bk.use(("krow", h, half), half)
            for half in range(2):
                bk.use(("sc", h, half), 2 + half)
            for i in range(4):
                bk.use(("kvs", h, i), 4 + i)

        def use_phase2(h):
            for i in range(4):
                bk.use(("ro", h, i), i)

        def use_turn(h):
            for j in range(2):
                for half in range(2):
                    bk.use(("rT", h, j, half), 4 + 2 * j + half)
        ret_order = [("block", "gate0"), ("block", "head0"), ("phase1", 0), ("block", "head1"), ("phase2", 0),
                     ("phase1", 1), ("block", "q0"), ("turn", 0), ("phase2", 1), ("block", "gate1"), ("turn", 1),
                     ("block", "head2"), ("phase1", 2), ("block", "head3"), ("phase2", 2), ("phase1", 3),
                     ("block", "q1"), ("turn", 2), ("phase2", 3)]
        for what, n in ret_order:
            {"block": use_block, "phase1": use_phase1, "phase2": use_phase2, "turn": use_turn}[what](n)
        STEPS = NT * HA
        TURN_AT = HA

        def q_turned_at(m):
            return 0 if m == 0 else m // HA + 1 if m % HA == 6 and m // HA + 1 < NT else None
        for m in range(STEPS + 2):
            if q_turned_at(m) is not None:
                for g in range(2):
                    bk.use(("qT", q_turned_at(m), g), 6 + g)
            if m == TURN_AT:
                use_turn(HR - 1)
            if m < STEPS:
                bk.use(("lg", m), 2 * (m % 2), 2)
            if m >= 2:
                t, h = divmod(m - 2, HA)
                for i in range(t // 4 + 1):
                    bk.use(("pT", m - 2, i), 4 + i)
                if h % 4 == 3:
                    bk.use(("pv", t, h // 4), 6 + h // 4)
        for name in [b[0] for b in blocks[10:]]:
            use_block(name)
        for t in range(NT):
            bk.use(("n2T", t), 2 * (t % 2), 2)
            if t % 4 == 3:
                bk.use(("rt", t // 4), 4 + t // 4)
        bk.use(("lgt",), 6)
        bk.use(("rank",), 6)
        bk.use(("token",), 7)
        B_XT, B_GU, B_AT, B_Y = 0, 2 * BANK, 3 * BANK, 4 * BANK

        def bank(name, n=BANK):
            c = bk.col(name)
            return ps[:, c:c + n]

        def used(c):
            i, k = chunks[c]
            if k == KT - 1:
                b, n, _ = bk.at[(blocks[i][0], 7)]
                return full[b], n
            return chunk_used, i * (KT - 1) + k + 1

        def tile_at(i):
            return i // 2 + i % 2 * ((NTILE + 1) // 2)

        def tile_off(t):
            return t * (t + 1) // 2 * P

        block = ctx.enter_context(nc.Block())

        @block.sync
        def _(sp):
            def load_chunk(c):
                i, k = chunks[c]
                if c >= NR:
                    sp.wait_ge(lo_ready, c - NR + 1)
                for src, c0, n, at in blocks[i][2]:
                    sp.dma_start(w_raw[c % NR][:, at:at + n],
                                 src[k * P:(k + 1) * P, c0:c0 + n]).then_inc(w_in[c % NR], 16)

            for t in range(NT):
                sp.dma_start(xin[:, t, :], w["x"][t * P:(t + 1) * P, :]).then_inc(x_in[t], 16)
                if t == 0:
                    sp.dma_start(cst[:], w["cst"]).then_inc(const_in, 16)
                    sp.dma_start(gains[:, 0:NGAIN], w["gains"]).then_inc(const_in, 16)
            for j in range(2):
                sp.dma_start(w_up[:, j, :], w["w_kv_up"][j * P:(j + 1) * P, :]).then_inc(const_in, 16)
            first = number["ga0"] * KT + NR - 1
            for c in range(min(first, len(chunks))):
                load_chunk(c)
            if stop < 2:
                return

            def load_q(t):
                if t >= 2:
                    bk.wait_full(sp, ("qT", t - 2, 1))
                if t == 0:
                    for i in range(2):
                        sp.wait_ge(q_stored[i], 16 * NT)
                    bk.wait_full(sp, ("ro", HR - 1, 3))
                sp.dma_start(qrow[t % 2][:].rearrange("p h d -> p (h d)"),
                             q_dram[t * P:(t + 1) * P, :]).then_inc(q_in[t % 2], 16)
            load_q(0)
            load_q(1)
            for t in range(NT):
                for g in range(2):
                    bk.wait_read(sp, ("pv", t, g))
                sp.dma_start(att_dram.rearrange("(h p) s -> p h s", p=P)[:, :, t * P:(t + 1) * P],
                             aT[t % 2][:]).then_inc(att_stored[t % 2], 16)
                if t + 2 < NT:
                    load_q(t + 2)
            if stop < 3:
                return
            sp.wait_ge(att_stored[0], 16 * NT // 2)
            sp.wait_ge(att_stored[1], 16 * NT // 2)
            for c in range(first, number["ba0"] * KT):
                load_chunk(c)
            sp.wait_ge(ret_stored, 16 * (2 * HR + 1))
            for n, (name, k) in enumerate(act_chunks):
                load_chunk(number["ba0"] * KT + n)
                if n >= 2:
                    sp.wait_ge(a_lo_ready, n - 1)
                src = att_dram if name[:2] == "ba" else ret_dram
                sp.dma_start(a_raw[n % 2][:], src[k * P:(k + 1) * P, :]).then_inc(a_in[n % 2], 16)
            for c in range(number["wo0"] * KT, number["wo0"] * KT + NH - 1):
                load_chunk(c)
            sp.wait_ge(mix_lo, 16)
            sp.dma_start(xres[:], w["x"].rearrange("(t p) d -> p t d", p=P)).then_inc(xres_in, 16)
            for c in range(number["wo0"] * KT + NH - 1, len(chunks)):
                load_chunk(c)
            sp.dma_start(g2b[:], w["norm2_g"].partition_broadcast(P)).then_inc(rt_in, 16)
            sp.dma_start(w_rt[:], w["w_rt"].rearrange("(k p) n -> p k n", p=P)).then_inc(rt_in, 16)
            sp.dma_start(b_rt[:], w["b_rt"].unsqueeze(1)).then_inc(rt_in, 16)
            for t in range(NT):
                sp.wait_ge(h_done, NT + t + 1)
                sp.dma_start(h_dram[t * P:(t + 1) * P, :], h_sb[:, t, :]).then_inc(h_stored, 16)
                sp.wait_ge(n2_done, t + 1)
                sp.dma_start(n2_dram[t * P:(t + 1) * P, :], xres[:, t, :]).then_inc(n2_stored, 16)
            if stop < 4:
                sp.wait_ge(h_stored, 16 * NT)
                return
            sp.wait_ge(owner_done, 1)

            def load_expert(i):
                n = tile_at(i)
                e = sp.value_load(owner[0:1, n:n + 1], min_val=0, max_val=NE - 1)
                b = i % 2
                new = {"cond": sp.value_load(fresh[0:1, n:n + 1], min_val=0, max_val=1)} if i >= 2 else {}
                for j in range(2):
                    if i >= 2:
                        sp.wait_ge(elo_done[j], i - 1)
                    for at, src in ((0, w["w_gate"]), (FF, w["w_up"])):
                        rows = src[bass.ds(e * D, D), :].rearrange("(p k) f -> p (k f)", p=P)[:, j * 1024:(j + 1) * 1024]
                        sp.dma_start(e_raw[b][:, j * 2048 + at * 4:j * 2048 + at * 4 + 1024], rows, **new).then_inc(ew_in[b][j], 16)
                if i >= 2:
                    sp.wait_ge(elo_done[2], i - 1)
                rows = w["w_down"][bass.ds(e * FF, FF), :].rearrange("(p k) n -> p (k n)", p=P)
                sp.dma_start(e_raw[b][:, 4096:], rows, **new).then_inc(ew_in[b][2], 16)
            for i in range(NTILE):
                load_expert(i)

            sp.wait_ge(h_stored, 16 * NT)
            for j in range(3):
                sp.wait_ge(elo_done[j], NTILE - 1)
            for t in range(NT):
                sp.dma_start(t_h[t][:], h_dram[t * P:(t + 1) * P, :]).then_inc(th_in, 16)
            for t in range(NT):
                sp.wait_ge(t_sum, t + 1)
                sp.dma_start(out[t * P:(t + 1) * P, :], t_h[t][:]).then_inc(t_out, 16)
            sp.wait_ge(t_out, 16 * NT)

        @block.tensor
        def _(pe):
            mm, tr = nc.tensor.matmul, nc.tensor.transpose

            def three(out, a, b, first, last, skip=False):
                mm(out, a[0], b[0], start=first, stop=False, skip_group_check=skip)
                mm(out, a[0], b[1], start=False, stop=False, skip_group_check=skip)
                return mm(out, a[1], b[0], start=False, stop=last, skip_group_check=skip)

            def gemm(name):
                i = number[name]
                kind = blocks[i][1]
                width = sum(p[2] for p in blocks[i][2])
                for k in range(KT):
                    c = i * KT + k
                    pe.wait_ge(lo_ready, c + 1)
                    if kind == "A":
                        n = act_chunks.index((name, k))
                        pe.wait_ge(a_lo_ready, n + 1)
                    wh, wl = w_hi[c % NH], w_lo[c % NH]
                    for b in range(8):
                        if k == 0:
                            bk.wait_free(pe, (name, b))
                        o = bank((name, b))
                        f, l = k == 0, k == KT - 1
                        if kind in ("R", "M"):
                            t = slice(b * P, (b + 1) * P)
                            last = three(o[:, :width], (n_hi[:, k, t], n_lo[:, k, t]),
                                         (wh[:, :width], wl[:, :width]), f, l)
                        elif kind in ("C", "A") or b < 4:
                            fs = slice(b // 2 * P, (b // 2 + 1) * P)
                            ts = slice(b % 2 * BANK, (b % 2 + 1) * BANK)
                            act = (a_hi[n % 2][:, ts], a_lo[n % 2][:, ts]) if kind == "A" else (n_hi[:, k, ts], n_lo[:, k, ts])
                            last = three(o, (wh[:, fs], wl[:, fs]), act, f, l)
                        else:
                            for s in range(2):
                                t = slice((2 * (b - 4) + s) * P, (2 * (b - 4) + s + 1) * P)
                                last = three(o[:, s * DV:(s + 1) * DV], (n_hi[:, k, t], n_lo[:, k, t]),
                                             (wh[:, 2 * DK:], wl[:, 2 * DK:]), f and s == 0, l, skip=True)
                        if l:
                            bk.filled(last, (name, b))
                        elif b == 7:
                            last.then_inc(chunk_used, 1)

            pe.wait_ge(const_in, 16 * 4)
            for half in range(2):
                pe.wait_ge(xn_done, 4 * (half + 1))
                for k in range(KT):
                    bk.wait_free(pe, ("xT", half, k))
                    for t in range(4):
                        last = tr(bank(("xT", half, k))[:, t * P:(t + 1) * P],
                                  xin[:, 4 * half + t, k * P:(k + 1) * P], ident)
                    bk.filled(last, ("xT", half, k))
            gemm("kv")
            gemm("qi")
            pe.wait_ge(ckv_n, 1)
            for j in range(2):
                for half in range(2):
                    bk.wait_free(pe, ("cT", j, half))
                    for t in range(4):
                        last = tr(bank(("cT", j, half))[:, t * P:(t + 1) * P],
                                  kvrows[:, 4 * half + t, j * P:(j + 1) * P], ident)
                    bk.filled(last, ("cT", j, half))
            for half in range(2):
                bk.wait_free(pe, ("kiT", half))
                for t in range(4):
                    last = tr(bank(("kiT", half))[:, t * P:(t + 1) * P],
                              kdup[:, 4 * half + t].rearrange("p a d -> p (a d)"), ident)
                bk.filled(last, ("kiT", half))
            for i in range(4):
                bk.wait_read(pe, ("cT", i // 2, i % 2))
            for i in range(4):
                bk.wait_free(pe, ("kvu", i))
                for s in range(2):
                    t = 2 * i + s
                    for j in range(2):
                        last = mm(bank(("kvu", i))[:, s * 2 * DH:(s + 1) * 2 * DH], cT[:, j, t * P:(t + 1) * P],
                                  w_up[:, j, :], start=j == 0, stop=j == 1)
                bk.filled(last, ("kvu", i))
            for half in range(2):
                pe.wait_ge(free[4 + half], bk.at[("kiT", half)][1])
            for half in range(2):
                pass
            pe.wait_ge(k_n, 1)
            for half in range(2):
                bk.wait_free(pe, ("kT", half))
                for t in range(4):
                    last = tr(bank(("kT", half))[:, t * P:(t + 1) * P], kvu[:, 4 * half + t, 0:DH], ident)
                bk.filled(last, ("kT", half))
            for t in range(2, NT):
                nk = (t + 1) * P
                for h in range(HI):
                    name = ("idx", t, h)
                    bk.wait_free(pe, name)
                    c = bk.col(name)
                    s = slice(h % 2 * DI, (h % 2 + 1) * DI)
                    for k0 in range(0, nk, BANK):
                        n = min(BANK, nk - k0)
                        last = mm(ps[:, c + k0:c + k0 + n], qiT[s, h // 2, t * P:(t + 1) * P],
                                  kiT[s, k0:k0 + n], start=True, stop=True)
                    bk.filled(last, name)

            def phase1(h):
                for half in range(2):
                    name = ("krow", h, half)
                    bk.wait_free(pe, name)
                    if half == 0:
                        for b in range(8):
                            pe.wait_ge(free[b], bk.at[(f"head{h}", b)][1])
                    for t in range(4):
                        cs = slice((4 * half + t) * P, (4 * half + t + 1) * P)
                        last = tr(bank(name)[:, t * P:(t + 1) * P], rkT[:, cs], ident)
                    bk.filled(last, name)
                for half in range(2):
                    name = ("sc", h, half)
                    bk.wait_free(pe, name)
                    for t in range(4):
                        cs = slice((4 * half + t) * P, (4 * half + t + 1) * P)
                        last = mm(bank(name)[:, t * P:(t + 1) * P], rkT[:, cs], rqT[h % 2][:, cs], start=True, stop=True)
                    bk.filled(last, name)
                for half in range(2):
                    pe.wait_ge(free[half], bk.at[("krow", h, half)][1])
                for i in range(4):
                    name = ("kvs", h, i)
                    bk.wait_free(pe, name)
                    for s in range(2):
                        c = 2 * i + s
                        if c < NT - 1:
                            last = mm(bank(name)[:, s * DV:(s + 1) * DV], krow[:, c, :], rv[h % 2][:, c, :], start=True, stop=True)
                    bk.filled(last, name)

            def phase2(h):
                pe.wait_ge(sT_done, h + 1)
                pe.wait_ge(state_done, h + 1)
                for i in range(4):
                    name = ("ro", h, i)
                    bk.wait_free(pe, name)
                    for s in range(2):
                        c = 2 * i + s
                        o = bank(name)[:, s * DV:(s + 1) * DV]
                        last = mm(o, sT[:, c, :], rv[h % 2][:, c, :], start=True, stop=c == 0)
                        if c:
                            last = mm(o, rqT[h % 2][:, c * P:(c + 1) * P], state[:, c - 1, :], start=False, stop=True)
                    bk.filled(last, name)

            def turn(h):
                pe.wait_ge(o_done, h + 1)
                for j in range(2):
                    for half in range(2):
                        name = ("rT", h, j, half)
                        bk.wait_free(pe, name)
                        for t in range(4):
                            last = tr(bank(name)[:, t * P:(t + 1) * P], ro[:, 4 * half + t, j * P:(j + 1) * P], ident)
                        bk.filled(last, name)
            for what, n in ret_order:
                {"block": gemm, "phase1": phase1, "phase2": phase2, "turn": turn}[what](n)
            if stop < 2:
                return
            for m in range(STEPS + 2):
                t = q_turned_at(m)
                if t is not None:
                    pe.wait_ge(q_scaled, t + 1)
                    for g in range(2):
                        bk.wait_free(pe, ("qT", t, g))
                        for s in range(4):
                            last = tr(bank(("qT", t, g))[:, s * P:(s + 1) * P], qrow[t % 2][:, 4 * g + s, :], ident)
                        bk.filled(last, ("qT", t, g))
                if m == TURN_AT:
                    turn(HR - 1)
                if m < STEPS:
                    t, h = divmod(m, HA)
                    nk = (t + 1) * P
                    name = ("lg", m)
                    bk.wait_free(pe, name)
                    if h == 0:
                        for g in range(2):
                            bk.wait_read(pe, ("qT", t, g))
                    c = bk.col(name)
                    for k0 in range(0, nk, BANK):
                        n = min(BANK, nk - k0)
                        last = mm(ps[:, c + k0:c + k0 + n], qT[t % 2][:, h, :], kT[:, k0:k0 + n], start=True, stop=True)
                    bk.filled(last, name)
                if m >= 2:
                    t, h = divmod(m - 2, HA)
                    g = h // 4
                    pe.wait_ge(p_done, m - 1)
                    for i in range(t // 4 + 1):
                        name = ("pT", m - 2, i)
                        bk.wait_free(pe, name)
                        for kt in range(4 * i, min(4 * i + 4, t + 1)):
                            last = tr(bank(name)[:, kt % 4 * P:(kt % 4 + 1) * P], prob[h % 4][:, kt * P:(kt + 1) * P], ident)
                        bk.filled(last, name)
                    if h % 4 == 3:
                        name = ("pv", t, g)
                        bk.wait_free(pe, name)
                        for i in range(t // 4 + 1):
                            bk.wait_read(pe, ("pT", m - 2, i))
                        for kt in range(t + 1):
                            last = mm(bank(name), kvu[:, kt, DH:2 * DH], pT[:, kt, g], start=kt == 0, stop=kt == t)
                        bk.filled(last, name)
            if stop < 3:
                return
            for name in [b[0] for b in blocks[10:]]:
                if name == "wo0":
                    pe.wait_ge(mix_lo, 16)
                gemm(name)
            if stop < 4:
                return
            pe.wait_ge(rt_in, 48)
            for t in range(NT):
                pe.wait_ge(n2_done, t + 1)
                bk.wait_free(pe, ("n2T", t))
                for k in range(KT):
                    last = tr(ps[:, bk.col(("n2T", t)) + k * P:bk.col(("n2T", t)) + (k + 1) * P], xres[:, t, k * P:(k + 1) * P], ident)
                bk.filled(last, ("n2T", t))
                if t % 4 == 3:
                    g = t // 4
                    bk.wait_free(pe, ("rt", g))
                    bk.wait_read(pe, ("n2T", t - 1))
                    bk.wait_read(pe, ("n2T", t))
                    for k in range(KT):
                        last = mm(bank(("rt", g))[0:NG + NE, :], w_rt[:, k, :], n2T[:, 4 * g:4 * g + 4, k * P:(k + 1) * P], start=k == 0, stop=k == KT - 1)
                    bk.filled(last, ("rt", g))
            bk.wait_free(pe, ("lgt",))
            for t in range(NT):
                if t % 4 == 0:
                    bk.wait_read(pe, ("rt", t // 4))
                last = tr(bank(("lgt",))[:, t * (NG + NE):(t + 1) * (NG + NE)], lgT[:, t * P:(t + 1) * P], ident[0:NG + NE, 0:NG + NE])
            bk.filled(last, ("lgt",))
            pe.wait_ge(chosen, 1)
            name = ("rank",)
            bk.wait_free(pe, name)
            mm(bank(name, (NT + 1) * NE), ones[:], o_pre[:], start=True, stop=False, skip_group_check=True)
            bk.filled(mm(bank(name, NT * NE), cst[:, K_TRI:K_TRI + P], rs[:, 7, :], start=False, stop=True, skip_group_check=True), name)
            pe.wait_ge(hot_done, 1)
            name = ("token",)
            bk.wait_free(pe, name)
            for n in range(2 * NT):
                last = mm(bank(name, 32), hot[:, n, :], rs[:, 4:8, :].rearrange("p a n -> p (a n)")[:, n * 32:(n + 1) * 32],
                          start=n == 0, stop=n == 2 * NT - 1)
            bk.filled(last, name)

            def turn_rows(i):
                pe.wait_ge(ex_in[i % 2], 16 * (i // 2 + 1))
                if i:
                    pe.wait_ge(exT_lo, i)
                for k in range(KT):
                    last = tr(ps[:, B_XT + k * P:B_XT + (k + 1) * P], e_x[i % 2][:].rearrange("s (p k) -> s k p", k=KT)[:, k, :], ident)
                last.then_inc(exT_full, 1)

            def gate_up(i):
                b = i % 2
                pe.wait_ge(exT_lo, i + 1)
                if i:
                    pe.wait_ge(gu_read, i)
                for k in range(KT):
                    if k % 4 == 0:
                        pe.wait_ge(elo_done[k // 4], i + 1)
                    wk = [e[b][:, k // 4 * 2048:(k // 4 + 1) * 2048].rearrange("p (a k f) -> p k a f", a=2, f=FF)[:, k % 4]
                          for e in (e_hi, e_lo)]
                    last = three(ps[:, B_GU:B_GU + 2 * FF].rearrange("p (a f) -> p a f", a=2),
                                 (x_hi[b][:, k, :], x_lo[b][:, k, :]), wk, k == 0, k == KT - 1)
                last.then_inc(gu_full, 1)

            def turn_act(i):
                pe.wait_ge(gu_read, i + 1)
                if i:
                    pe.wait_ge(eaT_lo, i)
                for k in range(2):
                    last = tr(ps[:, B_AT + k * P:B_AT + (k + 1) * P], arow[:].rearrange("s (p k) -> s k p", k=2)[:, k, :], ident)
                last.then_inc(eaT_full, 1)

            def down(i):
                b = i % 2
                pe.wait_ge(eaT_lo, i + 1)
                pe.wait_ge(elo_done[2], i + 1)
                if i:
                    pe.wait_ge(ey_read, i)
                for n in range(2):
                    for k in range(2):
                        ws = slice(4096 + k * D + n * BANK, 4096 + k * D + (n + 1) * BANK)
                        last = three(ps[:, B_Y + n * BANK:B_Y + (n + 1) * BANK], (at_hi[:, k, :], at_lo[:, k, :]),
                                     (e_hi[b][:, ws], e_lo[b][:, ws]), k == 0, k == 1)
                last.then_inc(ey_full, 1)
            turn_rows(0)
            for i in range(NTILE + 1):
                if i:
                    turn_act(i - 1)
                if i + 1 < NTILE:
                    turn_rows(i + 1)
                if i < NTILE:
                    gate_up(i)
                if i:
                    down(i - 1)

        @block.scalar
        def _(act):
            seq = Seq(act, s_act)
            A = nc.scalar.activation

            def hi(c):
                if c >= len(chunks):
                    return
                i, k = chunks[c]
                width = sum(p[2] for p in blocks[i][2])
                act.wait_ge(w_in[c % NR], landed[c])
                if c >= NH:
                    act.wait_ge(*used(c - NH))
                nc.scalar.copy(w_hi[c % NH][:, :width], w_raw[c % NR][:, :width]).then_inc(hi_ready, 1)

            act.wait_ge(const_in, 16 * 4)
            for t in range(NT):
                act.wait_ge(x_in[t], 16)
                if t >= 2:
                    act.wait_ge(sq_done, t - 1)
                A(junk[:, t % 2, :], xin[:, t, :], ACT.Square, accum_out=small[:, t:t + 1]).then_inc(sq_done, 1)
            for c in range(NH - 1):
                hi(c)
            for half in range(2):
                for k in range(KT):
                    name = ("xT", half, k)
                    bk.wait_full(act, name)
                    A(n_hi[:, k, half * BANK:(half + 1) * BANK], bank(name), ACT.Identity,
                      scale=gains[:, G1 + k:G1 + k + 1]).then_inc(nhi_done, 1)

            def ahead(name):
                for k in range(KT):
                    hi(number[name] * KT + k + NH - 1)
            ahead("kv")
            for t in range(NT):
                bk.wait_full(act, ("kv", t))
                if t == 0:
                    act.wait_ge(nhi_done, 16)
                bk.read(nc.scalar.copy(kvrows[:, t, :], bank(("kv", t), KVW)), ("kv", t))
            ahead("qi")
            for b in range(8):
                bk.wait_full(act, ("qi", b))
                bk.read(nc.scalar.copy(qiT[:, b // 2, b % 2 * BANK:(b % 2 + 1) * BANK], bank(("qi", b))), ("qi", b))
            act.wait_ge(gains_done, 1)
            for j in range(2):
                for half in range(2):
                    name = ("cT", j, half)
                    bk.wait_full(act, name)
                    bk.read(A(cT[:, j, half * BANK:(half + 1) * BANK], bank(name), ACT.Identity,
                              scale=gains[:, GKV + j:GKV + j + 1]), name)
            for half in range(2):
                name = ("kiT", half)
                bk.wait_full(act, name)
                bk.read(A(kiT[:, half * BANK:(half + 1) * BANK], bank(name), ACT.Identity,
                          scale=gains[:, GKI:GKI + 1]), name)
            for i in range(4):
                name = ("kvu", i)
                bk.wait_full(act, name)
                bk.read(nc.scalar.copy(kvu[:, 2 * i:2 * i + 2, :].rearrange("p t d -> p (t d)"), bank(name)), name)
            for half in range(2):
                name = ("kT", half)
                bk.wait_full(act, name)
                bk.read(A(kT[:, half * BANK:(half + 1) * BANK], bank(name), ACT.Identity,
                          scale=gains[:, GK:GK + 1]), name)
            n = 0
            for t in range(2, NT):
                nk = (t + 1) * P
                for h in range(HI):
                    name = ("idx", t, h)
                    bk.wait_full(act, name)
                    if n >= 2:
                        act.wait_ge(relu_used, n - 1)
                    c = bk.col(name)
                    bk.read(A(relu[n % 2][:, :nk], ps[:, c:c + nk], ACT.Relu), name)
                    n += 1

            def out_gate(p):
                if p:
                    act.wait_ge(o_done, 2 * p)
                for t in range(NT):
                    name = (f"gate{p}", t)
                    bk.wait_full(act, name)
                    if t == 0 and p == 0:
                        act.wait_ge(relu_used, n)
                    bk.read(A(gate[:, t, :], bank(name), ACT.Silu), name)

            def out_head(h):
                for b in range(8):
                    name = (f"head{h}", b)
                    bk.wait_full(act, name)
                    if b < 2:
                        dst = rqT[h % 2][:, b * BANK:(b + 1) * BANK]
                    elif b < 4:
                        dst = rkT[:, (b - 2) * BANK:(b - 1) * BANK]
                    else:
                        dst = rv[h % 2][:, 2 * (b - 4):2 * (b - 4) + 2, :].rearrange("p t d -> p (t d)")
                    bk.read(nc.scalar.copy(dst, bank(name)), name)

            def out_q(b):
                for t in range(NT):
                    n = b * NT + t
                    name = (f"q{b}", t)
                    bk.wait_full(act, name)
                    if n >= 2:
                        act.wait_ge(q_stored[n % 2], 16 * (n // 2))
                    nc.scalar.copy(qst[n % 2][:], bank(name)).then_inc(q_copied, 1)
                    act.wait_ge(q_copied, n + 1)
                    act.dma_start(q_dram[t * P:(t + 1) * P, b * BANK:(b + 1) * BANK], qst[n % 2][:]).then_inc(q_stored[n % 2], 16)
                    for h in range(4):
                        col = S_QR + HA * t + 4 * b + h
                        inst = A(junk2[:, h % 2 * P:(h % 2 + 1) * P], bank(name)[:, h * DH:(h + 1) * DH], ACT.Square,
                                 accum_out=small[:, col:col + 1])
                        if h == 3:
                            bk.read(inst, name)
                        else:
                            seq(inst)

            def out_phase1(h):
                for half in range(2):
                    name = ("krow", h, half)
                    bk.wait_full(act, name)
                    bk.read(A(krow[:, 4 * half:4 * half + 4, :].rearrange("p t d -> p (t d)"), bank(name), ACT.Identity,
                              scale=cst[:, K_KD + h:K_KD + h + 1]), name)
                for half in range(2):
                    name = ("sc", h, half)
                    bk.wait_full(act, name)
                    bk.read(nc.scalar.copy(sT[:, 4 * half:4 * half + 4, :].rearrange("p t d -> p (t d)"), bank(name)), name)
                for i in range(4):
                    name = ("kvs", h, i)
                    bk.wait_full(act, name)
                    m = min(2, NT - 1 - 2 * i)
                    bk.read(nc.scalar.copy(state[:, 2 * i:2 * i + m, :].rearrange("p t d -> p (t d)"), bank(name, m * DV)), name)

            def out_phase2(h):
                if h:
                    act.wait_ge(full[7], bk.at[("rT", h - 1, 1, 1)][1])
                for i in range(4):
                    name = ("ro", h, i)
                    bk.wait_full(act, name)
                    for s in range(2):
                        c = 2 * i + s
                        inst = A(ro[:, c, :], bank(name)[:, s * DV:(s + 1) * DV], ACT.Identity,
                                 scale=cst[:, K_QD + h:K_QD + h + 1], accum_out=small[:, 96 + c:97 + c])
                        bk.read(inst, name) if s else seq(inst)
                act.wait_ge(o_mu, h + 1)
                for c in range(NT):
                    seq(A(junk2[:], ro[:, c, :], ACT.Square, bias=small[:, 104 + c:105 + c],
                          accum_out=small[:, 112 + c:113 + c])) if c < NT - 1 else \
                        A(junk2[:], ro[:, c, :], ACT.Square, bias=small[:, 104 + c:105 + c],
                          accum_out=small[:, 112 + c:113 + c]).then_inc(o_var, 1)
                act.wait_ge(o_var, h + 1)

            def out_turn(h):
                for j in range(2):
                    final = h == HR - 1 and j == 1
                    dst = [q[:] for q in qst] if final else [rT[:, 0:BANK], rT[:, BANK:]]
                    if final:
                        for i in range(2):
                            act.wait_ge(q_stored[i], 16 * NT)
                    elif h or j:
                        act.wait_ge(ret_stored, 16 * (2 * h + j))
                    for half in range(2):
                        name = ("rT", h, j, half)
                        bk.wait_full(act, name)
                        bk.read(A(dst[half], bank(name), ACT.Identity,
                                  scale=gains[:, GRT + 2 * h + j:GRT + 2 * h + j + 1]), name)
                    for half in range(2):
                        bk.wait_read(act, ("rT", h, j, half))
                    rows = ret_dram[(2 * h + j) * P:(2 * h + j + 1) * P, :]
                    if final:
                        for half in range(2):
                            act.dma_start(rows[:, half * BANK:(half + 1) * BANK], dst[half]).then_inc(ret_stored, 16)
                    else:
                        act.dma_start(rows, rT[:]).then_inc(ret_stored, 16)

            def out_block(name):
                ahead(name)
                kind, i = name[:-1], int(name[-1])
                {"gate": out_gate, "head": out_head, "q": out_q}[kind](i)
            for what, m in ret_order:
                {"block": out_block, "phase1": out_phase1, "phase2": out_phase2, "turn": out_turn}[what](m)
            if stop < 2:
                act.wait_ge(ret_stored, 16 * (2 * HR + 1))
                return
            for m in range(STEPS + 1):
                t = q_turned_at(m)
                if t is not None:
                    for g in range(2):
                        name = ("qT", t, g)
                        bk.wait_full(act, name)
                        bk.read(nc.scalar.copy(qT[t % 2][:, 4 * g:4 * g + 4, :].rearrange("p h q -> p (h q)"), bank(name)), name)
                if m < STEPS:
                    t, h = divmod(m, HA)
                    nk = (t + 1) * P
                    act.wait_ge(mx_done, m + 1)
                    A(prob[h % 4][:, :nk], prob[h % 4][:, :nk], ACT.Exp, bias=small[:, 128 + h:129 + h],
                      scale=2.0 ** -(h + 1), accum_out=small[:, 144 + h:145 + h]).then_inc(ex_done, 1)
                if m == TURN_AT - 1:
                    out_turn(HR - 1)
                if m >= 1:
                    t, h = divmod(m - 1, HA)
                    g = h // 4
                    for i in range(t // 4 + 1):
                        name = ("pT", m - 1, i)
                        bk.wait_full(act, name)
                        n = min(4, t + 1 - 4 * i)
                        bk.read(nc.scalar.copy(pT[:, 4 * i:4 * i + n, g, h % 4 * P:(h % 4 + 1) * P],
                                               bank(name, n * P).rearrange("p (k q) -> p k q", q=P)), name)
                    if h % 4 == 3:
                        name = ("pv", t, g)
                        bk.wait_full(act, name)
                        if t == 0 and g == 0:
                            act.wait_ge(o_done, HR)
                        if t == 1 and g == 0:
                            act.wait_ge(ret_stored, 16 * (2 * HR + 1))
                        if t >= 2 and g == 0:
                            act.wait_ge(att_stored[t % 2], 16 * (t // 2))
                        bk.read(nc.scalar.copy(aT[t % 2][:, 4 * g:4 * g + 4, :].rearrange("p h q -> p (h q)"), bank(name)), name)
            if stop < 3:
                return
            for n, name in enumerate(("ga0", "ga1", "gr0", "gr1")):
                ahead(name)
                if n == 0:
                    for i in range(2):
                        act.wait_ge(att_stored[i], 16 * NT // 2)
                for b in range(8):
                    bk.wait_full(act, (name, b))
                    bk.read(A(sig[n][:, b // 2, b % 2 * BANK:(b % 2 + 1) * BANK], bank((name, b)), ACT.Sigmoid), (name, b))

            def a_part(n):
                if n >= len(act_chunks):
                    return
                act.wait_ge(a_in[n % 2], 16 * (n // 2 + 1))
                if n >= 2:
                    c = number["ba0"] * KT + n - 2
                    act.wait_ge(*used(c))
                nc.scalar.copy(a_hi[n % 2][:], a_raw[n % 2][:]).then_inc(a_hi_ready, 1)
            a_part(0)
            for n, (name, k) in enumerate(act_chunks):
                a_part(n + 1)
                hi(number["ba0"] * KT + n + NH - 1)
                if k == KT - 1 and name[:2] == "br":
                    bi = int(name[-1])
                    for b in range(8):
                        f, half = b // 2, b % 2
                        m = bi * 8 + b
                        act.wait_ge(mixed, m + 1)
                        nc.scalar.copy(n_hi[:, 4 * bi + f, half * BANK:(half + 1) * BANK],
                                       sig[2 + bi][:, f, half * BANK:(half + 1) * BANK]).then_inc(mix_hi, 1)
            ahead("wo0")
            ahead("wo1")
            if stop < 4:
                return
            for t in range(NT):
                act.wait_ge(h_done, t + 1)
                A(n2sq[:, 0:BANK], h_sb[:, t, 0:BANK], ACT.Square, accum_out=small[:, 280 + t:281 + t]).then_inc(h_half_sq, 1)
                act.wait_ge(h_half_sq, t + 1)
            for t in range(NT):
                act.wait_ge(h_done, NT + t + 1)
                A(n2sq[:, BANK:], h_sb[:, t, BANK:], ACT.Square, accum_out=small[:, 296 + t:297 + t]).then_inc(h_sq, 1)
                act.wait_ge(h_sq, t + 1)
                if t >= 1:
                    name = ("n2T", t - 1)
                    bk.wait_full(act, name)
                    bk.read(nc.scalar.copy(n2T[:, t - 1, :], ps[:, bk.col(name):bk.col(name) + D]), name)
            name = ("n2T", NT - 1)
            bk.wait_full(act, name)
            bk.read(nc.scalar.copy(n2T[:, NT - 1, :], ps[:, bk.col(name):bk.col(name) + D]), name)
            for g in range(2):
                name = ("rt", g)
                bk.wait_full(act, name)
                bk.read(A(lgT[:, g * BANK:(g + 1) * BANK], bank(name)[0:NG + NE, :], ACT.Identity, bias=b_rt[:]), name)
            act.wait_ge(g_shift, 1)
            A(rs[:, 1, 0:NT * NG], rs[:, 1, 0:NT * NG], ACT.Exp).then_inc(g_exp, 1)
            act.wait_ge(e_shift, 1)
            A(rs[:, 8, 0:NT], rs[:, 8, 0:NT], ACT.Exp).then_inc(e_exp, 1)

            def w_part(i, j):
                b = i % 2
                act.wait_ge(ew_in[b][j], (32, 32, 16)[j] * (i // 2 + 1))
                if i >= 2:
                    act.wait_ge(ey_full if j == 2 else gu_full, i - 1)
                ws = slice(j * 2048, (j + 1) * 2048)
                nc.scalar.copy(e_hi[b][:, ws], e_raw[b][:, ws]).then_inc(ehi_done[j], 1)

            def x_part(i):
                act.wait_ge(exT_full, i + 1)
                if i >= 2:
                    act.wait_ge(gu_full, i - 1)
                nc.scalar.copy(x_hi[i % 2][:].rearrange("p k q -> p (k q)"), ps[:, B_XT:B_XT + D]).then_inc(exT_hi, 1)
            for j in range(3):
                w_part(0, j)
            act.wait_ge(n2_stored, 16 * NT)
            act.wait_ge(h_stored, 16 * NT)
            x_part(0)
            for i in range(NTILE):
                if i:
                    act.wait_ge(eaT_full, i)
                    if i >= 2:
                        act.wait_ge(ey_full, i - 1)
                    nc.scalar.copy(at_hi[:].rearrange("p k q -> p (k q)"), ps[:, B_AT:B_AT + FF]).then_inc(eaT_hi, 1)
                if i + 1 < NTILE:
                    x_part(i + 1)
                    w_part(i + 1, 0)
                    w_part(i + 1, 1)
                act.wait_ge(gu_full, i + 1)
                if i:
                    act.wait_ge(gu_read, i)
                A(gated[:], ps[:, B_GU:B_GU + FF], ACT.Silu).then_inc(gu_silu, 1)
                if i + 1 < NTILE:
                    w_part(i + 1, 2)
            act.wait_ge(eaT_full, NTILE)
            act.wait_ge(ey_full, NTILE - 1)
            nc.scalar.copy(at_hi[:].rearrange("p k q -> p (k q)"), ps[:, B_AT:B_AT + FF]).then_inc(eaT_hi, 1)

        @block.vector
        def _(dve):
            seq = Seq(dve, s_dve)
            V = nc.vector
            dve.wait_ge(const_in, 16 * 4)
            seq(V.scalar_tensor_tensor(gains[:, GK:GK + 1], gains[:, GQ:GQ + 1], DH ** -0.5, gains[:, GK:GK + 1], ALU.mult, ALU.mult))
            V.tensor_scalar(gains[:, GKI:GKI + 1], gains[:, GKI:GKI + 1], DI ** -0.5, None, ALU.mult).then_inc(gains_done, 1)
            for half in range(2):
                dve.wait_ge(rstd1, half + 1)
                for t in range(4 * half, 4 * half + 4):
                    V.tensor_scalar(xin[:, t, :], xin[:, t, :], small[:, 8 + t:9 + t], None, ALU.mult).then_inc(xn_done, 1)
            for half in range(2):
                for k in range(KT):
                    name = ("xT", half, k)
                    dve.wait_ge(nhi_done, half * KT + k + 1)
                    hs = slice(half * BANK, (half + 1) * BANK)
                    bk.read(V.scalar_tensor_tensor(n_lo[:, k, hs], bank(name), gains[:, G1 + k:G1 + k + 1],
                                                   n_hi[:, k, hs].bitcast(F32), ALU.mult, ALU.subtract), name)
            for t in range(NT):
                dve.wait_ge(free[t], bk.at[("kv", t)][1])
            seq(V.tensor_tensor(sq[:], kvrows[:], kvrows[:], ALU.mult))
            seq(V.tensor_reduce(small[:, 16:24], sq[:, :, 0:KVL], X, ALU.add))
            V.tensor_reduce(small[:, 24:32], sq[:, :, KVL:KVL + DI], X, ALU.add).then_inc(kv_sq, 1)
            dve.wait_ge(kv_rstd, 1)
            seq(V.tensor_tensor(kdup[:, :, 0, :], kvrows[:, :, KVL:KVL + DI], small[:, 40:48].unsqueeze(2).to_broadcast([P, NT, DI]), ALU.mult))
            seq(V.tensor_copy(kdup[:, :, 1, :], kdup[:, :, 0, :]))
            seq(V.tensor_scalar(small[:, 192:256].rearrange("p (t h) -> p t h", h=HI), kvrows[:, :, KVL + DI:KVW], HI ** -0.5, None, ALU.mult))
            V.tensor_tensor(kvrows[:, :, 0:KVL], kvrows[:, :, 0:KVL], small[:, 32:40].unsqueeze(2).to_broadcast([P, NT, KVL]), ALU.mult).then_inc(ckv_n, 1)
            for i in range(4):
                dve.wait_ge(free[i], bk.at[("kvu", i)][1])
            ksq = sq[:].rearrange("p t d -> p (t d)")[:, 0:S].rearrange("p (t d) -> p t d", d=DH)
            seq(V.tensor_tensor(ksq, kvu[:, :, 0:DH], kvu[:, :, 0:DH], ALU.mult))
            V.tensor_reduce(small[:, 48:56], ksq, X, ALU.add).then_inc(k_sq, 1)
            dve.wait_ge(k_rstd, 1)
            V.tensor_tensor(kvu[:, :, 0:DH], kvu[:, :, 0:DH], small[:, 56:64].unsqueeze(2).to_broadcast([P, NT, DH]), ALU.mult).then_inc(k_n, 1)
            n = 0
            for t in range(2, NT):
                nk = (t + 1) * P
                sc = dist[:, tile_off(t):tile_off(t) + nk]
                for h in range(HI):
                    b, cnt, _ = bk.at[("idx", t, h)]
                    dve.wait_ge(free[b], cnt)
                    wv = small[:, 192 + t * HI + h:193 + t * HI + h]
                    if n:
                        dve.wait_ge(relu_used, n)
                    if h == 0:
                        V.tensor_scalar(sc, relu[n % 2][:, :nk], wv, None, ALU.mult).then_inc(relu_used, 1)
                    else:
                        V.scalar_tensor_tensor(sc, relu[n % 2][:, :nk], wv, sc, ALU.mult, ALU.add).then_inc(relu_used, 1)
                    n += 1
                dve.wait_ge(relu_used, n)
                seq(V.tensor_tensor(sc[:, t * P:], sc[:, t * P:], cst[:, K_CAUS:K_CAUS + P], ALU.add))
            for t in range(NT):
                nk = (t + 1) * P
                sc = dist[:, tile_off(t):tile_off(t) + nk]
                if nk <= TOPK:
                    seq(V.tensor_scalar(sc, cst[:, K_REL:K_REL + nk], float(-t * P), None, ALU.add))
                    V.tensor_tensor(sc[:, t * P:], sc[:, t * P:], cst[:, K_CAUS:K_CAUS + P], ALU.add).then_inc(dist_done, 1)
                    dve.wait_ge(dist_done, t + 1)
                    continue
                for r in range(TOPK // 8):
                    m8 = small[:, 256 + r % 2 * 8:264 + r % 2 * 8]
                    seq(V.max(m8, sc))
                    seq(V.match_replace(sc, m8, sc, TAKEN))
                seq(V.tensor_scalar(sc, sc, TAKEN, -BIG, ALU.not_equal, ALU.mult))
                V.scalar_tensor_tensor(sc, cst[:, K_REL:K_REL + nk], float(-t * P), sc, ALU.add, ALU.add).then_inc(dist_done, 1)
                dve.wait_ge(dist_done, t + 1)

            def out_phase1(h):
                for half in range(2):
                    bk.wait_read(dve, ("sc", h, half))
                V.tensor_tensor(sT[:], sT[:], cst[:, K_RM + h * P:K_RM + (h + 1) * P].unsqueeze(1).to_broadcast([P, NT, P]),
                                ALU.mult).then_inc(sT_done, 1)
                for i in range(4):
                    bk.wait_read(dve, ("kvs", h, i))
                for c in range(1, NT - 1):
                    inst = V.scalar_tensor_tensor(state[:, c, :], state[:, c - 1, :], GC[h], state[:, c, :], ALU.mult, ALU.add)
                    if c == NT - 2:
                        inst.then_inc(state_done, 1)
                    else:
                        seq(inst)

            def out_phase2(h):
                dve.wait_ge(o_rstd, h - 1)
                for c in range(NT):
                    inst = V.tensor_scalar(ro[:, c, :], ro[:, c, :], small[:, 104 + c:105 + c], small[:, 120 + c:121 + c], ALU.add, ALU.mult)
                seq(inst)
                V.tensor_tensor(ro[:], ro[:], gate[:, :, h % 2 * DV:(h % 2 + 1) * DV], ALU.mult).then_inc(o_done, 1)
            for what, h in ret_order:
                if (what == "phase1" and h == HR - 1) or (what == "phase2" and h >= 2):
                    {"phase1": out_phase1, "phase2": out_phase2}[what](h)
            if stop < 2:
                return
            for m in range(STEPS + 1):
                if m < STEPS:
                    t, h = divmod(m, HA)
                    nk = (t + 1) * P
                    name = ("lg", m)
                    bk.wait_full(dve, name)
                    c = bk.col(name)
                    if m >= 4:
                        for i in range((m - 4) // HA // 4 + 1):
                            bk.wait_full(dve, ("pT", m - 4, i))
                    bk.read(V.tensor_tensor_reduce(out=prob[h % 4][:, :nk], in0=ps[:, c:c + nk], in1=dist[:, tile_off(t):tile_off(t) + nk],
                                                   scale=1.0, scalar=-3e38, op0=ALU.add, op1=ALU.max, accum_out=small[:, 160 + h:161 + h]), name)
                    bk.wait_read(dve, name)
                    V.tensor_scalar(small[:, 128 + h:129 + h], small[:, 160 + h:161 + h], -(2.0 ** -(h + 1)), None, ALU.mult).then_inc(mx_done, 1)
                if m >= 1:
                    t, h = divmod(m - 1, HA)
                    nk = (t + 1) * P
                    dve.wait_ge(ex_done, m)
                    seq(V.reciprocal(small[:, 152 + h % 2:153 + h % 2], small[:, 144 + h:145 + h]))
                    V.tensor_scalar(prob[h % 4][:, :nk], prob[h % 4][:, :nk], small[:, 152 + h % 2:153 + h % 2], None, ALU.mult).then_inc(p_done, 1)
                    dve.wait_ge(p_done, m)
            if stop < 3:
                return

            def a_part(n):
                if n >= len(act_chunks):
                    return
                dve.wait_ge(a_hi_ready, n + 1)
                V.tensor_tensor(a_lo[n % 2][:], a_raw[n % 2][:], a_hi[n % 2][:].bitcast(F32), ALU.subtract).then_inc(a_lo_ready, 1)
            a_part(0)
            for n, (name, k) in enumerate(act_chunks):
                a_part(n + 1)
                if k < KT - 1:
                    continue
                bi = int(name[-1])
                for b in range(8):
                    f, half = b // 2, b % 2
                    hs = slice(half * BANK, (half + 1) * BANK)
                    sa, sr = sig[bi][:, f, hs], sig[2 + bi][:, f, hs]
                    bk.wait_full(dve, (name, b))
                    cnt = bk.at[(name, b)][1]
                    if name[:2] == "ba":
                        bk.read(V.tensor_tensor(sa, sa, bank((name, b)), ALU.mult), (name, b))
                    else:
                        m = bi * 8 + b
                        dve.wait_ge(free[b], bk.at[(f"ba{bi}", b)][1])
                        bk.read(V.tensor_tensor(sr, sr, bank((name, b)), ALU.mult), (name, b))
                        dve.wait_ge(free[b], cnt)
                        V.tensor_tensor(sr, sr, sa, ALU.add).then_inc(mixed, 1)
                        dve.wait_ge(mix_hi, m + 1)
                        V.tensor_tensor(n_lo[:, 4 * bi + f, hs], sr, n_hi[:, 4 * bi + f, hs].bitcast(F32), ALU.subtract).then_inc(mix_lo, 1)
            dve.wait_ge(xres_in, 16)
            for bi in range(2):
                for t in range(NT):
                    name = (f"wo{bi}", t)
                    bk.wait_full(dve, name)
                    cs = slice(bi * BANK, (bi + 1) * BANK)
                    V.tensor_tensor(h_sb[:, t, cs], xres[:, t, cs], bank(name), ALU.add).then_inc(h_done, 1)
                    dve.wait_ge(h_done, bi * NT + t + 1)
                    bk.read(V.memset(small[:, 276:277], 0.0), name)
                    bk.wait_read(dve, name)
            if stop < 4:
                return
            dve.wait_ge(rt_in, 48)
            for t in range(NT):
                dve.wait_ge(h_rstd, t + 1)
                V.scalar_tensor_tensor(xres[:, t, :], h_sb[:, t, :], small[:, 288 + t:289 + t], g2b[:], ALU.mult, ALU.mult).then_inc(n2_done, 1)
            name = ("lgt",)
            bk.wait_full(dve, name)
            bk.read(V.tensor_copy(lgt[:].rearrange("p t e -> p (t e)"), bank(name, NT * (NG + NE))), name)
            bk.wait_read(dve, name)

            def r(i, n=NT * NE):
                return rs[:, i, 0:n]

            def r3(i, n=NE):
                return rs[:, i, 0:NT * n].rearrange("p (t e) -> p t e", e=n)

            def wide(a, n=NE):
                return a.unsqueeze(2).to_broadcast([P, NT, n])
            gl, el = lgt[:, :, 0:NG], lgt[:, :, NG:]

            def first_of_max(dst, src, top, pri, n):
                seq(V.tensor_reduce(top, src, X, ALU.max))
                seq(V.tensor_tensor(dst, src, wide(top, n), ALU.is_equal))
                seq(V.tensor_tensor(dst, dst, cst[:, pri:pri + n].unsqueeze(1).to_broadcast([P, NT, n]), ALU.mult))
                seq(V.tensor_reduce(r(15, NT), dst, X, ALU.max))
                seq(V.tensor_tensor(dst, dst, wide(r(15, NT), n), ALU.is_equal))
            first_of_max(r3(0, NG), gl, r(9, NT), K_P4, NG)
            V.tensor_tensor(r3(1, NG), gl, wide(r(9, NT), NG), ALU.subtract).then_inc(g_shift, 1)
            seq(V.tensor_scalar(r(2, NT * NG), r(0, NT * NG), 1.0, BIG, ALU.subtract, ALU.mult))
            for e in range(EPG):
                el_e = el.rearrange("p t (g e) -> p t g e", e=EPG)[:, :, :, e]
                em_e = r3(3).rearrange("p t (g e) -> p t g e", e=EPG)[:, :, :, e]
                seq(V.tensor_tensor(em_e, el_e, r3(0, NG), ALU.mult))
                seq(V.tensor_tensor(em_e, em_e, r3(2, NG), ALU.add))
            first_of_max(r3(4), r3(3), r(10, NT), K_P16, NE)
            seq(V.scalar_tensor_tensor(r(5), r(4), -3 * BIG, r(3), ALU.mult, ALU.add))
            first_of_max(r3(6), r3(5), r(11, NT), K_P16, NE)
            V.tensor_tensor(r(8, NT), r(11, NT), r(10, NT), ALU.subtract).then_inc(e_shift, 1)
            seq(V.tensor_tensor(r(7), r(4), r(6), ALU.add))
            seq(V.memset(o_pre[:, 0:NE], 0.0))
            seq(V.memset(ones[:], 1.0))
            for t in range(NT):
                inst = V.tensor_tensor(o_pre[:, (t + 1) * NE:(t + 2) * NE], o_pre[:, t * NE:(t + 1) * NE], r3(7)[:, t, :], ALU.add)
                seq(inst) if t < NT - 1 else inst.then_inc(chosen, 1)
            dve.wait_ge(g_exp, 1)
            seq(V.tensor_reduce(r(12, NT), r3(1, NG), X, ALU.add))
            seq(V.reciprocal(r(12, NT), r(12, NT)))
            dve.wait_ge(e_exp, 1)
            seq(V.tensor_scalar(r(13, NT), r(8, NT), 1.0, None, ALU.add))
            seq(V.reciprocal(r(13, NT), r(13, NT)))
            p1, p2 = small[:, 304:312], small[:, 312:320]
            seq(V.tensor_tensor(p1, r(12, NT), r(13, NT), ALU.mult))
            seq(V.tensor_tensor(p2, p1, r(8, NT), ALU.mult))
            bk.wait_full(dve, ("rank",))
            c = bk.col(("rank",))
            seq(V.tensor_copy(small[:, 320:336], ps[:, c + NT * NE:c + (NT + 1) * NE]))
            seq(V.tensor_tensor(r3(0, NT) if False else rs[:, 0, 0:NE * NT].rearrange("p (e m) -> p e m", m=NT),
                                small[:, 320:336].unsqueeze(2).to_broadcast([P, NE, NT]),
                                cst[:, K_THR:K_THR + NE * NT].rearrange("p (e m) -> p e m", m=NT), ALU.is_gt))
            seq(V.tensor_reduce(small[:, 336:352], rs[:, 0, 0:NE * NT].rearrange("p (e m) -> p e m", m=NT), X, ALU.add))
            two = rs[:, 0:2, :].rearrange("p a n -> p (a n)").rearrange("p (e f) -> p e f", f=NE)
            seq(V.tensor_tensor(two, cst[:, K_EXC:K_EXC + NE * NE].rearrange("p (e f) -> p e f", f=NE),
                                small[:, 336:352].unsqueeze(1).to_broadcast([P, NE, NE]), ALU.mult))
            seq(V.tensor_reduce(small[:, 352:368], two, X, ALU.add))
            seq(V.tensor_tensor(small[:, 368:384], small[:, 352:368], small[:, 336:352], ALU.add))
            four = rs[:, 0:4, :].rearrange("p a n -> p (a n)").rearrange("p (i e) -> p i e", e=NE)
            seq(V.tensor_tensor(four, small[:, 368:384].unsqueeze(1).to_broadcast([P, 32, NE]),
                                cst[:, K_TI:K_TI + 32].unsqueeze(2).to_broadcast([P, 32, NE]), ALU.is_le))
            seq(V.tensor_reduce(small[:, 384:416], four, X, ALU.add))
            seq(V.tensor_scalar(small[:, 384:416], small[:, 384:416], float(NE - 1), None, ALU.min))
            seq(V.tensor_copy(owner[:], small[:, 384:416]))
            V.tensor_tensor(fresh[:, 1:32], small[:, 385:416], small[:, 384:415], ALU.not_equal).then_inc(owner_done, 1)
            seq(V.tensor_scalar(small[:, 352:368], small[:, 352:368], float(P), None, ALU.mult))
            V.tensor_tensor(r3(5), ps[:, c:c + NT * NE].rearrange("p (t e) -> p t e", e=NE),
                            small[:, 352:368].unsqueeze(1).to_broadcast([P, NT, NE]), ALU.add).then_inc(ranked, 1)
            dve.wait_ge(ranked, 1)
            for j, oh in ((0, 4), (1, 6)):
                seq(V.tensor_tensor(r(oh), r(oh), r(5), ALU.mult))
                seq(V.tensor_reduce(small[:, 416 + 8 * j:424 + 8 * j], r3(oh), X, ALU.add))
            seq(V.tensor_copy(slot[:].rearrange("p j t -> p (j t)"), small[:, 416:432]))
            NS = 2 * NT
            at_least = rs[:, 0:4, :].rearrange("p a n -> p (a n)").rearrange("p (s i) -> p s i", i=32)
            tile_hot = rs[:, 4:8, :].rearrange("p a n -> p (a n)").rearrange("p (s i) -> p s i", i=32)
            seq(V.tensor_scalar(r(8, NS), small[:, 416:432], 1.0 / P, None, ALU.mult))
            seq(V.tensor_tensor(at_least, r(8, NS).unsqueeze(2).to_broadcast([P, NS, 32]),
                                cst[:, K_TI:K_TI + 32].unsqueeze(1).to_broadcast([P, NS, 32]), ALU.is_ge))
            seq(V.tensor_reduce(r(9, NS), at_least, X, ALU.add))
            seq(V.tensor_scalar(r(9, NS), r(9, NS), -1.0, float(P), ALU.add, ALU.mult))
            seq(V.tensor_tensor(r(10, NS), small[:, 416:432], r(9, NS), ALU.subtract))
            V.tensor_tensor(hot[:], r(10, NS).unsqueeze(2).to_broadcast([P, NS, P]),
                            cst[:, K_IO:K_IO + P].unsqueeze(1).to_broadcast([P, NS, P]), ALU.is_equal)
            seq(V.memset(tile_hot, 0.0))
            seq(V.tensor_tensor(tile_hot[:, :, 0:31], at_least[:, :, 0:31], at_least[:, :, 1:32], ALU.subtract))
            V.tensor_tensor(tile_hot, tile_hot, cst[:, K_TOK:K_TOK + NS].unsqueeze(2).to_broadcast([P, NS, 32]), ALU.mult).then_inc(hot_done, 1)
            bk.wait_full(dve, ("token",))
            V.tensor_copy(token[:], bank(("token",), 32)).then_inc(token_done, 1)

            def w_part(i, j):
                b = i % 2
                dve.wait_ge(ehi_done[j], i + 1)
                ws = slice(j * 2048, (j + 1) * 2048)
                V.tensor_tensor(e_lo[b][:, ws], e_raw[b][:, ws], e_hi[b][:, ws].bitcast(F32), ALU.subtract).then_inc(elo_done[j], 1)

            def x_part(i):
                dve.wait_ge(exT_hi, i + 1)
                V.tensor_tensor(x_lo[i % 2][:].rearrange("p k q -> p (k q)"), ps[:, B_XT:B_XT + D],
                                x_hi[i % 2][:].rearrange("p k q -> p (k q)").bitcast(F32), ALU.subtract).then_inc(exT_lo, 1)

            def a_part2(i):
                dve.wait_ge(eaT_hi, i + 1)
                V.tensor_tensor(at_lo[:].rearrange("p k q -> p (k q)"), ps[:, B_AT:B_AT + FF],
                                at_hi[:].rearrange("p k q -> p (k q)").bitcast(F32), ALU.subtract).then_inc(eaT_lo, 1)

            def rows_out(i):
                dve.wait_ge(ey_full, i + 1)
                if i >= 2:
                    dve.wait_ge(ey_out[i % 2], 16 * (i // 2))
                V.tensor_copy(e_y[i % 2][:], ps[:, B_Y:B_Y + D]).then_inc(ey_read, 1)
            dve.wait_ge(n2_stored, 16 * NT)
            dve.wait_ge(h_stored, 16 * NT)
            w_part(0, 0)
            w_part(0, 2)
            x_part(0)
            for i in range(NTILE):
                if i:
                    a_part2(i - 1)
                if i + 1 < NTILE:
                    x_part(i + 1)
                    w_part(i + 1, 0)
                dve.wait_ge(gu_silu, i + 1)
                if i:
                    dve.wait_ge(eaT_full, i)
                V.tensor_tensor(arow[:], gated[:], ps[:, B_GU + FF:B_GU + 2 * FF], ALU.mult).then_inc(gu_read, 1)
                if i:
                    rows_out(i - 1)
                if i + 1 < NTILE:
                    w_part(i + 1, 2)
            a_part2(NTILE - 1)
            rows_out(NTILE - 1)
            dve.wait_ge(th_in, 16 * NT)
            for t in range(NT):
                dve.wait_ge(ty_in[t % 3], 32 * (t // 3 + 1))
                y0, y1 = (y[:] for y in t_y[t % 3])
                V.scalar_tensor_tensor(t_h[t][:], y0, small[:, 304 + t:305 + t], t_h[t][:], ALU.mult, ALU.add).then_inc(t_half, 1)
                dve.wait_ge(t_half, t + 1)
                V.scalar_tensor_tensor(t_h[t][:], y1, small[:, 312 + t:313 + t], t_h[t][:], ALU.mult, ALU.add).then_inc(t_sum, 1)

        @block.gpsimd
        def _(pool):
            seq = Seq(pool, s_pool)
            G = nc.gpsimd
            nhalf = cst[:, K_NH:K_NH + 1]

            def rstd(dst, src, n, width, last=None):
                seq(G.tensor_scalar(dst, src, 1.0 / width, EPS, ALU.mult, ALU.add))
                inst = G.tensor_tensor(dst, dst, nhalf.to_broadcast([P, n]), ALU.pow)
                if last is None:
                    seq(inst)
                else:
                    inst.then_inc(*last)

            def lo(c):
                if c >= len(chunks):
                    return
                i, k = chunks[c]
                width = sum(p[2] for p in blocks[i][2])
                pool.wait_ge(hi_ready, c + 1)
                G.tensor_tensor(w_lo[c % NH][:, :width], w_raw[c % NR][:, :width], w_hi[c % NH][:, :width].bitcast(F32),
                                ALU.subtract).then_inc(lo_ready, 1)

            def ahead(name):
                for k in range(KT):
                    lo(number[name] * KT + k + NH - 1)
            pool.wait_ge(const_in, 16 * 4)
            for half in range(2):
                pool.wait_ge(sq_done, 4 * (half + 1))
                rstd(small[:, 8 + 4 * half:12 + 4 * half], small[:, 4 * half:4 * half + 4], 4, D, (rstd1, 1))
            for c in range(NH - 1):
                lo(c)
            ahead("kv")
            ahead("qi") if False else None
            pool.wait_ge(kv_sq, 1)
            rstd(small[:, 32:40], small[:, 16:24], NT, KVL)
            rstd(small[:, 40:48], small[:, 24:32], NT, DI, (kv_rstd, 1))
            ahead("qi")
            pool.wait_ge(k_sq, 1)
            rstd(small[:, 56:64], small[:, 48:56], NT, DH, (k_rstd, 1))

            def out_gate(p):
                pass

            def out_head(h):
                pass

            def out_q(b):
                if b == 1:
                    for bb in range(2):
                        for t in range(NT):
                            bk.wait_read(pool, (f"q{bb}", t))
                    qr = small[:, S_QR:S_QR + NT * HA]
                    rstd(qr, qr, NT * HA, DH)
                    seq(G.tensor_tensor(qr.rearrange("p (t h) -> p t h", h=HA), qr.rearrange("p (t h) -> p t h", h=HA),
                                        cst[:, K_SI:K_SI + HA].unsqueeze(1).to_broadcast([P, NT, HA]), ALU.mult))

            def out_phase1(h):
                if h == HR - 1:
                    return
                for half in range(2):
                    b, cnt, _ = bk.at[("sc", h, half)]
                    pool.wait_ge(free[b], cnt)
                G.tensor_tensor(sT[:], sT[:], cst[:, K_RM + h * P:K_RM + (h + 1) * P].unsqueeze(1).to_broadcast([P, NT, P]),
                                ALU.mult).then_inc(sT_done, 1)
                for i in range(4):
                    b, cnt, _ = bk.at[("kvs", h, i)]
                    pool.wait_ge(free[b], cnt)
                for c in range(1, NT - 1):
                    seq(G.tensor_scalar(stmp[:], state[:, c - 1, :], GC[h], 0.0, ALU.mult, ALU.add))
                    inst = G.tensor_tensor(state[:, c, :], state[:, c, :], stmp[:], ALU.add)
                    if c == NT - 2:
                        inst.then_inc(state_done, 1)
                        pool.wait_ge(state_done, h + 1)
                    else:
                        seq(inst)

            def out_phase2(h):
                for i in range(4):
                    b, cnt, _ = bk.at[("ro", h, i)]
                    pool.wait_ge(free[b], cnt)
                G.tensor_scalar(small[:, 104:112], small[:, 96:104], -1.0 / DV, 0.0, ALU.mult, ALU.add).then_inc(o_mu, 1)
                pool.wait_ge(o_var, h + 1)
                if h >= 2:
                    rstd(small[:, 120:128], small[:, 112:120], NT, DV, (o_rstd, 1))
                    return
                rstd(small[:, 120:128], small[:, 112:120], NT, DV)
                for c in range(NT):
                    inst = G.tensor_scalar(ro[:, c, :], ro[:, c, :], small[:, 104 + c:105 + c], small[:, 120 + c:121 + c], ALU.add, ALU.mult)
                seq(inst)
                G.tensor_tensor(ro[:], ro[:], gate[:, :, h % 2 * DV:(h % 2 + 1) * DV], ALU.mult).then_inc(o_done, 1)

            def out_block(name):
                ahead(name)
                kind, i = name[:-1], int(name[-1])
                {"gate": out_gate, "head": out_head, "q": out_q}[kind](i)
            for what, m in ret_order:
                {"block": out_block, "phase1": out_phase1, "phase2": out_phase2, "turn": lambda h: None}[what](m)
            if stop < 2:
                return
            for t in range(NT):
                pool.wait_ge(q_in[t % 2], 16 * (t // 2 + 1))
                G.tensor_tensor(qrow[t % 2][:], qrow[t % 2][:], small[:, S_QR + HA * t:S_QR + HA * (t + 1)].unsqueeze(2).to_broadcast([P, HA, DH]),
                                ALU.mult).then_inc(q_scaled, 1)
            if stop < 3:
                return
            for b in blocks[10:]:
                ahead(b[0])
            if stop < 4:
                return
            for t in range(NT):
                pool.wait_ge(h_half_sq, t + 1)
                pool.wait_ge(h_sq, t + 1)
                seq(G.tensor_tensor(small[:, 288 + t:289 + t], small[:, 280 + t:281 + t], small[:, 296 + t:297 + t], ALU.add))
                rstd(small[:, 288 + t:289 + t], small[:, 288 + t:289 + t], 1, D, (h_rstd, 1))

            def store_y(i):
                pool.wait_ge(ey_read, i + 1)
                pool.dma_start(y_dram[tile_at(i) * P:(tile_at(i) + 1) * P, :], e_y[i % 2][:]).then_inc(ey_out[i % 2], 16)

            def gather_rows(i):
                if i >= NTILE:
                    return
                if i >= 2:
                    pool.wait_ge(exT_full, i - 1)
                G.indirect_dma_start(out=e_x[i % 2][:], out_offset=None, in_=n2_dram,
                                     in_offset=bass.IndirectOffsetOnAxis(ap=token[:, tile_at(i):tile_at(i) + 1], axis=0)).then_inc(ex_in[i % 2], 16)
            pool.wait_ge(token_done, 1)
            pool.wait_ge(n2_stored, 16 * NT)
            pool.wait_ge(h_stored, 16 * NT)
            gather_rows(0)
            gather_rows(1)
            for i in range(NTILE + 1):
                if i < NTILE:
                    pool.wait_ge(ehi_done[1], i + 1)
                    G.tensor_tensor(e_lo[i % 2][:, 2048:4096], e_raw[i % 2][:, 2048:4096], e_hi[i % 2][:, 2048:4096].bitcast(F32),
                                    ALU.subtract).then_inc(elo_done[1], 1)
                gather_rows(i + 2)
                if i >= 2:
                    store_y(i - 2)
            store_y(NTILE - 1)
            for i in range(2):
                pool.wait_ge(ey_out[i], 16 * ((NTILE + 1 - i) // 2))
            for j in range(3):
                pool.wait_ge(elo_done[j], NTILE)
            for t in range(NT):
                if t >= 3:
                    pool.wait_ge(t_sum, t - 2)
                for j in range(2):
                    G.indirect_dma_start(out=t_y[t % 3][j][:], out_offset=None, in_=y_dram,
                                         in_offset=bass.IndirectOffsetOnAxis(ap=slot[:, j, t:t + 1], axis=0)).then_inc(ty_in[t % 3], 16)


def kernel(**inputs):
    import concourse.bacc as bacc
    from concourse.bass_utils import run_bass_kernel_spmd as run

    nc = bacc.Bacc("TRN2", target_bir_lowering=False, num_devices=1)
    arrays, w = {}, {}
    shapes = {
        "x": ("x", (S, D)), "w_in": ("w_in", (D, C_GR + D)),
        "w_kv_up": ("w_kv_up", (KVL, 2 * DH)), "w_att": ("w_att_branch", (D, D)), "w_ret": ("w_ret_branch", (D, D)), "w_out": ("w_out", (D, D)),
        "norm2_g": ("norm2_g", (D,)),
        "w_gate": ("w_exp_gate", (NE * D, FF)), "w_up": ("w_exp_up", (NE * D, FF)), "w_down": ("w_exp_down", (NE * FF, D)),
    }
    for name, (src, shape) in shapes.items():
        arrays[f"in_{name}"] = np.ascontiguousarray(inputs[src]).reshape(shape)
    arrays["in_w_rt"] = np.concatenate([np.asarray(inputs["w_group_router"]).reshape(D, NG),
                                        np.asarray(inputs["w_expert_router"]).reshape(D, NE)], axis=1)
    arrays["in_b_rt"] = np.concatenate([np.asarray(inputs["b_group_router"]).reshape(NG),
                                        np.asarray(inputs["b_expert_router"]).reshape(NE)])
    arrays["in_cst"] = constants()
    g = {n: np.asarray(inputs[n], np.float32).reshape(-1) for n in inputs if n.endswith("_g")}
    arrays["in_gains"] = np.ascontiguousarray(np.concatenate([
        g["norm1_g"].reshape(KT, P), g["kv_norm_g"].reshape(2, P), g["k_norm_g"].reshape(1, P),
        np.tile(g["idx_k_norm_g"], 2).reshape(1, P), g["ret_norm_g"].reshape(KT, P), g["q_norm_g"].reshape(1, P)]).T)
    for name, a in arrays.items():
        w[name[3:]] = nc.dram_tensor(name, a.shape, F32, kind="ExternalInput").ap()
    out = nc.dram_tensor("out", (S, D), F32, kind="ExternalOutput").ap()
    scratch = {n: nc.dram_tensor(f"{n}_dram", (S, D), F32, kind=SCRATCH).ap() for n in ("q", "att", "ret", "h", "n2")}
    scratch["y"] = nc.dram_tensor("y_dram", (NTILE * P, D), F32, kind=SCRATCH).ap()
    program(nc, w, scratch, out, STOP)
    r = run(nc, [arrays], core_ids=[0])
    return r.results[0]["out"].reshape(1, S, D)


SCRATCH = "Internal"
STOP = 4
```

```python
from contextlib import ExitStack

import numpy as np
import concourse.bass as bass
from concourse import mybir

ALU = mybir.AluOpType
ACT = mybir.ActivationFunctionType
F32 = mybir.dt.float32
F32R = mybir.dt.float32r
I32 = mybir.dt.int32
U32 = mybir.dt.uint32
X = mybir.AxisListType.X

P = 128
S = 1024
D = 1024
NT = S // P
KT = D // P
HA, DH = 8, 128
KVL = 256
HI, DI = 8, 64
TOPK = 256
HR, DK, DV = 4, 128, 256
NG, EPG, NE, FF = 4, 4, 16, 256
EPS = 1e-6
BIG = 1e30
TAKEN = -3e38
BANK = 512

C_Q = 0
C_KV = C_Q + HA * DH
C_QI = C_KV + KVL
C_KI = C_QI + HI * DI
C_RQ = C_KI + DI + HI
C_RK = C_RQ + HR * DK
C_RV = C_RK + HR * DK
C_RG = C_RV + HR * DV
C_GA = C_RG + HR * DV
C_GR = C_GA + D
KVW = KVL + DI + HI

K_ID = 0
K_REL = K_ID + P
K_CAUS = K_REL + S
K_RM = K_CAUS + P
K_QD = K_RM + HR * P
K_KD = K_QD + HR
K_TRI = K_KD + HR
K_THR = K_TRI + P
K_EXC = K_THR + NE * NT
K_P16 = K_EXC + NE * NE
K_P4 = K_P16 + NE
K_TI = K_P4 + NG
NTILE = S * 2 // P + NE - 1
LOOP_FROM, LOOP_TO = 4, NTILE // 2 * 2 - 2
K_SI = K_TI + 32
K_TOK = K_SI + HA
K_IO = K_TOK + 2 * NT
K_END = K_IO + P
NGAIN = 21

GAMMA = [1.0 - 2.0 ** (-5.0 - h) for h in range(HR)]
GC = [g ** P for g in GAMMA]


def constants():
    c = np.zeros((P, K_END), np.float64)
    p = np.arange(P)[:, None]
    i = np.arange(P)[None, :]
    c[:, K_ID:K_ID + P] = p == i
    c[:, K_REL:K_REL + S] = np.arange(S)[None, :] - p
    c[:, K_CAUS:K_CAUS + P] = np.where(i <= p, 0.0, -BIG)
    for h, g in enumerate(GAMMA):
        c[:, K_RM + h * P:K_RM + (h + 1) * P] = np.where(p <= i, g ** -(p + 1.0), 0.0) * DK ** -0.5
        c[:, K_QD + h] = g ** (np.arange(P) + 1.0)
        c[:, K_KD + h] = g ** (P - 1.0 - np.arange(P)) * DK ** -0.5
    c[:, K_TRI:K_TRI + P] = p < i
    c[:, K_THR:K_THR + NE * NT] = np.tile(np.arange(NT) * float(P), NE)[None, :]
    e = np.arange(NE)
    c[:, K_EXC:K_EXC + NE * NE] = (e[None, :] < e[:, None]).astype(np.float64).reshape(1, -1)
    c[:, K_P16:K_P16 + NE] = NE - e
    c[:, K_P4:K_P4 + NG] = NG - np.arange(NG)
    c[:, K_TI:K_TI + 32] = np.arange(32)
    c[:, K_SI:K_SI + HA] = 2.0 ** (np.arange(HA) + 1.0)
    c[:, K_TOK:K_TOK + 2 * NT] = np.tile(np.arange(NT) * float(P), 2)[None, :] + p
    c[:, K_IO:K_IO + P] = i
    return c.astype(np.float32)


class Banks:

    def __init__(self, full, free):
        self.full, self.free = full, free
        self.count = [0] * 8
        self.released = [None] * 8
        self.at = {}

    def use(self, name, bank, n=1):
        before = sorted({self.released[b] for b in range(bank, bank + n)} - {None})
        self.count[bank] += 1
        for b in range(bank, bank + n):
            self.released[b] = (bank, self.count[bank])
        self.at[name] = (bank, self.count[bank], before)

    def col(self, name):
        return self.at[name][0] * BANK

    def wait_free(self, eng, name):
        for b, n in self.at[name][2]:
            eng.wait_ge(self.free[b], n)

    def wait_full(self, eng, name):
        eng.wait_ge(self.full[self.at[name][0]], self.at[name][1])

    def wait_read(self, eng, name):
        eng.wait_ge(self.free[self.at[name][0]], self.at[name][1])

    def filled(self, inst, name):
        inst.then_inc(self.full[self.at[name][0]], 1)

    def read(self, inst, name):
        inst.then_inc(self.free[self.at[name][0]], 1)


class Seq:

    def __init__(self, eng, sem):
        self.eng, self.sem, self.n = eng, sem, 0

    def mark(self, inst):
        self.n += 1
        inst.then_inc(self.sem, 1)

    def wait(self):
        self.eng.wait_ge(self.sem, self.n)

    def __call__(self, inst):
        self.mark(inst)
        self.wait()


class Step:

    def __init__(self, half, parity):
        self.half, self.parity = half, parity
        self.n = half * 2 + parity

    def __add__(self, d):
        s = self.parity + d
        return Step(self.half + s // 2, s % 2)

    def __sub__(self, d):
        return self + -d

    def reached(self, n):
        return self.n >= n if isinstance(self.half, int) else n <= LOOP_FROM - 2


def each_step(eng, work, last):
    for i in range(LOOP_FROM):
        work(Step(i // 2, i % 2))
    with eng.Fori(LOOP_FROM // 2, LOOP_TO // 2) as half:
        work(Step(half, 0))
        work(Step(half, 1))
    for i in range(LOOP_TO, last + 1):
        work(Step(i // 2, i % 2))


def program(nc, w, scratch, out):
    ctx = ExitStack()
    with ctx:
        def sem(name):
            return ctx.enter_context(nc.semaphore(name))

        base = (nc.sbuf_base + 63) // 64 * 64
        place = [base]

        def sb(name, shape, dt=F32, at=None):
            n = 4 * int(np.prod(shape[1:]))
            off = place[0] if at is None else at
            if at is None:
                place[0] += (n + 31) // 32 * 32
            assert off + n <= nc.sbuf_usable_end, (name, off + n, nc.sbuf_usable_end)
            return nc.alloc_sbuf_tensor_at(name, shape, dt, offset=off)

        cst = sb("cst", [P, K_END])
        gains = sb("gains", [P, 64])
        small = sb("small", [P, 512])
        slot = sb("slot", [P, 2, NT], U32)
        owner = sb("owner", [P, 32], I32)
        fresh = sb("fresh", [P, 32], I32)
        token = sb("token", [P, 32], U32)
        rows_now = sb("rows_now", [P, 2], U32)
        nt_at = place[0]
        n_hi = sb("n_hi", [P, KT, S], F32R)
        n_lo = sb("n_lo", [P, KT, S], F32R)
        NR, NH = 4, 4
        wr_at = place[0]
        w_raw = [sb(f"w_raw{i}", [P, BANK]) for i in range(NR)]
        w_hi = [sb(f"w_hi{i}", [P, BANK], F32R) for i in range(NH)]
        w_lo = [sb(f"w_lo{i}", [P, BANK], F32R) for i in range(NH)]
        dist_at = place[0]
        dist = sb("dist", [P, NT * (NT + 1) // 2 * P])
        up_at = place[0]
        w_up = sb("w_up", [P, 2, 2 * DH])
        kT_hi = sb("kT_hi", [P, S], F32R)
        v_at = place[0]
        kvu = sb("kvu", [P, NT, 2 * DH])
        kT_lo = sb("kT_lo", [P, NT, 2 * DH], F32R, at=v_at)[:, :, 0:DH]
        r1 = place[0]
        ps = ctx.enter_context(nc.psum_tensor("ps", [P, 8 * BANK], F32))

        def r1t(name, shape, off, dt=F32):
            return sb(name, shape, dt, at=r1 + 4 * off)

        xin = r1t("xin", [P, NT, D], 0)
        kvrows = r1t("kvrows", [P, NT, KVW], 0)
        sq = r1t("sq", [P, NT, KVW], 2624)
        cT = r1t("cT", [P, 2, S], 5248)
        kdup = r1t("kdup", [P, NT, 2, DI], 7296)
        kiT_hi = r1t("kiT_hi", [P, S], 8320, F32R)
        qiT_hi = r1t("qiT_hi", [P, 4, S], 9344, F32R)
        qiT_lo = [r1t(f"qiT_lo{i}", [P, S], at, F32R) for i, at in enumerate((15488, 16512, 17536, 4096))]
        kiT_lo = r1t("kiT_lo", [P, S], 0, F32R)
        relu = [r1t(f"relu{i}", [P, S], 13440 + i * S) for i in range(2)]
        junk = r1t("junk", [P, 2, D], 15488)
        rqT = [r1t(f"rqT{i}", [P, S], i * S) for i in range(2)]
        rkT = r1t("rkT", [P, S], 2048)
        rv = [r1t(f"rv{i}", [P, NT, DV], 3072 + i * 2048) for i in range(2)]
        krow = r1t("krow", [P, NT, P], 7168)
        sT = r1t("sT", [P, NT, P], 8192)
        state = r1t("state", [P, NT - 1, DV], 9216)
        ro = r1t("ro", [P, NT, DV], 11008)
        gate = r1t("gate", [P, NT, 2 * DV], 13056)
        rT = r1t("rT", [P, S], 17408)
        rT_odd = [sb("rT_odd0", [P, BANK], at=up_at), r1t("rT_odd1", [P, BANK], 18432)]
        junk2 = r1t("junk2", [P, DV], 18432 + BANK)
        stmp = r1t("stmp", [P, DV], 17152)
        qst0 = [r1t(f"qst0_{t}", [P, BANK], at) for t, at in
                enumerate([i * BANK for i in range(2)] + [3072 + i * BANK for i in range(4)] + [7168 + i * BANK for i in range(2)])]
        qst1 = [None, None] + [r1t(f"qst1_{i}", [P, BANK], at) for i, at in
                               enumerate((6144, 3072, 3072 + BANK, 9216, 9216 + BANK, 9216 + 2 * BANK))]
        q_sq = [r1t(f"q_sq{i}", [P, 4, DH], 7168 + i * BANK) for i in range(2)]
        qrow = [r1t(f"qrow{i}", [P, HA, DH], i * D) for i in range(2)]
        qT_hi = [r1t(f"qT_hi{i}", [P, HA, P], 2048 + i * D, F32R) for i in range(2)]
        qT_lo = [[sb(f"qT_lo{2 * i + g}", [P, 4, P], F32R, at=at) for g, at in enumerate(pair)] for i, pair in enumerate(
            [(wr_at + 4 * BANK * (NR - 1), wr_at + 4 * BANK * (NR + NH - 1)),
             (wr_at + 4 * BANK * (NR + 2 * NH - 1), r1 + 4 * 18432)])]
        prob = [r1t(f"prob{i}", [P, S], 4096 + i * S) for i in range(4)]
        pT = r1t("pT", [P, NT, 2, 4 * P], 8192)
        aT = [r1t(f"aT{i}", [P, HA, P], 16384 + i * D) for i in range(2)]
        sig = [r1t(f"sig{i}", [P, 4, S], i * 4096) for i in range(4)]
        a_raw = [sb(f"a_raw{i}", [P, S], at=v_at + i * 4096) for i in range(2)]
        a_hi = [sb(f"a_hi{i}", [P, S], F32R, at=dist_at + i * 4096) for i in range(2)]
        a_lo = [sb(f"a_lo{i}", [P, S], F32R, at=dist_at + 8192 + i * 4096) for i in range(2)]
        h_sb = r1t("h_sb", [P, NT, D], 0)
        xres = r1t("xres", [P, NT, D], 8192)

        g2b = r1t("g2b", [P, D], 16384)
        w_rt = r1t("w_rt", [P, KT, NG + NE], 17408)
        b_rt = r1t("b_rt", [NG + NE, 1], 17568)
        lgT = r1t("lgT", [NG + NE, S], 17760)
        lgt = r1t("lgt", [P, NT, NG + NE], 17592)
        n2T = sb("n2T", [P, NT, D], at=nt_at)
        n2sq = sb("n2sq", [P, D], at=dist_at + 4 * 2048)
        rs = sb("rs", [P, 16, NT * NE], at=dist_at)
        o_pre = sb("o_pre", [P, (NT + 1) * NE], at=dist_at + 16 * 4 * NT * NE)
        ones = sb("ones", [P, P], at=dist_at + 4 * 4240)
        tile_tok = sb("tile_tok", [P, 2 * NT, 32], F32R, at=dist_at + 4 * 4 * NT * NE)
        hot = sb("hot", [P, 2 * NT, P], F32R, at=dist_at + 4 * (16 * NT * NE + (NT + 1) * NE))
        W3 = 3 * 4 * BANK
        e_raw = [sb(f"e_raw{i}", [P, W3], at=nt_at + i * 4 * W3) for i in range(2)]
        e_x = [sb(f"e_x{i}", [P, D], at=nt_at + 8 * W3 + i * 4 * D) for i in range(2)]
        e_y = [sb(f"e_y{i}", [P, D], at=nt_at + 8 * W3 + 8 * D + i * 4 * D) for i in range(2)]
        e_hi = [sb(f"e_hi{i}", [P, W3], F32R, at=wr_at + i * 4 * W3) for i in range(2)]
        e_lo = [sb(f"e_lo{i}", [P, W3], F32R, at=wr_at + (2 + i) * 4 * W3) for i in range(2)]
        e_at = wr_at + 16 * W3
        x_hi = [sb(f"x_hi{i}", [P, KT, P], F32R, at=e_at + i * 4 * D) for i in range(2)]
        x_lo = [sb(f"x_lo{i}", [P, KT, P], F32R, at=e_at + (2 + i) * 4 * D) for i in range(2)]
        gated = sb("gated", [P, FF], at=e_at + 16 * D)
        arow = sb("arow", [P, FF], at=e_at + 16 * D + 4 * FF)
        at_hi = sb("at_hi", [P, 2, P], F32R, at=e_at + 16 * D + 8 * FF)
        at_lo = sb("at_lo", [P, 2, P], F32R, at=e_at + 16 * D + 12 * FF)
        t_h = [sb(f"t_h{t}", [P, D], at=nt_at + 4 * W3 + t * 4 * D) if t < 6 else r1t(f"t_h{t}", [P, D], 15424 + (t - 6) * D)
               for t in range(NT)]
        t_y = [[sb(f"t_y{i}{j}", [P, D], at=nt_at + (2 * i + j) * 4 * D) for j in range(2)] for i in range(3)]

        ident = cst[:, K_ID:K_ID + P]
        G1, GKV, GK, GKI, GRT, GQ = 0, 8, 10, 11, 12, 20

        S_QR = 432

        q_dram, att_dram, ret_dram, h_dram = scratch["q"], scratch["att"], scratch["ret"], scratch["h"]
        n2_dram, y_dram = scratch["n2"], scratch["y"]

        const_in, up_in = sem("const_in"), sem("up_in")
        x_in = [sem(f"x_in{t}") for t in range(NT)]
        full = [sem(f"bank_full{b}") for b in range(8)]
        free = [sem(f"bank_free{b}") for b in range(8)]
        w_in = [sem(f"w_in{i}") for i in range(NR)]
        hi_ready, lo_ready, chunk_used = sem("hi_ready"), sem("lo_ready"), sem("chunk_used")
        s_dve, s_act, s_pool = sem("dve_seq"), sem("act_seq"), sem("pool_seq")
        sq_done, rstd1, xn_done, nhi_done = sem("sq_done"), sem("rstd1"), sem("xn_done"), sem("nhi_done")
        kv_sq, kv_rstd, ckv_n, k_sq, k_rstd, k_n = (sem(n) for n in ("kv_sq", "kv_rstd", "ckv_n", "k_sq", "k_rstd", "k_n"))
        gains_done, relu_used, dist_done = sem("gains_done"), sem("relu_used"), sem("dist_done")
        qi_hi_done, ki_hi_done = sem("qi_hi_done"), sem("ki_hi_done")
        kT_hi_done, qT_hi_done = sem("kT_hi_done"), sem("qT_hi_done")
        q0_stored, q0_squares, q1_stored, q_squares = sem("q0_stored"), sem("q0_squares"), sem("q1_stored"), sem("q_squares")
        sT_done, state_done, ret_stored = sem("sT_done"), sem("state_done"), sem("ret_stored")
        o_mu, o_var, o_rstd, o_done = sem("o_mu"), sem("o_var"), sem("o_rstd"), sem("o_done")
        q_in, q_scaled = [sem(f"q_in{i}") for i in range(2)], sem("q_scaled")
        mx_done, ex_done, p_done = sem("mx_done"), sem("ex_done"), sem("p_done")
        att_stored = [sem(f"att_stored{i}") for i in range(2)]
        a_in = [sem(f"a_in{i}") for i in range(2)]
        a_hi_ready, a_lo_ready = sem("a_hi_ready"), sem("a_lo_ready")
        mixed, mix_hi, mix_lo = sem("mixed"), sem("mix_hi"), sem("mix_lo")
        xres_in, h_stored = [sem(f"xres_in{t}") for t in range(NT)], sem("h_stored")
        rt_in, h_half_sq, h_sq, h_rstd, n2_done, n2_stored = (sem(n) for n in ("rt_in", "h_half_sq", "h_sq", "h_rstd", "n2_done", "n2_stored"))
        g_shift, g_exp, e_shift, e_exp = (sem(n) for n in ("g_shift", "g_exp", "e_shift", "e_exp"))
        chosen, ranked, owner_done = sem("chosen"), sem("ranked"), sem("owner_done")
        hot_done, token_done, rows_placed = sem("hot_done"), sem("token_done"), sem("rows_placed")
        ew_in = [[sem(f"ew_in{i}{j}") for j in range(3)] for i in range(2)]
        ex_in = [sem(f"ex_in{i}") for i in range(2)]
        ehi_done, elo_done = [sem(f"ehi_done{j}") for j in range(3)], [sem(f"elo_done{j}") for j in range(3)]
        exT_full, exT_hi, exT_lo = sem("exT_full"), sem("exT_hi"), sem("exT_lo")
        gu_full, gu_silu, gu_read = sem("gu_full"), sem("gu_silu"), sem("gu_read")
        eaT_full, eaT_hi, eaT_lo = sem("eaT_full"), sem("eaT_hi"), sem("eaT_lo")
        ey_full, ey_read, ey_out = sem("ey_full"), sem("ey_read"), [sem(f"ey_out{i}") for i in range(2)]
        ty_in, th_in = [sem(f"ty_in{i}") for i in range(3)], sem("th_in")
        t_half, t_sum, t_out = sem("t_half"), sem("t_sum"), sem("t_out")

        def cols(src, c0, n, at=0):
            return (src, c0, n, at)
        wi = w["w_in"]
        blocks = [
            ("kv", "R", [cols(wi, C_KV, KVL, 0), cols(wi, C_KI, DI + HI, KVL)]),
            ("qi", "C", [cols(wi, C_QI, BANK)]),
        ]

        def gate_block(p):
            return (f"gate{p}", "R", [cols(wi, C_RG + p * BANK, BANK)])

        def head_block(h):
            return (f"head{h}", "H", [cols(wi, C_RQ + h * DK, DK, 0), cols(wi, C_RK + h * DK, DK, DK),
                                      cols(wi, C_RV + h * DV, DV, 2 * DK)])

        def q_block(b):
            return (f"q{b}", "R", [cols(wi, C_Q + b * BANK, BANK)])
        blocks += [gate_block(0), head_block(0), head_block(1), q_block(0),
                   gate_block(1), head_block(2), head_block(3), q_block(1)]
        for g, c0 in (("ga", C_GA), ("gr", C_GR)):
            blocks += [(f"{g}{b}", "C", [cols(wi, c0 + b * BANK, BANK)]) for b in range(2)]
        for g, src in (("ba", w["w_att"]), ("br", w["w_ret"])):
            blocks += [(f"{g}{b}", "A", [cols(src, b * BANK, BANK)]) for b in range(2)]
        blocks += [(f"wo{b}", "M", [cols(w["w_out"], b * BANK, BANK)]) for b in range(2)]
        number = {name: i for i, (name, _, _) in enumerate(blocks)}
        chunks = [(i, k) for i in range(len(blocks)) for k in range(KT)]
        landed, n_in = [], [0] * NR
        for c, (i, k) in enumerate(chunks):
            n_in[c % NR] += 16 * len(blocks[i][2])
            landed.append(n_in[c % NR])
        act_chunks = [(name, k) for name in ("ba0", "ba1", "br0", "br1") for k in range(KT)]

        bk = Banks(full, free)

        def use_block(name):
            for b in range(8):
                bk.use((name, b), b)
        for half in range(2):
            for k in range(KT):
                bk.use(("xT", half, k), k)
        use_block("kv")
        use_block("qi")
        for j in range(2):
            for half in range(2):
                bk.use(("cT", j, half), 2 * j + half)
        for half in range(2):
            bk.use(("kiT", half), 4 + half)
        for i in range(4):
            bk.use(("kvu", i), i)
        for t in range(2, NT):
            for h in range(HI):
                bk.use(("idx", t, h), 2 * (h % 4), 2)
        for half in range(2):
            bk.use(("kT", half), 6 + half)

        def use_phase1(h):
            for half in range(2):
                bk.use(("krow", h, half), half)
            for half in range(2):
                bk.use(("sc", h, half), 2 + half)
            for i in range(4):
                bk.use(("kvs", h, i), 4 + i)

        def use_phase2(h):
            for i in range(4):
                bk.use(("ro", h, i), i)

        def use_turn(h):
            for j in range(2):
                for half in range(2):
                    bk.use(("rT", h, j, half), 4 + 2 * j + half)
        ret_order = [("block", "gate0"), ("block", "head0"), ("phase1", 0), ("block", "head1"), ("phase2", 0),
                     ("phase1", 1), ("block", "q0"), ("turn", 0), ("phase2", 1), ("block", "gate1"), ("turn", 1),
                     ("block", "head2"), ("phase1", 2), ("block", "head3"), ("phase2", 2), ("phase1", 3),
                     ("turn", 2), ("phase2", 3), ("block", "q1"), ("turn", 3)]
        for what, n in ret_order:
            {"block": use_block, "phase1": use_phase1, "phase2": use_phase2, "turn": use_turn}[what](n)
        STEPS = NT * HA

        def q_turned_at(m):
            return (m // HA + 1, m % HA // 2 - 1) if m % HA in (3, 5) and m // HA + 1 < NT else None

        RET_ROUND = 23

        def pv_at(m):
            if 6 <= m < STEPS + 6:
                (t, h) = divmod(m - 6, HA)
                return t, h // 4, h % 4

        for g in range(2):
            bk.use(("qT", 0, g), 6 + g)
        for m in range(STEPS + 6):
            if m < STEPS:
                bk.use(("lg", m), 2 * (m % 2), 2)
            if 2 <= m < STEPS + 2:
                for i in range((m - 2) // HA // 4 + 1):
                    bk.use(("pT", m - 2, i), 4 + i)
            if pv_at(m) and pv_at(m)[2] == 0:
                bk.use(("pv", *pv_at(m)[:2]), 6)
            if q_turned_at(m):
                bk.use(("qT", *q_turned_at(m)), 7)
        for name in [b[0] for b in blocks[10:]]:
            use_block(name)
        for t in range(NT):
            bk.use(("n2T", t), 2 * (t % 2), 2)
        for g in range(2):
            bk.use(("rt", g), 4 + g)
        bk.use(("lgt",), 6)
        bk.use(("rank",), 6)
        bk.use(("token",), 7)
        B_XT, B_GU, B_AT, B_Y = 0, 2 * BANK, 3 * BANK, 4 * BANK

        def bank(name, n=BANK):
            c = bk.col(name)
            return ps[:, c:c + n]

        def used(c):
            i, k = chunks[c]
            if k == KT - 1:
                b, n, _ = bk.at[(blocks[i][0], 7)]
                return full[b], n
            return chunk_used, i * (KT - 1) + k + 1

        def tile_at(i):
            return i.half + i.parity * ((NTILE + 1) // 2)

        def tile_off(t):
            return t * (t + 1) // 2 * P

        block = ctx.enter_context(nc.Block())

        @block.sync
        def _(sp):
            def load_chunk(c):
                i, k = chunks[c]
                if c >= NR:
                    sp.wait_ge(lo_ready, c - NR + 1)
                for src, c0, n, at in blocks[i][2]:
                    sp.dma_start(w_raw[c % NR][:, at:at + n],
                                 src[k * P:(k + 1) * P, c0:c0 + n]).then_inc(w_in[c % NR], 16)

            for t in range(NT):
                sp.dma_start(xin[:, t, :], w["x"][t * P:(t + 1) * P, :]).then_inc(x_in[t], 16)
                if t == 3:
                    sp.dma_start(cst[:], w["cst"]).then_inc(const_in, 16)
                    sp.dma_start(gains[:, 0:NGAIN], w["gains"]).then_inc(const_in, 16)
            for j in range(2):
                sp.dma_start(w_up[:, j, :], w["w_kv_up"][j * P:(j + 1) * P, :]).then_inc(up_in, 16)
            first = number["ga0"] * KT + NR - 1
            for c in range(min(first, len(chunks))):
                load_chunk(c)

            def load_q(t):
                if t >= 2:
                    bk.wait_full(sp, ("qT", t - 2, 1))
                    sp.dma_start(qrow[t % 2][:].rearrange("p h d -> p (h d)"),
                                 q_dram[t * P:(t + 1) * P, :]).then_inc(q_in[t % 2], 16)
                    return
                bk.wait_full(sp, ("ro", HR - 2 + t, 3))
                sp.dma_start(qrow[t][:, 0:4].rearrange("p h d -> p (h d)"),
                             q_dram[t * P:(t + 1) * P, 0:BANK]).then_inc(q_in[t], 16)
            sp.wait_ge(q0_stored, 16 * NT)
            load_q(0)
            load_q(1)
            sp.wait_ge(q1_stored, 16 * (NT - 2))
            for t in range(NT):
                if t + 2 < NT:
                    load_q(t + 2)
                for g in range(2):
                    bk.wait_read(sp, ("pv", t, g))
                sp.dma_start(att_dram.rearrange("(h p) s -> p h s", p=P)[:, :, t * P:(t + 1) * P],
                             aT[t % 2][:]).then_inc(att_stored[t % 2], 16)
            sp.wait_ge(att_stored[0], 16 * NT // 2)
            sp.wait_ge(att_stored[1], 16 * NT // 2)
            for c in range(first, number["ba0"] * KT):
                load_chunk(c)
            sp.wait_ge(ret_stored, 48 * HR)
            for n, (name, k) in enumerate(act_chunks):
                load_chunk(number["ba0"] * KT + n)
                if n >= 2:
                    sp.wait_ge(a_lo_ready, n - 1)
                src = att_dram if name[:2] == "ba" else ret_dram
                sp.dma_start(a_raw[n % 2][:], src[k * P:(k + 1) * P, :]).then_inc(a_in[n % 2], 16)
            for c in range(number["wo0"] * KT, len(chunks)):
                load_chunk(c)
                k = c - number["wo0"] * KT
                if k == 4:
                    sp.wait_ge(mix_lo, 16)
                if 4 <= k < 8:
                    for t in range(2 * k - 8, 2 * k - 6):
                        sp.dma_start(xres[:, t, :], w["x"][t * P:(t + 1) * P, :]).then_inc(xres_in[t], 16)
            sp.dma_start(g2b[:], w["norm2_g"].partition_broadcast(P)).then_inc(rt_in, 16)
            sp.dma_start(w_rt[:], w["w_rt"].rearrange("(k p) n -> p k n", p=P)).then_inc(rt_in, 16)
            sp.dma_start(b_rt[:], w["b_rt"].unsqueeze(1)).then_inc(rt_in, 16)
            for t in range(NT):
                bk.wait_read(sp, ("wo1", t))
                sp.dma_start(h_dram[t * P:(t + 1) * P, :], h_sb[:, t, :]).then_inc(h_stored, 16)
                sp.wait_ge(n2_done, t + 1)
                sp.dma_start(n2_dram[t * P:(t + 1) * P, :], xres[:, t, :]).then_inc(n2_stored, 16)
            sp.wait_ge(owner_done, 1)

            def load_expert(i):
                n = tile_at(i)
                e = sp.value_load(owner[0:1, bass.ds(n, 1)], min_val=0, max_val=NE - 1)
                b = i.parity
                new = {"cond": sp.value_load(fresh[0:1, bass.ds(n, 1)], min_val=0, max_val=1)} if i.reached(2) else {}
                for j in range(2):
                    if i.reached(2):
                        sp.wait_ge(elo_done[j], i.n - 1)
                    for at, src in ((0, w["w_gate"]), (FF, w["w_up"])):
                        rows = src[bass.ds(e * D, D), :].rearrange("(p k) f -> p (k f)", p=P)[:, j * 1024:(j + 1) * 1024]
                        sp.dma_start(e_raw[b][:, j * 2048 + at * 4:j * 2048 + at * 4 + 1024], rows, **new).then_inc(ew_in[b][j], 16)
                    if not i.reached(2) and i.n == 1 and j == 0:
                        sp.wait_ge(ex_in[0], 16)
                if i.reached(2):
                    sp.wait_ge(elo_done[2], i.n - 1)
                rows = w["w_down"][bass.ds(e * FF, FF), :].rearrange("(p k) n -> p (k n)", p=P)
                sp.dma_start(e_raw[b][:, 4096:], rows, **new).then_inc(ew_in[b][2], 16)
            each_step(sp, load_expert, NTILE - 1)

            sp.wait_ge(h_stored, 16 * NT)
            for j in range(3):
                sp.wait_ge(elo_done[j], NTILE - 1)
            for t in range(NT):
                sp.dma_start(t_h[t][:], h_dram[t * P:(t + 1) * P, :]).then_inc(th_in, 16)
            for t in range(NT):
                sp.wait_ge(t_sum, t + 1)
                sp.dma_start(out[t * P:(t + 1) * P, :], t_h[t][:]).then_inc(t_out, 16)
            sp.wait_ge(t_out, 16 * NT)

        @block.tensor
        def _(pe):
            mm, tr = nc.tensor.matmul, nc.tensor.transpose

            def three(out, a, b, first, last, skip=False):
                mm(out, a[0], b[0], start=first, stop=False, skip_group_check=skip)
                mm(out, a[0], b[1], start=False, stop=False, skip_group_check=skip)
                return mm(out, a[1], b[0], start=False, stop=last, skip_group_check=skip)

            def gemm(name):
                i = number[name]
                kind = blocks[i][1]
                width = sum(p[2] for p in blocks[i][2])
                for k in range(KT):
                    c = i * KT + k
                    pe.wait_ge(lo_ready, c + 1)
                    if name == "wo0":
                        pe.wait_ge(mix_lo, 2 * (k + 1))
                    if kind == "A":
                        n = act_chunks.index((name, k))
                        pe.wait_ge(a_lo_ready, n + 1)
                    wh, wl = w_hi[c % NH], w_lo[c % NH]
                    for b in range(8):
                        if k == 0:
                            bk.wait_free(pe, (name, b))
                        o = bank((name, b))
                        f, l = k == 0, k == KT - 1
                        if kind in ("R", "M"):
                            t = slice(b * P, (b + 1) * P)
                            last = three(o[:, :width], (n_hi[:, k, t], n_lo[:, k, t]),
                                         (wh[:, :width], wl[:, :width]), f, l)
                        elif kind in ("C", "A") or b < 4:
                            fs = slice(b // 2 * P, (b // 2 + 1) * P)
                            ts = slice(b % 2 * BANK, (b % 2 + 1) * BANK)
                            act = (a_hi[n % 2][:, ts], a_lo[n % 2][:, ts]) if kind == "A" else (n_hi[:, k, ts], n_lo[:, k, ts])
                            last = three(o, (wh[:, fs], wl[:, fs]), act, f, l)
                        else:
                            for s in range(2):
                                t = slice((2 * (b - 4) + s) * P, (2 * (b - 4) + s + 1) * P)
                                last = three(o[:, s * DV:(s + 1) * DV], (n_hi[:, k, t], n_lo[:, k, t]),
                                             (wh[:, 2 * DK:], wl[:, 2 * DK:]), f and s == 0, l, skip=True)
                        if l:
                            bk.filled(last, (name, b))
                        elif b == 7:
                            last.then_inc(chunk_used, 1)

            pe.wait_ge(const_in, 16 * 2)
            for half in range(2):
                pe.wait_ge(xn_done, 4 * (half + 1))
                for k in range(KT):
                    bk.wait_free(pe, ("xT", half, k))
                    for t in range(4):
                        last = tr(bank(("xT", half, k))[:, t * P:(t + 1) * P],
                                  xin[:, 4 * half + t, k * P:(k + 1) * P], ident)
                    bk.filled(last, ("xT", half, k))
            gemm("kv")
            gemm("qi")
            pe.wait_ge(ckv_n, 1)
            for j in range(2):
                for half in range(2):
                    bk.wait_free(pe, ("cT", j, half))
                    for t in range(4):
                        last = tr(bank(("cT", j, half))[:, t * P:(t + 1) * P],
                                  kvrows[:, 4 * half + t, j * P:(j + 1) * P], ident)
                    bk.filled(last, ("cT", j, half))
            for half in range(2):
                bk.wait_free(pe, ("kiT", half))
                for t in range(4):
                    last = tr(bank(("kiT", half))[:, t * P:(t + 1) * P],
                              kdup[:, 4 * half + t].rearrange("p a d -> p (a d)"), ident)
                bk.filled(last, ("kiT", half))
            pe.wait_ge(up_in, 16 * 2)
            for i in range(4):
                bk.wait_read(pe, ("cT", i // 2, i % 2))
            for i in range(4):
                bk.wait_free(pe, ("kvu", i))
                for s in range(2):
                    t = 2 * i + s
                    for j in range(2):
                        last = mm(bank(("kvu", i))[:, s * 2 * DH:(s + 1) * 2 * DH], cT[:, j, t * P:(t + 1) * P],
                                  w_up[:, j, :], start=j == 0, stop=j == 1)
                bk.filled(last, ("kvu", i))
            for half in range(2):
                pe.wait_ge(free[4 + half], bk.at[("kiT", half)][1])
            for t in range(2, NT):
                nk = (t + 1) * P
                for h in range(HI):
                    name = ("idx", t, h)
                    bk.wait_free(pe, name)
                    c = bk.col(name)
                    s = slice(h % 2 * DI, (h % 2 + 1) * DI)
                    for k0 in range(0, nk, BANK):
                        n = min(BANK, nk - k0)
                        qs, ks = slice(t * P, (t + 1) * P), slice(k0, k0 + n)
                        last = three(ps[:, c + k0:c + k0 + n], (qiT_hi[s, h // 2, qs], qiT_lo[h // 2][s, qs]),
                                     (kiT_hi[s, ks], kiT_lo[s, ks]), True, True)
                    bk.filled(last, name)
            pe.wait_ge(k_n, 1)
            for half in range(2):
                bk.wait_free(pe, ("kT", half))
                for t in range(4):
                    last = tr(bank(("kT", half))[:, t * P:(t + 1) * P], kvu[:, 4 * half + t, 0:DH], ident)
                bk.filled(last, ("kT", half))

            def phase1(h):
                for half in range(2):
                    name = ("krow", h, half)
                    bk.wait_free(pe, name)
                    if half == 0:
                        for b in range(8):
                            pe.wait_ge(free[b], bk.at[(f"head{h}", b)][1])
                    for t in range(4):
                        cs = slice((4 * half + t) * P, (4 * half + t + 1) * P)
                        last = tr(bank(name)[:, t * P:(t + 1) * P], rkT[:, cs], ident)
                    bk.filled(last, name)
                for half in range(2):
                    name = ("sc", h, half)
                    bk.wait_free(pe, name)
                    for t in range(4):
                        cs = slice((4 * half + t) * P, (4 * half + t + 1) * P)
                        last = mm(bank(name)[:, t * P:(t + 1) * P], rkT[:, cs], rqT[h % 2][:, cs], start=True, stop=True)
                    bk.filled(last, name)
                for half in range(2):
                    pe.wait_ge(free[half], bk.at[("krow", h, half)][1])
                for i in range(4):
                    name = ("kvs", h, i)
                    bk.wait_free(pe, name)
                    for s in range(2):
                        c = 2 * i + s
                        if c < NT - 1:
                            last = mm(bank(name)[:, s * DV:(s + 1) * DV], krow[:, c, :], rv[h % 2][:, c, :], start=True, stop=True)
                    bk.filled(last, name)

            def phase2(h):
                pe.wait_ge(sT_done, h + 1)
                pe.wait_ge(state_done, h + 1)
                for i in range(4):
                    name = ("ro", h, i)
                    bk.wait_free(pe, name)
                    for s in range(2):
                        c = 2 * i + s
                        o = bank(name)[:, s * DV:(s + 1) * DV]
                        last = mm(o, sT[:, c, :], rv[h % 2][:, c, :], start=True, stop=c == 0)
                        if c:
                            last = mm(o, rqT[h % 2][:, c * P:(c + 1) * P], state[:, c - 1, :], start=False, stop=True)
                    bk.filled(last, name)

            def turn(h):
                pe.wait_ge(o_done, h + 1)
                for j in range(2):
                    for half in range(2):
                        name = ("rT", h, j, half)
                        bk.wait_free(pe, name)
                        for t in range(4):
                            last = tr(bank(name)[:, t * P:(t + 1) * P], ro[:, 4 * half + t, j * P:(j + 1) * P], ident)
                        bk.filled(last, name)
            for what, n in ret_order:
                {"block": gemm, "phase1": phase1, "phase2": phase2, "turn": turn}[what](n)

            def turn_q(t, g):
                pe.wait_ge(q_scaled, t + 1)
                bk.wait_free(pe, ("qT", t, g))
                for s in range(4):
                    last = tr(bank(("qT", t, g))[:, s * P:(s + 1) * P], qrow[t % 2][:, 4 * g + s, :], ident)
                bk.filled(last, ("qT", t, g))
            turn_q(0, 0)
            turn_q(0, 1)
            for m in range(STEPS + 6):
                if m < STEPS:
                    t, h = divmod(m, HA)
                    nk = (t + 1) * P
                    name = ("lg", m)
                    bk.wait_free(pe, name)
                    if h == 0:
                        for g in range(2):
                            bk.wait_read(pe, ("qT", t, g))
                    c = bk.col(name)
                    for k0 in range(0, nk, BANK):
                        n = min(BANK, nk - k0)
                        last = three(ps[:, c + k0:c + k0 + n].rearrange("p (t k) -> p t k", k=P),
                                     (qT_hi[t % 2][:, h, :], qT_lo[t % 2][h // 4][:, h % 4, :]),
                                     (kT_hi[:, k0:k0 + n].rearrange("p (t k) -> p t k", k=P), kT_lo[:, k0 // P:(k0 + n) // P]), True, True)
                    bk.filled(last, name)
                if 2 <= m < STEPS + 2:
                    t, h = divmod(m - 2, HA)
                    pe.wait_ge(p_done, m - 1)
                    for i in range(t // 4 + 1):
                        name = ("pT", m - 2, i)
                        bk.wait_free(pe, name)
                        for kt in range(4 * i, min(4 * i + 4, t + 1)):
                            last = tr(bank(name)[:, kt % 4 * P:(kt % 4 + 1) * P], prob[h % 4][:, kt * P:(kt + 1) * P], ident)
                        bk.filled(last, name)
                if pv_at(m):
                    t, g, part = pv_at(m)
                    name = ("pv", t, g)
                    if part == 0:
                        bk.wait_free(pe, name)
                        for i in range(t // 4 + 1):
                            bk.wait_read(pe, ("pT", HA * t + 4 * g + 3, i))
                    for kt in range(part * (t + 1) // 4, (part + 1) * (t + 1) // 4):
                        last = mm(bank(name), kvu[:, kt, DH:2 * DH], pT[:, kt, g], start=kt == 0, stop=kt == t)
                    if part == 3:
                        bk.filled(last, name)
                if q_turned_at(m):
                    turn_q(*q_turned_at(m))
            for name in [b[0] for b in blocks[10:]]:
                gemm(name)
            pe.wait_ge(rt_in, 48)

            def logits(g, ks):
                name = ("rt", g)
                for k in ks:
                    if k == 0:
                        bk.wait_free(pe, name)
                        for t in range(4 * g + 2, 4 * g + 4):
                            bk.wait_read(pe, ("n2T", t))
                    last = mm(bank(name)[0:NG + NE, :], w_rt[:, k, :], n2T[:, 4 * g:4 * g + 4, k * P:(k + 1) * P], start=k == 0, stop=k == KT - 1)
                if k == KT - 1:
                    bk.filled(last, name)
            for t in range(NT):
                pe.wait_ge(n2_done, t + 1)
                bk.wait_free(pe, ("n2T", t))
                for k in range(KT):
                    last = tr(ps[:, bk.col(("n2T", t)) + k * P:bk.col(("n2T", t)) + (k + 1) * P], xres[:, t, k * P:(k + 1) * P], ident)
                bk.filled(last, ("n2T", t))
                if t >= 4:
                    logits(0, range(2 * t - 8, 2 * t - 6))
            logits(1, range(KT))
            bk.wait_free(pe, ("lgt",))
            for t in range(NT):
                if t % 4 == 0:
                    bk.wait_read(pe, ("rt", t // 4))
                last = tr(bank(("lgt",))[:, t * (NG + NE):(t + 1) * (NG + NE)], lgT[:, t * P:(t + 1) * P], ident[0:NG + NE, 0:NG + NE])
            bk.filled(last, ("lgt",))
            pe.wait_ge(chosen, 1)
            name = ("rank",)
            bk.wait_free(pe, name)
            mm(bank(name, (NT + 1) * NE), ones[:], o_pre[:], start=True, stop=False, skip_group_check=True)
            bk.filled(mm(bank(name, NT * NE), cst[:, K_TRI:K_TRI + P], rs[:, 7, :], start=False, stop=True, skip_group_check=True), name)
            pe.wait_ge(hot_done, 1)
            name = ("token",)
            bk.wait_free(pe, name)
            for n in range(2 * NT):
                last = mm(bank(name, 32), hot[:, n, :], tile_tok[:, n, :],
                          start=n == 0, stop=n == 2 * NT - 1)
            bk.filled(last, name)

            def turn_rows(i):
                pe.wait_ge(ex_in[i.parity], 16 * (i.half + 1))
                if i.reached(1):
                    pe.wait_ge(exT_lo, i.n)
                for k in range(KT):
                    last = tr(ps[:, B_XT + k * P:B_XT + (k + 1) * P], e_x[i.parity][:].rearrange("s (p k) -> s k p", k=KT)[:, k, :], ident)
                last.then_inc(exT_full, 1)

            def gate_up(i):
                b = i.parity
                pe.wait_ge(exT_lo, i.n + 1)
                if i.reached(1):
                    pe.wait_ge(gu_read, i.n)
                for k in range(KT):
                    if k % 4 == 0:
                        pe.wait_ge(elo_done[k // 4], i.n + 1)
                    wk = [e[b][:, k // 4 * 2048:(k // 4 + 1) * 2048].rearrange("p (a k f) -> p k a f", a=2, f=FF)[:, k % 4]
                          for e in (e_hi, e_lo)]
                    last = three(ps[:, B_GU:B_GU + 2 * FF].rearrange("p (a f) -> p a f", a=2),
                                 (x_hi[b][:, k, :], x_lo[b][:, k, :]), wk, k == 0, k == KT - 1)
                last.then_inc(gu_full, 1)

            def turn_act(i):
                pe.wait_ge(gu_read, i.n + 1)
                if i.reached(1):
                    pe.wait_ge(eaT_lo, i.n)
                for k in range(2):
                    last = tr(ps[:, B_AT + k * P:B_AT + (k + 1) * P], arow[:].rearrange("s (p k) -> s k p", k=2)[:, k, :], ident)
                last.then_inc(eaT_full, 1)

            def down(i):
                b = i.parity
                pe.wait_ge(eaT_lo, i.n + 1)
                pe.wait_ge(elo_done[2], i.n + 1)
                if i.reached(1):
                    pe.wait_ge(ey_read, i.n)
                for n in range(2):
                    for k in range(2):
                        ws = slice(4096 + k * D + n * BANK, 4096 + k * D + (n + 1) * BANK)
                        last = three(ps[:, B_Y + n * BANK:B_Y + (n + 1) * BANK], (at_hi[:, k, :], at_lo[:, k, :]),
                                     (e_hi[b][:, ws], e_lo[b][:, ws]), k == 0, k == 1)
                last.then_inc(ey_full, 1)
            turn_rows(Step(0, 0))

            def work(i):
                if i.reached(1):
                    turn_act(i - 1)
                if not (i + 1).reached(NTILE):
                    turn_rows(i + 1)
                if not i.reached(NTILE):
                    gate_up(i)
                if i.reached(1):
                    down(i - 1)
            each_step(pe, work, NTILE)

        @block.scalar
        def _(act):
            seq = Seq(act, s_act)
            A = nc.scalar.activation

            def hi(c):
                if c >= len(chunks):
                    return
                i, k = chunks[c]
                width = sum(p[2] for p in blocks[i][2])
                act.wait_ge(w_in[c % NR], landed[c])
                if c >= NH:
                    act.wait_ge(*used(c - NH))
                nc.scalar.copy(w_hi[c % NH][:, :width], w_raw[c % NR][:, :width]).then_inc(hi_ready, 1)

            def square_x(tiles):
                for t in tiles:
                    act.wait_ge(x_in[t], 16)
                    if t >= 2:
                        act.wait_ge(sq_done, t - 1)
                    A(junk[:, t % 2, :], xin[:, t, :], ACT.Square, accum_out=small[:, t:t + 1]).then_inc(sq_done, 1)

            def turned_hi(half):
                for k in range(KT):
                    name = ("xT", half, k)
                    bk.wait_full(act, name)
                    A(n_hi[:, k, half * BANK:(half + 1) * BANK], bank(name), ACT.Identity,
                      scale=gains[:, G1 + k:G1 + k + 1]).then_inc(nhi_done, 1)
            square_x(range(NT))
            act.wait_ge(const_in, 16 * 2)
            turned_hi(0)
            for c in range(NH - 1):
                hi(c)
            turned_hi(1)

            def ahead(name):
                for k in range(KT):
                    hi(number[name] * KT + k + NH - 1)
            ahead("kv")
            for t in range(NT):
                bk.wait_full(act, ("kv", t))
                if t == 0:
                    act.wait_ge(nhi_done, 16)
                bk.read(nc.scalar.copy(kvrows[:, t, :], bank(("kv", t), KVW)), ("kv", t))
            ahead("qi")
            for b in range(8):
                bk.wait_full(act, ("qi", b))
                nc.scalar.copy(qiT_hi[:, b // 2, b % 2 * BANK:(b % 2 + 1) * BANK], bank(("qi", b))).then_inc(qi_hi_done, 1)
            act.wait_ge(gains_done, 1)
            for j in range(2):
                for half in range(2):
                    name = ("cT", j, half)
                    bk.wait_full(act, name)
                    bk.read(A(cT[:, j, half * BANK:(half + 1) * BANK], bank(name), ACT.Identity,
                              scale=gains[:, GKV + j:GKV + j + 1]), name)
            for half in range(2):
                name = ("kiT", half)
                bk.wait_full(act, name)
                A(kiT_hi[:, half * BANK:(half + 1) * BANK], bank(name), ACT.Identity,
                  scale=gains[:, GKI:GKI + 1]).then_inc(ki_hi_done, 1)
            for i in range(4):
                name = ("kvu", i)
                bk.wait_full(act, name)
                bk.read(nc.scalar.copy(kvu[:, 2 * i:2 * i + 2, :].rearrange("p t d -> p (t d)"), bank(name)), name)
            n = 0
            for t in range(2, NT):
                nk = (t + 1) * P
                for h in range(HI):
                    name = ("idx", t, h)
                    bk.wait_full(act, name)
                    if n >= 2:
                        act.wait_ge(relu_used, n - 1)
                    c = bk.col(name)
                    bk.read(A(relu[n % 2][:, :nk], ps[:, c:c + nk], ACT.Relu), name)
                    n += 1
            for half in range(2):
                name = ("kT", half)
                bk.wait_full(act, name)
                A(kT_hi[:, half * BANK:(half + 1) * BANK], bank(name), ACT.Identity,
                  scale=gains[:, GK:GK + 1]).then_inc(kT_hi_done, 1)

            def out_gate(p):
                if p:
                    act.wait_ge(o_done, 2 * p)
                for t in range(NT):
                    name = (f"gate{p}", t)
                    bk.wait_full(act, name)
                    if t == 0 and p == 0:
                        act.wait_ge(relu_used, n)
                    bk.read(A(gate[:, t, :], bank(name), ACT.Silu), name)

            def out_head(h):
                if h == 2:
                    act.wait_ge(q0_stored, 16 * NT)
                for b in range(8):
                    name = (f"head{h}", b)
                    bk.wait_full(act, name)
                    if b < 2:
                        dst = rqT[h % 2][:, b * BANK:(b + 1) * BANK]
                    elif b < 4:
                        dst = rkT[:, (b - 2) * BANK:(b - 1) * BANK]
                    else:
                        dst = rv[h % 2][:, 2 * (b - 4):2 * (b - 4) + 2, :].rearrange("p t d -> p (t d)")
                    bk.read(nc.scalar.copy(dst, bank(name)), name)

            def out_q(b):
                if b == 1:
                    bk.wait_full(act, ("ro", HR - 1, 3))
                places = [qrow[t][:, 4:8].rearrange("p h d -> p (h d)") if b == 1 and t < 2 else (qst1 if b else qst0)[t][:]
                          for t in range(NT)]
                for t in range(NT):
                    name = (f"q{b}", t)
                    bk.wait_full(act, name)
                    bk.read(nc.scalar.copy(places[t], bank(name)), name)
                for t in range(2 * b, NT):
                    bk.wait_read(act, (f"q{b}", t))
                    act.dma_start(q_dram[t * P:(t + 1) * P, b * BANK:(b + 1) * BANK], places[t]).then_inc(q1_stored if b else q0_stored, 16)

            def square_q0():
                for t in range(NT):
                    for h in range(4):
                        col = S_QR + HA * t + h
                        inst = A(junk2[:, h % 2 * P:(h % 2 + 1) * P], qst0[t][:, h * DH:(h + 1) * DH], ACT.Square,
                                 accum_out=small[:, col:col + 1])
                        if h == 3:
                            inst.then_inc(q0_squares, 1)
                            act.wait_ge(q0_squares, t + 1)
                        else:
                            seq(inst)

            def out_phase1(h):
                for half in range(2):
                    name = ("krow", h, half)
                    bk.wait_full(act, name)
                    bk.read(A(krow[:, 4 * half:4 * half + 4, :].rearrange("p t d -> p (t d)"), bank(name), ACT.Identity,
                              scale=cst[:, K_KD + h:K_KD + h + 1]), name)
                for half in range(2):
                    name = ("sc", h, half)
                    bk.wait_full(act, name)
                    bk.read(nc.scalar.copy(sT[:, 4 * half:4 * half + 4, :].rearrange("p t d -> p (t d)"), bank(name)), name)
                for i in range(4):
                    name = ("kvs", h, i)
                    bk.wait_full(act, name)
                    m = min(2, NT - 1 - 2 * i)
                    bk.read(nc.scalar.copy(state[:, 2 * i:2 * i + m, :].rearrange("p t d -> p (t d)"), bank(name, m * DV)), name)

            def out_phase2(h):
                if h:
                    act.wait_ge(full[7], bk.at[("rT", h - 1, 1, 1)][1])
                for i in range(4):
                    name = ("ro", h, i)
                    bk.wait_full(act, name)
                    for s in range(2):
                        c = 2 * i + s
                        inst = A(ro[:, c, :], bank(name)[:, s * DV:(s + 1) * DV], ACT.Identity,
                                 scale=cst[:, K_QD + h:K_QD + h + 1], accum_out=small[:, 96 + c:97 + c])
                        bk.read(inst, name) if s else seq(inst)

            def out_stats(h):
                act.wait_ge(o_mu, h + 1)
                for c in range(NT):
                    seq(A(junk2[:], ro[:, c, :], ACT.Square, bias=small[:, 104 + c:105 + c],
                          accum_out=small[:, 112 + c:113 + c])) if c < NT - 1 else \
                        A(junk2[:], ro[:, c, :], ACT.Square, bias=small[:, 104 + c:105 + c],
                          accum_out=small[:, 112 + c:113 + c]).then_inc(o_var, 1)
                act.wait_ge(o_var, h + 1)

            def out_turn(h):
                for j in range(2):
                    dst = [r[:] for r in rT_odd] if j else [rT[:, 0:BANK], rT[:, BANK:]]
                    if h:
                        act.wait_ge(ret_stored, 48 * h)
                    for half in range(2):
                        name = ("rT", h, j, half)
                        bk.wait_full(act, name)
                        bk.read(A(dst[half], bank(name), ACT.Identity,
                                  scale=gains[:, GRT + 2 * h + j:GRT + 2 * h + j + 1]), name)
                    for half in range(2):
                        bk.wait_read(act, ("rT", h, j, half))
                    rows = ret_dram[(2 * h + j) * P:(2 * h + j + 1) * P, :]
                    if j:
                        for half in range(2):
                            act.dma_start(rows[:, half * BANK:(half + 1) * BANK], dst[half]).then_inc(ret_stored, 16)
                    else:
                        act.dma_start(rows, rT[:]).then_inc(ret_stored, 16)

            def out_block(name):
                ahead(name)
                kind, i = name[:-1], int(name[-1])
                {"gate": out_gate, "head": out_head, "q": out_q}[kind](i)
            for what, m in ret_order:
                {"block": out_block, "phase1": out_phase1, "phase2": out_phase2, "turn": out_turn}[what](m)
                if what == "phase2" and m != 0:
                    out_stats(m)
                if (what, m) == ("phase1", 1):
                    out_stats(0)
                if (what, m) == ("phase2", 1):
                    square_q0()

            def out_qT(t, g):
                name = ("qT", t, g)
                if t == 1:
                    act.wait_ge(q1_stored, 16 * (NT - 2))
                bk.wait_full(act, name)
                nc.scalar.copy(qT_hi[t % 2][:, 4 * g:4 * g + 4, :].rearrange("p h q -> p (h q)"), bank(name)).then_inc(qT_hi_done, 1)
            out_qT(0, 0)
            out_qT(0, 1)
            for m in range(STEPS + 6):
                if m < STEPS:
                    t, h = divmod(m, HA)
                    nk = (t + 1) * P
                    act.wait_ge(mx_done, m + 1)
                    A(prob[h % 4][:, :nk], prob[h % 4][:, :nk], ACT.Exp, bias=small[:, 128 + h:129 + h],
                      scale=2.0 ** -(h + 1), accum_out=small[:, 144 + h:145 + h]).then_inc(ex_done, 1)
                if pv_at(m) and pv_at(m)[2] == 3:
                    t, g, _ = pv_at(m)
                    name = ("pv", t, g)
                    bk.wait_full(act, name)
                    if t == 1 and g == 0:
                        act.wait_ge(ret_stored, 48 * HR)
                    if t >= 2 and g == 0:
                        act.wait_ge(att_stored[t % 2], 16 * (t // 2))
                    bk.read(nc.scalar.copy(aT[t % 2][:, 4 * g:4 * g + 4, :].rearrange("p h q -> p (h q)"), bank(name)), name)
                if q_turned_at(m - 1):
                    out_qT(*q_turned_at(m - 1))
                if 1 <= m < STEPS + 1:
                    t, h = divmod(m - 1, HA)
                    g = h // 4
                    for i in range(t // 4 + 1):
                        name = ("pT", m - 1, i)
                        bk.wait_full(act, name)
                        n = min(4, t + 1 - 4 * i)
                        bk.read(nc.scalar.copy(pT[:, 4 * i:4 * i + n, g, h % 4 * P:(h % 4 + 1) * P],
                                               bank(name, n * P).rearrange("p (k q) -> p k q", q=P)), name)
            for n, name in enumerate(("ga0", "ga1", "gr0", "gr1")):
                ahead(name)
                if n == 0:
                    for i in range(2):
                        act.wait_ge(att_stored[i], 16 * NT // 2)
                for b in range(8):
                    bk.wait_full(act, (name, b))
                    bk.read(A(sig[n][:, b // 2, b % 2 * BANK:(b % 2 + 1) * BANK], bank((name, b)), ACT.Sigmoid), (name, b))

            def a_part(n):
                if n >= len(act_chunks):
                    return
                act.wait_ge(a_in[n % 2], 16 * (n // 2 + 1))
                if n >= 2:
                    c = number["ba0"] * KT + n - 2
                    act.wait_ge(*used(c))
                nc.scalar.copy(a_hi[n % 2][:], a_raw[n % 2][:]).then_inc(a_hi_ready, 1)

            def mix_part(m):
                act.wait_ge(mixed, m + 1)
                f, hs = m // 2, slice(m % 2 * BANK, (m % 2 + 1) * BANK)
                nc.scalar.copy(n_hi[:, f, hs], sig[2 + f // 4][:, f % 4, hs]).then_inc(mix_hi, 1)
            a_part(0)
            for n, (name, k) in enumerate(act_chunks):
                a_part(n + 1)
                hi(number["ba0"] * KT + n + NH - 1)
                if name == "br1":
                    mix_part(k)
            for m in range(8, 16):
                mix_part(m)
            ahead("wo0")
            ahead("wo1")
            for t in range(NT):
                bk.wait_read(act, ("wo0", t))
                A(n2sq[:, 0:BANK], h_sb[:, t, 0:BANK], ACT.Square, accum_out=small[:, 280 + t:281 + t]).then_inc(h_half_sq, 1)
                act.wait_ge(h_half_sq, t + 1)
            for t in range(NT):
                bk.wait_read(act, ("wo1", t))
                A(n2sq[:, BANK:], h_sb[:, t, BANK:], ACT.Square, accum_out=small[:, 296 + t:297 + t]).then_inc(h_sq, 1)
                act.wait_ge(h_sq, t + 1)
                if t >= 1:
                    name = ("n2T", t - 1)
                    bk.wait_full(act, name)
                    bk.read(nc.scalar.copy(n2T[:, t - 1, :], ps[:, bk.col(name):bk.col(name) + D]), name)
            name = ("n2T", NT - 1)
            bk.wait_full(act, name)
            bk.read(nc.scalar.copy(n2T[:, NT - 1, :], ps[:, bk.col(name):bk.col(name) + D]), name)
            for g in range(2):
                name = ("rt", g)
                bk.wait_full(act, name)
                bk.read(A(lgT[:, g * BANK:(g + 1) * BANK], bank(name)[0:NG + NE, :], ACT.Identity, bias=b_rt[:]), name)
            act.wait_ge(g_shift, 1)
            A(rs[:, 15, 64:64 + NT * NG], rs[:, 15, 64:64 + NT * NG], ACT.Exp).then_inc(g_exp, 1)
            act.wait_ge(e_shift, 1)
            A(rs[:, 8, 0:NT], rs[:, 8, 0:NT], ACT.Exp).then_inc(e_exp, 1)

            def w_part(i, j):
                b = i.parity
                act.wait_ge(ew_in[b][j], (32, 32, 16)[j] * (i.half + 1))
                if i.reached(2):
                    act.wait_ge(ey_full if j == 2 else gu_full, i.n - 1)
                ws = slice(j * 2048, (j + 1) * 2048)
                nc.scalar.copy(e_hi[b][:, ws], e_raw[b][:, ws]).then_inc(ehi_done[j], 1)

            def x_part(i):
                act.wait_ge(exT_full, i.n + 1)
                if i.reached(2):
                    act.wait_ge(gu_full, i.n - 1)
                nc.scalar.copy(x_hi[i.parity][:].rearrange("p k q -> p (k q)"), ps[:, B_XT:B_XT + D]).then_inc(exT_hi, 1)
            for j in range(3):
                w_part(Step(0, 0), j)
            act.wait_ge(n2_stored, 16 * NT)
            act.wait_ge(h_stored, 16 * NT)
            x_part(Step(0, 0))

            def work(i):
                if i.reached(1):
                    act.wait_ge(eaT_full, i.n)
                    if i.reached(2):
                        act.wait_ge(ey_full, i.n - 1)
                    nc.scalar.copy(at_hi[:].rearrange("p k q -> p (k q)"), ps[:, B_AT:B_AT + FF]).then_inc(eaT_hi, 1)
                if not (i + 1).reached(NTILE):
                    x_part(i + 1)
                    w_part(i + 1, 0)
                    w_part(i + 1, 1)
                act.wait_ge(gu_full, i.n + 1)
                if i.reached(1):
                    act.wait_ge(gu_read, i.n)
                A(gated[:], ps[:, B_GU:B_GU + FF], ACT.Silu).then_inc(gu_silu, 1)
                if not (i + 1).reached(NTILE):
                    w_part(i + 1, 2)
            each_step(act, work, NTILE - 1)
            act.wait_ge(eaT_full, NTILE)
            act.wait_ge(ey_full, NTILE - 1)
            nc.scalar.copy(at_hi[:].rearrange("p k q -> p (k q)"), ps[:, B_AT:B_AT + FF]).then_inc(eaT_hi, 1)

        @block.vector
        def _(dve):
            seq = Seq(dve, s_dve)
            V = nc.vector
            def turned_lo(half):
                for k in range(KT):
                    name = ("xT", half, k)
                    dve.wait_ge(nhi_done, half * KT + k + 1)
                    hs = slice(half * BANK, (half + 1) * BANK)
                    bk.read(V.scalar_tensor_tensor(n_lo[:, k, hs], bank(name), gains[:, G1 + k:G1 + k + 1],
                                                   n_hi[:, k, hs].bitcast(F32), ALU.mult, ALU.subtract), name)
            for pair in range(NT // 2):
                dve.wait_ge(rstd1, pair + 1)
                for t in range(2 * pair, 2 * pair + 2):
                    V.tensor_scalar(xin[:, t, :], xin[:, t, :], small[:, 8 + t:9 + t], None, ALU.mult).then_inc(xn_done, 1)
            dve.wait_ge(const_in, 16 * 2)
            seq(V.scalar_tensor_tensor(gains[:, GK:GK + 1], gains[:, GQ:GQ + 1], DH ** -0.5, gains[:, GK:GK + 1], ALU.mult, ALU.mult))
            V.tensor_scalar(gains[:, GKI:GKI + 1], gains[:, GKI:GKI + 1], DI ** -0.5, None, ALU.mult).then_inc(gains_done, 1)
            turned_lo(0)
            turned_lo(1)
            for t in range(NT):
                dve.wait_ge(free[t], bk.at[("kv", t)][1])
            seq(V.tensor_tensor(sq[:], kvrows[:], kvrows[:], ALU.mult))
            seq(V.tensor_reduce(small[:, 16:24], sq[:, :, 0:KVL], X, ALU.add))
            V.tensor_reduce(small[:, 24:32], sq[:, :, KVL:KVL + DI], X, ALU.add).then_inc(kv_sq, 1)
            dve.wait_ge(kv_rstd, 1)
            seq(V.tensor_tensor(kdup[:, :, 0, :], kvrows[:, :, KVL:KVL + DI], small[:, 40:48].unsqueeze(2).to_broadcast([P, NT, DI]), ALU.mult))
            seq(V.tensor_copy(kdup[:, :, 1, :], kdup[:, :, 0, :]))
            seq(V.tensor_scalar(small[:, 192:256].rearrange("p (t h) -> p t h", h=HI), kvrows[:, :, KVL + DI:KVW], HI ** -0.5, None, ALU.mult))
            V.tensor_tensor(kvrows[:, :, 0:KVL], kvrows[:, :, 0:KVL], small[:, 32:40].unsqueeze(2).to_broadcast([P, NT, KVL]), ALU.mult).then_inc(ckv_n, 1)
            for b in range(8):
                dve.wait_ge(qi_hi_done, b + 1)
                hs = slice(b % 2 * BANK, (b % 2 + 1) * BANK)
                bk.read(V.tensor_tensor(qiT_lo[b // 2][:, hs], bank(("qi", b)), qiT_hi[:, b // 2, hs].bitcast(F32), ALU.subtract), ("qi", b))
            for half in range(2):
                dve.wait_ge(ki_hi_done, half + 1)
                hs = slice(half * BANK, (half + 1) * BANK)
                bk.read(V.scalar_tensor_tensor(kiT_lo[:, hs], bank(("kiT", half)), gains[:, GKI:GKI + 1], kiT_hi[:, hs].bitcast(F32),
                                               ALU.mult, ALU.subtract), ("kiT", half))
            for i in range(4):
                dve.wait_ge(free[i], bk.at[("kvu", i)][1])
            ksq = sq[:].rearrange("p t d -> p (t d)")[:, 0:S].rearrange("p (t d) -> p t d", d=DH)
            seq(V.tensor_tensor(ksq, kvu[:, :, 0:DH], kvu[:, :, 0:DH], ALU.mult))
            V.tensor_reduce(small[:, 48:56], ksq, X, ALU.add).then_inc(k_sq, 1)
            dve.wait_ge(k_rstd, 1)
            V.tensor_tensor(kvu[:, :, 0:DH], kvu[:, :, 0:DH], small[:, 56:64].unsqueeze(2).to_broadcast([P, NT, DH]), ALU.mult).then_inc(k_n, 1)
            n = 0
            for t in range(2, NT):
                nk = (t + 1) * P
                sc = dist[:, tile_off(t):tile_off(t) + nk]
                for h in range(HI):
                    b, cnt, _ = bk.at[("idx", t, h)]
                    dve.wait_ge(free[b], cnt)
                    wv = small[:, 192 + t * HI + h:193 + t * HI + h]
                    if n:
                        dve.wait_ge(relu_used, n)
                    if h == 0:
                        V.tensor_scalar(sc, relu[n % 2][:, :nk], wv, None, ALU.mult).then_inc(relu_used, 1)
                    else:
                        V.scalar_tensor_tensor(sc, relu[n % 2][:, :nk], wv, sc, ALU.mult, ALU.add).then_inc(relu_used, 1)
                    n += 1
                dve.wait_ge(relu_used, n)
                seq(V.tensor_tensor(sc[:, t * P:], sc[:, t * P:], cst[:, K_CAUS:K_CAUS + P], ALU.add))
            def out_phase1(h):
                for half in range(2):
                    bk.wait_read(dve, ("sc", h, half))
                V.tensor_tensor(sT[:], sT[:], cst[:, K_RM + h * P:K_RM + (h + 1) * P].unsqueeze(1).to_broadcast([P, NT, P]),
                                ALU.mult).then_inc(sT_done, 1)
                for i in range(4):
                    bk.wait_read(dve, ("kvs", h, i))
                for c in range(1, NT - 1):
                    inst = V.scalar_tensor_tensor(state[:, c, :], state[:, c - 1, :], GC[h], state[:, c, :], ALU.mult, ALU.add)
                    if c == NT - 2:
                        inst.then_inc(state_done, 1)
                    else:
                        seq(inst)

            def out_phase2(h):
                dve.wait_ge(o_rstd, h + 1)
                for c in range(NT):
                    inst = V.tensor_scalar(ro[:, c, :], ro[:, c, :], small[:, 104 + c:105 + c], small[:, 120 + c:121 + c], ALU.add, ALU.mult)
                seq(inst)
                V.tensor_tensor(ro[:], ro[:], gate[:, :, h % 2 * DV:(h % 2 + 1) * DV], ALU.mult).then_inc(o_done, 1)
 
            def out_q1():
                for t in range(NT):
                    bk.wait_read(dve, ("q1", t))
                    src = qrow[t][:, 4:8] if t < 2 else qst1[t][:].rearrange("p (h d) -> p h d", d=DH)
                    seq(V.tensor_tensor(q_sq[t % 2][:], src, src, ALU.mult))
                    V.tensor_reduce(small[:, S_QR + HA * t + 4:S_QR + HA * (t + 1)], q_sq[t % 2][:], X, ALU.add).then_inc(q_squares, 1)
            def take_rounds(sc, first, end):
                for r in range(first, end):
                    m8 = small[:, 256 + r % 2 * 8:264 + r % 2 * 8]
                    seq(V.max(m8, sc))
                    seq(V.match_replace(sc, m8, sc, TAKEN))

            for half in range(2):
                name = ("kT", half)
                dve.wait_ge(kT_hi_done, half + 1)
                bk.read(V.scalar_tensor_tensor(kT_lo[:, 4 * half:4 * half + 4], bank(name).rearrange("p (t k) -> p t k", k=P), gains[:, GK:GK + 1],
                                               kT_hi[:, half * BANK:(half + 1) * BANK].rearrange("p (t k) -> p t k", k=P).bitcast(F32),
                                               ALU.mult, ALU.subtract), name)
            for t in range(NT):
                nk = (t + 1) * P
                sc = dist[:, tile_off(t):tile_off(t) + nk]
                if nk <= TOPK:
                    seq(V.tensor_scalar(sc, cst[:, K_REL:K_REL + nk], float(-t * P), None, ALU.add))
                    V.tensor_tensor(sc[:, t * P:], sc[:, t * P:], cst[:, K_CAUS:K_CAUS + P], ALU.add).then_inc(dist_done, 1)
                    dve.wait_ge(dist_done, t + 1)
                    continue
                if t == NT - 1:
                    take_rounds(sc, 0, RET_ROUND)
                    out_phase2(2)
                    out_phase1(3)
                    take_rounds(sc, RET_ROUND, TOPK // 8)
                else:
                    take_rounds(sc, 0, TOPK // 8)
                seq(V.tensor_scalar(sc, sc, TAKEN, -BIG, ALU.not_equal, ALU.mult))
                V.scalar_tensor_tensor(sc, cst[:, K_REL:K_REL + nk], float(-t * P), sc, ALU.add, ALU.add).then_inc(dist_done, 1)
                dve.wait_ge(dist_done, t + 1)

            out_phase2(3)
            out_q1()
            def out_qT(t, g):
                if (t, g) == (1, 1):
                    dve.wait_ge(ret_stored, 48 * HR)
                dve.wait_ge(qT_hi_done, 2 * t + g + 1)
                name = ("qT", t, g)
                bk.read(V.tensor_tensor(qT_lo[t % 2][g][:].rearrange("p h q -> p (h q)"), bank(name),
                                        qT_hi[t % 2][:, 4 * g:4 * g + 4, :].rearrange("p h q -> p (h q)").bitcast(F32), ALU.subtract), name)
            out_qT(0, 0)
            out_qT(0, 1)
            for m in range(STEPS + 1):
                if m < STEPS:
                    t, h = divmod(m, HA)
                    nk = (t + 1) * P
                    name = ("lg", m)
                    bk.wait_full(dve, name)
                    c = bk.col(name)
                    if m >= 4:
                        for i in range((m - 4) // HA // 4 + 1):
                            bk.wait_full(dve, ("pT", m - 4, i))
                    if m == 2:
                        dve.wait_ge(q1_stored, 16 * (NT - 2))
                    bk.read(V.tensor_tensor_reduce(out=prob[h % 4][:, :nk], in0=ps[:, c:c + nk], in1=dist[:, tile_off(t):tile_off(t) + nk],
                                                   scale=1.0, scalar=-3e38, op0=ALU.add, op1=ALU.max, accum_out=small[:, 160 + h:161 + h]), name)
                    bk.wait_read(dve, name)
                    V.tensor_scalar(small[:, 128 + h:129 + h], small[:, 160 + h:161 + h], -(2.0 ** -(h + 1)), None, ALU.mult).then_inc(mx_done, 1)
                if m >= 1:
                    t, h = divmod(m - 1, HA)
                    nk = (t + 1) * P
                    dve.wait_ge(ex_done, m)
                    seq(V.reciprocal(small[:, 152 + h % 2:153 + h % 2], small[:, 144 + h:145 + h]))
                    V.tensor_scalar(prob[h % 4][:, :nk], prob[h % 4][:, :nk], small[:, 152 + h % 2:153 + h % 2], None, ALU.mult).then_inc(p_done, 1)
                    dve.wait_ge(p_done, m)
                if q_turned_at(m - 1):
                    out_qT(*q_turned_at(m - 1))

            def a_part(n):
                if n >= len(act_chunks):
                    return
                dve.wait_ge(a_hi_ready, n + 1)
                V.tensor_tensor(a_lo[n % 2][:], a_raw[n % 2][:], a_hi[n % 2][:].bitcast(F32), ALU.subtract).then_inc(a_lo_ready, 1)

            def mix(m):
                if m < 16:
                    f, hs = m // 2, slice(m % 2 * BANK, (m % 2 + 1) * BANK)
                    sr = sig[2 + f // 4][:, f % 4, hs]
                    V.tensor_tensor(sr, sr, sig[f // 4][:, f % 4, hs], ALU.add).then_inc(mixed, 1)
                if m >= 1:
                    m -= 1
                    f, hs = m // 2, slice(m % 2 * BANK, (m % 2 + 1) * BANK)
                    dve.wait_ge(mix_hi, m + 1)
                    V.tensor_tensor(n_lo[:, f, hs], sig[2 + f // 4][:, f % 4, hs], n_hi[:, f, hs].bitcast(F32),
                                    ALU.subtract).then_inc(mix_lo, 1)
            a_part(0)
            for n, (name, k) in enumerate(act_chunks):
                a_part(n + 1)
                if name == "br1":
                    mix(k)
                if k == KT - 1:
                    gates = sig[int(name[-1]) + (2 if name[:2] == "br" else 0)]
                    for b in range(8):
                        g = gates[:, b // 2, b % 2 * BANK:(b % 2 + 1) * BANK]
                        bk.wait_full(dve, (name, b))
                        bk.read(V.tensor_tensor(g, g, bank((name, b)), ALU.mult), (name, b))
                    if name[:2] == "br":
                        for b in range(8):
                            bk.wait_read(dve, (name, b))
            for m in range(8, 17):
                mix(m)
            def norm2(t):
                dve.wait_ge(h_rstd, t + 1)
                V.scalar_tensor_tensor(xres[:, t, :], h_sb[:, t, :], small[:, 288 + t:289 + t], g2b[:], ALU.mult, ALU.mult).then_inc(n2_done, 1)
            for bi in range(2):
                for t in range(NT):
                    name = (f"wo{bi}", t)
                    bk.wait_full(dve, name)
                    cs = slice(bi * BANK, (bi + 1) * BANK)
                    if bi == 0:
                        dve.wait_ge(xres_in[t], 16)
                    bk.read(V.tensor_tensor(h_sb[:, t, cs], xres[:, t, cs], bank(name), ALU.add), name)
                    if bi == 1 and t >= 3:
                        if t == 3:
                            dve.wait_ge(rt_in, 48)
                        bk.wait_read(dve, ("wo1", t - 3))
                        norm2(t - 3)
            for t in range(NT - 3, NT):
                bk.wait_read(dve, ("wo1", t))
                norm2(t)
            seq(V.memset(o_pre[:, 0:NE], 0.0))
            seq(V.memset(ones[:], 1.0))
            name = ("lgt",)
            bk.wait_full(dve, name)
            bk.read(V.tensor_copy(lgt[:].rearrange("p t e -> p (t e)"), bank(name, NT * (NG + NE))), name)
            bk.wait_read(dve, name)

            def r(i, n=NT * NE):
                return rs[:, i, 0:n]

            def r3(i, n=NE):
                return rs[:, i, 0:NT * n].rearrange("p (t e) -> p t e", e=n)

            def wide(a, n=NE):
                return a.unsqueeze(2).to_broadcast([P, NT, n])
            gl, el = lgt[:, :, 0:NG], lgt[:, :, NG:]
            g_prob = rs[:, 15, 64:64 + NT * NG].rearrange("p (t g) -> p t g", g=NG)

            def first_of_max(dst, src, top, pri, n):
                seq(V.tensor_reduce(top, src, X, ALU.max))
                seq(V.tensor_tensor(dst, src, wide(top, n), ALU.is_equal))
                seq(V.tensor_tensor(dst, dst, cst[:, pri:pri + n].unsqueeze(1).to_broadcast([P, NT, n]), ALU.mult))
                seq(V.tensor_reduce(r(15, NT), dst, X, ALU.max))
                seq(V.tensor_tensor(dst, dst, wide(r(15, NT), n), ALU.is_equal))
            first_of_max(r3(0, NG), gl, r(9, NT), K_P4, NG)
            V.tensor_tensor(g_prob, gl, wide(r(9, NT), NG), ALU.subtract).then_inc(g_shift, 1)
            seq(V.tensor_scalar(r(2, NT * NG), r(0, NT * NG), 1.0, BIG, ALU.subtract, ALU.mult))
            for e in range(EPG):
                el_e = el.rearrange("p t (g e) -> p t g e", e=EPG)[:, :, :, e]
                em_e = r3(3).rearrange("p t (g e) -> p t g e", e=EPG)[:, :, :, e]
                seq(V.tensor_tensor(em_e, el_e, r3(0, NG), ALU.mult))
                seq(V.tensor_tensor(em_e, em_e, r3(2, NG), ALU.add))
            first_of_max(r3(4), r3(3), r(10, NT), K_P16, NE)
            seq(V.scalar_tensor_tensor(r(5), r(4), -3 * BIG, r(3), ALU.mult, ALU.add))
            first_of_max(r3(6), r3(5), r(11, NT), K_P16, NE)
            V.tensor_tensor(r(8, NT), r(11, NT), r(10, NT), ALU.subtract).then_inc(e_shift, 1)
            seq(V.tensor_tensor(r(7), r(4), r(6), ALU.add))
            for t in range(NT):
                inst = V.tensor_tensor(o_pre[:, (t + 1) * NE:(t + 2) * NE], o_pre[:, t * NE:(t + 1) * NE], r3(7)[:, t, :], ALU.add)
                seq(inst) if t < NT - 1 else inst.then_inc(chosen, 1)
            bk.wait_full(dve, ("rank",))
            c = bk.col(("rank",))
            seq(V.tensor_copy(small[:, 320:336], ps[:, c + NT * NE:c + (NT + 1) * NE]))
            seq(V.tensor_tensor(rs[:, 0, 0:NE * NT].rearrange("p (e m) -> p e m", m=NT),
                                small[:, 320:336].unsqueeze(2).to_broadcast([P, NE, NT]),
                                cst[:, K_THR:K_THR + NE * NT].rearrange("p (e m) -> p e m", m=NT), ALU.is_gt))
            seq(V.tensor_reduce(small[:, 336:352], rs[:, 0, 0:NE * NT].rearrange("p (e m) -> p e m", m=NT), X, ALU.add))
            two = rs[:, 0:2, :].rearrange("p a n -> p (a n)").rearrange("p (e f) -> p e f", f=NE)
            seq(V.tensor_tensor(two, cst[:, K_EXC:K_EXC + NE * NE].rearrange("p (e f) -> p e f", f=NE),
                                small[:, 336:352].unsqueeze(1).to_broadcast([P, NE, NE]), ALU.mult))
            seq(V.tensor_reduce(small[:, 352:368], two, X, ALU.add))
            seq(V.tensor_tensor(small[:, 368:384], small[:, 352:368], small[:, 336:352], ALU.add))
            four = rs[:, 0:4, :].rearrange("p a n -> p (a n)").rearrange("p (i e) -> p i e", e=NE)
            seq(V.tensor_tensor(four, small[:, 368:384].unsqueeze(1).to_broadcast([P, 32, NE]),
                                cst[:, K_TI:K_TI + 32].unsqueeze(2).to_broadcast([P, 32, NE]), ALU.is_le))
            seq(V.tensor_reduce(small[:, 384:416], four, X, ALU.add))
            seq(V.tensor_scalar(small[:, 384:416], small[:, 384:416], float(NE - 1), None, ALU.min))
            seq(V.tensor_copy(owner[:], small[:, 384:416]))
            V.tensor_tensor(fresh[:, 1:32], small[:, 385:416], small[:, 384:415], ALU.not_equal).then_inc(owner_done, 1)
            seq(V.tensor_scalar(small[:, 352:368], small[:, 352:368], float(P), None, ALU.mult))
            V.tensor_tensor(r3(5), ps[:, c:c + NT * NE].rearrange("p (t e) -> p t e", e=NE),
                            small[:, 352:368].unsqueeze(1).to_broadcast([P, NT, NE]), ALU.add).then_inc(ranked, 1)
            dve.wait_ge(ranked, 1)
            for j, oh in ((0, 4), (1, 6)):
                seq(V.tensor_tensor(r(oh), r(oh), r(5), ALU.mult))
                seq(V.tensor_reduce(small[:, 416 + 8 * j:424 + 8 * j], r3(oh), X, ALU.add))
            seq(V.tensor_copy(slot[:].rearrange("p j t -> p (j t)"), small[:, 416:432]))
            NS = 2 * NT
            at_least = rs[:, 0:4, :].rearrange("p a n -> p (a n)").rearrange("p (s i) -> p s i", i=32)
            tile_hot = rs[:, 4:8, :].rearrange("p a n -> p (a n)").rearrange("p (s i) -> p s i", i=32)
            seq(V.tensor_scalar(r(14, NS), small[:, 416:432], 1.0 / P, None, ALU.mult))
            seq(V.tensor_tensor(at_least, r(14, NS).unsqueeze(2).to_broadcast([P, NS, 32]),
                                cst[:, K_TI:K_TI + 32].unsqueeze(1).to_broadcast([P, NS, 32]), ALU.is_ge))
            seq(V.tensor_reduce(r(9, NS), at_least, X, ALU.add))
            seq(V.tensor_scalar(r(9, NS), r(9, NS), -1.0, float(P), ALU.add, ALU.mult))
            seq(V.tensor_tensor(r(10, NS), small[:, 416:432], r(9, NS), ALU.subtract))
            V.tensor_tensor(hot[:], r(10, NS).unsqueeze(2).to_broadcast([P, NS, P]),
                            cst[:, K_IO:K_IO + P].unsqueeze(1).to_broadcast([P, NS, P]), ALU.is_equal)
            seq(V.memset(tile_hot, 0.0))
            seq(V.tensor_tensor(tile_hot[:, :, 0:31], at_least[:, :, 0:31], at_least[:, :, 1:32], ALU.subtract))
            V.tensor_tensor(tile_tok[:], tile_hot, cst[:, K_TOK:K_TOK + NS].unsqueeze(2).to_broadcast([P, NS, 32]), ALU.mult).then_inc(hot_done, 1)
            bk.wait_full(dve, ("token",))
            V.tensor_copy(token[:], bank(("token",), 32)).then_inc(token_done, 1)
            dve.wait_ge(g_exp, 1)
            seq(V.tensor_reduce(r(12, NT), g_prob, X, ALU.add))
            seq(V.reciprocal(r(12, NT), r(12, NT)))
            dve.wait_ge(e_exp, 1)
            seq(V.tensor_scalar(r(13, NT), r(8, NT), 1.0, None, ALU.add))
            seq(V.reciprocal(r(13, NT), r(13, NT)))
            p1, p2 = small[:, 304:312], small[:, 312:320]
            seq(V.tensor_tensor(p1, r(12, NT), r(13, NT), ALU.mult))
            seq(V.tensor_tensor(p2, p1, r(8, NT), ALU.mult))

            def w_part(i, j):
                b = i.parity
                dve.wait_ge(ehi_done[j], i.n + 1)
                ws = slice(j * 2048, (j + 1) * 2048)
                V.tensor_tensor(e_lo[b][:, ws], e_raw[b][:, ws], e_hi[b][:, ws].bitcast(F32), ALU.subtract).then_inc(elo_done[j], 1)

            def x_part(i):
                dve.wait_ge(exT_hi, i.n + 1)
                V.tensor_tensor(x_lo[i.parity][:].rearrange("p k q -> p (k q)"), ps[:, B_XT:B_XT + D],
                                x_hi[i.parity][:].rearrange("p k q -> p (k q)").bitcast(F32), ALU.subtract).then_inc(exT_lo, 1)

            def a_part2(i):
                dve.wait_ge(eaT_hi, i.n + 1)
                V.tensor_tensor(at_lo[:].rearrange("p k q -> p (k q)"), ps[:, B_AT:B_AT + FF],
                                at_hi[:].rearrange("p k q -> p (k q)").bitcast(F32), ALU.subtract).then_inc(eaT_lo, 1)

            def rows_out(i):
                dve.wait_ge(ey_full, i.n + 1)
                if i.reached(2):
                    dve.wait_ge(ey_out[i.parity], 16 * i.half)
                V.tensor_copy(e_y[i.parity][:], ps[:, B_Y:B_Y + D]).then_inc(ey_read, 1)
            dve.wait_ge(n2_stored, 16 * NT)
            dve.wait_ge(h_stored, 16 * NT)
            w_part(Step(0, 0), 0)
            w_part(Step(0, 0), 2)
            x_part(Step(0, 0))

            def work(i):
                if i.reached(1):
                    a_part2(i - 1)
                if not (i + 1).reached(NTILE):
                    x_part(i + 1)
                    w_part(i + 1, 0)
                dve.wait_ge(gu_silu, i.n + 1)
                if i.reached(1):
                    dve.wait_ge(eaT_full, i.n)
                V.tensor_tensor(arow[:], gated[:], ps[:, B_GU + FF:B_GU + 2 * FF], ALU.mult).then_inc(gu_read, 1)
                if i.reached(1):
                    rows_out(i - 1)
                if not (i + 1).reached(NTILE):
                    w_part(i + 1, 2)
            each_step(dve, work, NTILE - 1)
            a_part2(Step((NTILE - 1) // 2, 0))
            rows_out(Step((NTILE - 1) // 2, 0))
            dve.wait_ge(th_in, 16 * NT)
            for t in range(NT):
                dve.wait_ge(ty_in[t % 3], 32 * (t // 3 + 1))
                y0, y1 = (y[:] for y in t_y[t % 3])
                V.scalar_tensor_tensor(t_h[t][:], y0, small[:, 304 + t:305 + t], t_h[t][:], ALU.mult, ALU.add).then_inc(t_half, 1)
                dve.wait_ge(t_half, t + 1)
                V.scalar_tensor_tensor(t_h[t][:], y1, small[:, 312 + t:313 + t], t_h[t][:], ALU.mult, ALU.add).then_inc(t_sum, 1)

        @block.gpsimd
        def _(pool):
            seq = Seq(pool, s_pool)
            G = nc.gpsimd
            nhalf = small[:, 500:501]
            seq(G.memset(nhalf, -0.5))

            def rstd(dst, src, n, width, last=None):
                seq(G.tensor_scalar(dst, src, 1.0 / width, EPS, ALU.mult, ALU.add))
                inst = G.tensor_tensor(dst, dst, nhalf.to_broadcast([P, n]), ALU.pow)
                if last is None:
                    seq(inst)
                else:
                    inst.then_inc(*last)

            def lo(c):
                if c >= len(chunks):
                    return
                i, k = chunks[c]
                width = sum(p[2] for p in blocks[i][2])
                pool.wait_ge(hi_ready, c + 1)
                G.tensor_tensor(w_lo[c % NH][:, :width], w_raw[c % NR][:, :width], w_hi[c % NH][:, :width].bitcast(F32),
                                ALU.subtract).then_inc(lo_ready, 1)

            def ahead(name):
                for k in range(KT):
                    lo(number[name] * KT + k + NH - 1)
            for pair in range(NT // 2):
                pool.wait_ge(sq_done, 2 * (pair + 1))
                rstd(small[:, 8 + 2 * pair:10 + 2 * pair], small[:, 2 * pair:2 * pair + 2], 2, D, (rstd1, 1))
            for c in range(NH - 1):
                lo(c)
            ahead("kv")
            pool.wait_ge(kv_sq, 1)
            rstd(small[:, 32:40], small[:, 16:24], NT, KVL)
            rstd(small[:, 40:48], small[:, 24:32], NT, DI, (kv_rstd, 1))
            ahead("qi")
            pool.wait_ge(k_sq, 1)
            rstd(small[:, 56:64], small[:, 48:56], NT, DH, (k_rstd, 1))

            def scale_q(t0, n):
                qr = small[:, S_QR + HA * t0:S_QR + HA * (t0 + n)]
                rstd(qr, qr, n * HA, DH)
                qr = qr.rearrange("p (t h) -> p t h", h=HA)
                pool.wait_ge(const_in, 16 * 2)
                seq(G.tensor_tensor(qr, qr, cst[:, K_SI:K_SI + HA].unsqueeze(1).to_broadcast([P, n, HA]), ALU.mult))

            def scale_rows(t):
                pool.wait_ge(q_in[t % 2], 16 * (t // 2 + 1))
                G.tensor_tensor(qrow[t % 2][:], qrow[t % 2][:], small[:, S_QR + HA * t:S_QR + HA * (t + 1)].unsqueeze(2).to_broadcast([P, HA, DH]),
                                ALU.mult).then_inc(q_scaled, 1)

            def out_q(b):
                if b == 0:
                    return
                pool.wait_ge(q0_squares, NT)
                for t in range(2):
                    pool.wait_ge(q_squares, t + 1)
                    scale_q(t, 1)
                    scale_rows(t)
                pool.wait_ge(q_squares, NT)
                scale_q(2, NT - 2)

            def mask_scores(h):
                for half in range(2):
                    bk.wait_read(pool, ("sc", h, half))
                G.tensor_tensor(sT[:], sT[:], cst[:, K_RM + h * P:K_RM + (h + 1) * P].unsqueeze(1).to_broadcast([P, NT, P]),
                                ALU.mult).then_inc(sT_done, 1)

            def run_states(h, cs):
                for i in range(4):
                    bk.wait_read(pool, ("kvs", h, i))
                for c in cs:
                    seq(G.tensor_scalar(stmp[:], state[:, c - 1, :], GC[h], 0.0, ALU.mult, ALU.add))
                    inst = G.tensor_tensor(state[:, c, :], state[:, c, :], stmp[:], ALU.add)
                    if c == NT - 2:
                        inst.then_inc(state_done, 1)
                        pool.wait_ge(state_done, h + 1)
                    else:
                        seq(inst)

            def means(h):
                for i in range(4):
                    bk.wait_read(pool, ("ro", h, i))
                G.tensor_scalar(small[:, 104:112], small[:, 96:104], -1.0 / DV, 0.0, ALU.mult, ALU.add).then_inc(o_mu, 1)

            def scales(h):
                pool.wait_ge(o_var, h + 1)
                rstd(small[:, 120:128], small[:, 112:120], NT, DV, (o_rstd, 1))
                pool.wait_ge(o_rstd, h + 1)

            def norm_rows(cs):
                for c in cs:
                    inst = G.tensor_scalar(ro[:, c, :], ro[:, c, :], small[:, 104 + c:105 + c], small[:, 120 + c:121 + c], ALU.add, ALU.mult)
                seq(inst)

            def gate_rows(h):
                G.tensor_tensor(ro[:], ro[:], gate[:, :, h % 2 * DV:(h % 2 + 1) * DV], ALU.mult).then_inc(o_done, 1)
            norm_in, states_in = {"q0": 0, "gate1": 1}, {"head1": 0, "q0": 1, "head3": 2}

            def out_block(name):
                for k in range(KT):
                    lo(number[name] * KT + k + NH - 1)
                    if name in norm_in:
                        if k == 0:
                            scales(norm_in[name])
                            norm_rows(range(0, 4))
                        if k == 1:
                            norm_rows(range(4, NT))
                        if k == 2:
                            gate_rows(norm_in[name])
                    if name in states_in:
                        if k == 3:
                            mask_scores(states_in[name])
                        if k == 4:
                            run_states(states_in[name], range(1, 4))
                        if k == 5:
                            run_states(states_in[name], range(4, NT - 1))
                if name[0] == "q":
                    out_q(int(name[1]))
            for what, m in ret_order:
                if what == "block":
                    out_block(m)
                if what == "phase2":
                    means(m)
                    if m >= 2:
                        scales(m)
            for t in range(2, NT):
                scale_rows(t)
            for b in blocks[10:]:
                ahead(b[0])
            for t in range(NT):
                pool.wait_ge(h_half_sq, t + 1)
                pool.wait_ge(h_sq, t + 1)
                seq(G.tensor_tensor(small[:, 288 + t:289 + t], small[:, 280 + t:281 + t], small[:, 296 + t:297 + t], ALU.add))
                rstd(small[:, 288 + t:289 + t], small[:, 288 + t:289 + t], 1, D, (h_rstd, 1))

            def store_y(i):
                pool.wait_ge(ey_read, i.n + 1)
                pool.dma_start(y_dram[bass.ds(tile_at(i) * P, P), :], e_y[i.parity][:]).then_inc(ey_out[i.parity], 16)

            def place_tokens(i):
                if i.reached(NTILE):
                    return
                if i.reached(2):
                    pool.wait_ge(exT_full, i.n - 1)
                G.tensor_copy(rows_now[:, i.parity:i.parity + 1], token[:, bass.ds(tile_at(i), 1)]).then_inc(rows_placed, 1)

            def gather_rows(i):
                if i.reached(NTILE):
                    return
                G.indirect_dma_start(out=e_x[i.parity][:], out_offset=None, in_=n2_dram,
                                     in_offset=bass.IndirectOffsetOnAxis(ap=rows_now[:, i.parity:i.parity + 1], axis=0)).then_inc(ex_in[i.parity], 16)
            pool.wait_ge(token_done, 1)
            pool.wait_ge(n2_stored, 16 * NT)
            pool.wait_ge(h_stored, 16 * NT)
            for i in range(2):
                place_tokens(Step(0, i))
            pool.wait_ge(rows_placed, 2)
            for i in range(2):
                gather_rows(Step(0, i))

            def work(i):
                place_tokens(i + 2)
                if not i.reached(NTILE):
                    if not (i + 2).reached(NTILE):
                        pool.wait_ge(rows_placed, i.n + 3)
                    pool.wait_ge(ehi_done[1], i.n + 1)
                    G.tensor_tensor(e_lo[i.parity][:, 2048:4096], e_raw[i.parity][:, 2048:4096], e_hi[i.parity][:, 2048:4096].bitcast(F32),
                                    ALU.subtract).then_inc(elo_done[1], 1)
                gather_rows(i + 2)
                if i.reached(2):
                    store_y(i - 2)
            each_step(pool, work, NTILE)
            store_y(Step((NTILE - 1) // 2, 0))
            for i in range(2):
                pool.wait_ge(ey_out[i], 16 * ((NTILE + 1 - i) // 2))
            for j in range(3):
                pool.wait_ge(elo_done[j], NTILE)
            for t in range(NT):
                if t >= 3:
                    pool.wait_ge(t_sum, t - 2)
                for j in range(2):
                    G.indirect_dma_start(out=t_y[t % 3][j][:], out_offset=None, in_=y_dram,
                                         in_offset=bass.IndirectOffsetOnAxis(ap=slot[:, j, t:t + 1], axis=0)).then_inc(ty_in[t % 3], 16)


def kernel(**inputs):
    import concourse.bacc as bacc
    from concourse.bass_utils import run_bass_kernel_spmd as run

    nc = bacc.Bacc("TRN2", target_bir_lowering=False, num_devices=1)
    arrays, w = {}, {}
    shapes = {
        "x": ("x", (S, D)), "w_in": ("w_in", (D, C_GR + D)),
        "w_kv_up": ("w_kv_up", (KVL, 2 * DH)), "w_att": ("w_att_branch", (D, D)), "w_ret": ("w_ret_branch", (D, D)), "w_out": ("w_out", (D, D)),
        "norm2_g": ("norm2_g", (D,)),
        "w_gate": ("w_exp_gate", (NE * D, FF)), "w_up": ("w_exp_up", (NE * D, FF)), "w_down": ("w_exp_down", (NE * FF, D)),
    }
    for name, (src, shape) in shapes.items():
        arrays[f"in_{name}"] = np.ascontiguousarray(inputs[src]).reshape(shape)
    arrays["in_w_rt"] = np.concatenate([np.asarray(inputs["w_group_router"]).reshape(D, NG),
                                        np.asarray(inputs["w_expert_router"]).reshape(D, NE)], axis=1)
    arrays["in_b_rt"] = np.concatenate([np.asarray(inputs["b_group_router"]).reshape(NG),
                                        np.asarray(inputs["b_expert_router"]).reshape(NE)])
    arrays["in_cst"] = constants()
    g = {n: np.asarray(inputs[n], np.float32).reshape(-1) for n in inputs if n.endswith("_g")}
    arrays["in_gains"] = np.ascontiguousarray(np.concatenate([
        g["norm1_g"].reshape(KT, P), g["kv_norm_g"].reshape(2, P), g["k_norm_g"].reshape(1, P),
        np.tile(g["idx_k_norm_g"], 2).reshape(1, P), g["ret_norm_g"].reshape(KT, P), g["q_norm_g"].reshape(1, P)]).T)
    for name, a in arrays.items():
        w[name[3:]] = nc.dram_tensor(name, a.shape, F32, kind="ExternalInput").ap()
    out = nc.dram_tensor("out", (S, D), F32, kind="ExternalOutput").ap()
    scratch = {n: nc.dram_tensor(f"{n}_dram", (S, D), F32, kind=SCRATCH).ap() for n in ("q", "att", "ret", "h", "n2")}
    scratch["y"] = nc.dram_tensor("y_dram", (NTILE * P, D), F32, kind=SCRATCH).ap()
    program(nc, w, scratch, out)
    r = run(nc, [arrays], core_ids=[0])
    return r.results[0]["out"].reshape(1, S, D)


SCRATCH = "Internal"
```
